# Optimizing a Trainium2 kernel written in Bass

```python
import math
import jax
import jax.numpy as jnp
from jax import lax
import numpy as np

D_MODEL = 1024
BATCH = 1
SEQ = 512
DEPTH = 2

RW_HEADS = 8
RW_HEAD_DIM = 64
RW_WIDTH = RW_HEADS * RW_HEAD_DIM
RW_DECAY_RANK = 64
RW_ICLR_RANK = 64
RW_GATE_RANK = 160
RW_GN_EPS = 64e-5
RW_PROJ = 3 * RW_WIDTH + RW_DECAY_RANK + RW_ICLR_RANK + RW_GATE_RANK
SC_WIDTH = 512
SC_CONV = 3
SC_PROJ = 3 * SC_WIDTH
AB_PROJ = RW_PROJ + SC_PROJ
AB_OUT_IN = RW_WIDTH + SC_WIDTH
DIL_PATTERNS = ((128, 1), (512, 4), (2048, 16))
N_GROUPS = 3
DIL_HEADS = 8
DIL_HEAD_DIM = 64
DIL_WIDTH = DIL_HEADS * DIL_HEAD_DIM
DIL_PROJ = N_GROUPS * 3 * DIL_WIDTH
BLOCK = 128
N_BUCKETS = 32
MAX_DISTANCE = 2048
D_FF = 4 * D_MODEL
N_EVEN = (DEPTH + 1) // 2
N_ODD = DEPTH // 2
DEEPNORM_ALPHA = (2 * DEPTH) ** 0.25
DEEPNORM_BETA = (8 * DEPTH) ** -0.25
LN_EPS = 1e-5

kernel_name = 'hybrid_rwkv7_shortconv_dilated_attn_trunk'

def _layer_norm(x, g, b):
    xf = x.astype(jnp.float32)
    mu = jnp.mean(xf, -1, keepdims=True)
    var = jnp.mean(jnp.square(xf - mu), -1, keepdims=True)
    return ((xf - mu) * lax.rsqrt(var + LN_EPS) * g + b).astype(x.dtype)

def _token_shift(p):
    return jnp.pad(p, ((0, 0), (1, 0), (0, 0)))[:, :-1]

def _rwkv7_step(state, inp):
    r, w, k, v, a, b = inp
    sa = jnp.einsum('bhvk,bhk->bhv', state, a)
    state = state * w[:, :, None, :] + sa[..., None] * b[:, :, None, :] + v[..., None] * k[:, :, None, :]
    return state, jnp.einsum('bhvk,bhk->bhv', state, r)

def _causal_depthwise_conv(z, w):
    return lax.conv_general_dilated(z, w[:, None, :].astype(z.dtype), window_strides=(1,),
                                    padding=((SC_CONV - 1, 0),),
                                    dimension_numbers=('NWC', 'WIO', 'NWC'),
                                    feature_group_count=z.shape[-1])

def rwkv_shortconv_mixer(u, w_in, mu, w0, w_up, a0, a_up, g_up, k_k, k_a, r_k, lnx_g, lnx_b, conv_w, w_out):
    f32 = jnp.float32
    B, T, _ = u.shape
    p = u @ w_in
    pa, pb = p[..., :RW_PROJ], p[..., RW_PROJ:]
    pa = pa + mu * (_token_shift(pa) - pa)
    W = RW_WIDTH
    r, k, v, wd, ad, gd = jnp.split(
        pa, [W, 2 * W, 3 * W, 3 * W + RW_DECAY_RANK, 3 * W + RW_DECAY_RANK + RW_ICLR_RANK], axis=-1)
    logw = -jax.nn.softplus(-(w0 + jnp.tanh(wd) @ w_up).astype(f32)) - 0.5
    decay = jnp.exp(-jnp.exp(logw))
    iclr = jax.nn.sigmoid((a0 + ad @ a_up).astype(f32))
    gate = (jax.nn.sigmoid(gd) @ g_up).astype(f32)

    def heads(t):
        return t.astype(f32).reshape(B, T, RW_HEADS, RW_HEAD_DIM)

    kf = k.astype(f32)
    kk = heads(kf * k_k)
    kk = kk / jnp.maximum(jnp.linalg.norm(kk, axis=-1, keepdims=True), 1e-12)
    k_h = heads(kf * (1.0 + (iclr - 1.0) * k_a))
    r_h, v_h, w_h, a_h = heads(r), heads(v), heads(decay), heads(iclr)
    xs = tuple(jnp.moveaxis(t, 1, 0) for t in (r_h, w_h, k_h, v_h, -kk, kk * a_h))
    s0 = jnp.zeros((B, RW_HEADS, RW_HEAD_DIM, RW_HEAD_DIM), f32)
    _, y = lax.scan(_rwkv7_step, s0, xs)
    y = jnp.moveaxis(y, 0, 1)
    mean = jnp.mean(y, -1, keepdims=True)
    var = jnp.mean(jnp.square(y - mean), -1, keepdims=True)
    y = ((y - mean) * lax.rsqrt(var + RW_GN_EPS)).reshape(B, T, W) * lnx_g + lnx_b
    bonus = jnp.sum(r_h * k_h * r_k, -1, keepdims=True) * v_h
    y_a = ((y + bonus.reshape(B, T, W)) * gate).astype(u.dtype)
    h, b_gate, c_gate = jnp.split(pb, 3, axis=-1)
    y_b = b_gate * _causal_depthwise_conv(c_gate * h, conv_w)
    return jnp.concatenate([y_a, y_b], axis=-1) @ w_out

def _t5_bucket(dist):
    exact = N_BUCKETS // 2
    logd = jnp.log(jnp.maximum(dist, 1).astype(jnp.float32) / exact) / math.log(MAX_DISTANCE / exact)
    large = jnp.minimum(exact + (logd * (N_BUCKETS - exact)).astype(jnp.int32), N_BUCKETS - 1)
    return jnp.where(dist < exact, dist, large)

def _to_blocks(x, dil, nb):
    b, t = x.shape[:2]
    rest = x.shape[2:]
    L = t // dil
    x = jnp.moveaxis(x.reshape((b, L, dil) + rest), 2, 1)
    pad = [(0, 0)] * x.ndim
    pad[2] = (0, nb * BLOCK - L)
    return jnp.pad(x, pad).reshape((b, dil, nb, BLOCK) + rest)

def _from_blocks(x, L):
    b, dil, nb, blk = x.shape[:4]
    rest = x.shape[4:]
    x = x.reshape((b, dil, nb * blk) + rest)[:, :, :L]
    return jnp.moveaxis(x, 1, 2).reshape((b, L * dil) + rest)

def _with_prev_block(xb):
    prev = jnp.pad(xb, ((0, 0), (0, 0), (1, 0)) + ((0, 0),) * (xb.ndim - 3))[:, :, :-1]
    return jnp.concatenate([prev, xb], axis=3)

def _dilated_group_attention(q, k, v, bias, band, dil):
    t = q.shape[1]
    L = t // dil
    nb = -(-L // BLOCK)
    qb = _to_blocks(q, dil, nb)
    kc = _with_prev_block(_to_blocks(k, dil, nb))
    vc = _with_prev_block(_to_blocks(v, dil, nb))
    s = jnp.einsum('brnqhd,brnkhd->brnhqk', qb, kc).astype(jnp.float32) * (DIL_HEAD_DIM ** -0.5) + bias
    kidx = jnp.arange(2 * BLOCK)
    not_pad = (jnp.arange(nb) > 0)[:, None, None] | (kidx >= BLOCK)[None, None, :]
    valid = (band[None] & not_pad)[None, None, :, None]
    s = jnp.where(valid, s, -jnp.inf)
    m = jnp.max(s, -1, keepdims=True)
    e = jnp.exp(s - m)
    den = jnp.sum(e, -1, keepdims=True)
    o = jnp.einsum('brnhqk,brnkhd->brnqhd', (e / den).astype(v.dtype), vc)
    lse = jnp.moveaxis((m + jnp.log(den))[..., 0], 3, 4)
    return _from_blocks(o, L), _from_blocks(lse, L)

def dilated_attention_mixer(u, w_qkv, w_out, rel_bias):
    B, T, _ = u.shape
    p = (u @ w_qkv).reshape(B, T, N_GROUPS, 3, DIL_HEADS, DIL_HEAD_DIM)
    qi = jnp.arange(BLOCK)[:, None]
    ki = jnp.arange(2 * BLOCK)[None, :]
    rel = BLOCK + qi - ki
    outs, lses = [], []
    for g, (window, dil) in enumerate(DIL_PATTERNS):
        span = window // dil
        band = (rel >= 0) & (rel <= span)
        bucket = _t5_bucket(jnp.clip(rel, 0, span) * dil)
        bias = jnp.transpose(rel_bias[bucket][..., g * DIL_HEADS:(g + 1) * DIL_HEADS], (2, 0, 1)).astype(jnp.float32)
        o, lse = _dilated_group_attention(p[:, :, g, 0], p[:, :, g, 1], p[:, :, g, 2], bias, band, dil)
        outs.append(o.astype(jnp.float32))
        lses.append(lse)
    wts = jax.nn.softmax(jnp.stack(lses), axis=0)
    o = jnp.sum(wts[..., None] * jnp.stack(outs), axis=0)
    return o.reshape(B, T, DIL_WIDTH).astype(u.dtype) @ w_out

def sq_relu_mlp(u, w1, w2):
    return jnp.square(jax.nn.relu(u @ w1)) @ w2

def setup_inputs(seed: int = 0) -> dict:
    key = jax.random.key(seed)
    ks = iter(jax.random.split(key, 32))
    D = D_MODEL

    def nrm(shape, s):
        return s * jax.random.normal(next(ks), shape, jnp.float32)

    return {
        'x': nrm((BATCH, SEQ, D), 1.0),
        'c': nrm((BATCH, D), 1.0),
        'ada_w': nrm((DEPTH, D, 6 * D), 0.1 * D ** -0.5),
        'ada_b': nrm((DEPTH, 6 * D), 0.01),
        'ln_g': 1.0 + nrm((DEPTH, 2, D), 0.02),
        'ln_b': nrm((DEPTH, 2, D), 0.02),
        'ab_w_in': nrm((N_EVEN, D, AB_PROJ), D ** -0.5),
        'rw_mu': jax.random.uniform(next(ks), (N_EVEN, RW_PROJ), jnp.float32),
        'rw_w0': -2.0 + nrm((N_EVEN, RW_WIDTH), 1.0),
        'rw_w_up': nrm((N_EVEN, RW_DECAY_RANK, RW_WIDTH), RW_DECAY_RANK ** -0.5),
        'rw_a0': nrm((N_EVEN, RW_WIDTH), 0.5),
        'rw_a_up': nrm((N_EVEN, RW_ICLR_RANK, RW_WIDTH), RW_ICLR_RANK ** -0.5),
        'rw_g_up': nrm((N_EVEN, RW_GATE_RANK, RW_WIDTH), RW_GATE_RANK ** -0.5),
        'rw_k_k': 0.85 + nrm((N_EVEN, RW_WIDTH), 0.05),
        'rw_k_a': 1.0 + nrm((N_EVEN, RW_WIDTH), 0.05),
        'rw_r_k': nrm((N_EVEN, RW_HEADS, RW_HEAD_DIM), 0.1),
        'rw_lnx_g': 1.0 + nrm((N_EVEN, RW_WIDTH), 0.02),
        'rw_lnx_b': nrm((N_EVEN, RW_WIDTH), 0.02),
        'sc_conv_w': nrm((N_EVEN, SC_CONV, SC_WIDTH), SC_CONV ** -0.5),
        'ab_w_out': nrm((N_EVEN, AB_OUT_IN, D), DEEPNORM_BETA * AB_OUT_IN ** -0.5),
        'dil_w_qkv': nrm((N_ODD, D, DIL_PROJ), D ** -0.5),
        'dil_w_out': nrm((N_ODD, DIL_WIDTH, D), DEEPNORM_BETA * DIL_WIDTH ** -0.5),
        'rel_bias': nrm((N_BUCKETS, N_GROUPS * DIL_HEADS), 0.5),
        'mlp_w1': nrm((DEPTH, D, D_FF), D ** -0.5),
        'mlp_w2': nrm((DEPTH, D_FF, D), DEEPNORM_BETA * D_FF ** -0.5),
    }

def reference(x, c, ada_w, ada_b, ln_g, ln_b, ab_w_in, rw_mu, rw_w0, rw_w_up, rw_a0, rw_a_up, rw_g_up,
              rw_k_k, rw_k_a, rw_r_k, rw_lnx_g, rw_lnx_b, sc_conv_w, ab_w_out, dil_w_qkv, dil_w_out,
              rel_bias, mlp_w1, mlp_w2):
    cond = jax.nn.silu(c)
    for i in range(DEPTH):
        mod = (cond @ ada_w[i] + ada_b[i])[:, None, :]
        sh1, sc1, g1, sh2, sc2, g2 = jnp.split(mod, 6, axis=-1)
        j = i // 2
        u = x * (1 + sc1) + sh1
        if i % 2 == 0:
            y = rwkv_shortconv_mixer(u, ab_w_in[j], rw_mu[j], rw_w0[j], rw_w_up[j], rw_a0[j], rw_a_up[j],
                                     rw_g_up[j], rw_k_k[j], rw_k_a[j], rw_r_k[j], rw_lnx_g[j], rw_lnx_b[j],
                                     sc_conv_w[j], ab_w_out[j])
        else:
            y = dilated_attention_mixer(u, dil_w_qkv[j], dil_w_out[j], rel_bias)
        x = _layer_norm(DEEPNORM_ALPHA * x + (1 + g1) * y, ln_g[i, 0], ln_b[i, 0])
        u = x * (1 + sc2) + sh2
        y = sq_relu_mlp(u, mlp_w1[i], mlp_w2[i])
        x = _layer_norm(DEEPNORM_ALPHA * x + (1 + g2) * y, ln_g[i, 1], ln_b[i, 1])
    return x


_drawn_inputs = setup_inputs


def setup_inputs(seed=0):
    import zlib

    import numpy as np

    out = dict(_drawn_inputs(seed))
    spreads = {}
    factors = {'ada_b': 4.023,
     'rw_w_up': 4.352,
     'rw_k_k': 123.112,
     'rw_k_a': 6.986,
     'rw_lnx_g': 77.726,
     'rw_lnx_b': 79.554}
    for name, (base, spread) in spreads.items():
        noise = np.random.default_rng([zlib.crc32(name.encode()), seed]).standard_normal(out[name].shape)
        drawn = base * np.exp(spread * noise) if base else spread * noise
        out[name] = jnp.asarray(drawn.astype(out[name].dtype))
    for name, factor in factors.items():
        out[name] = (out[name] * factor).astype(out[name].dtype)
    return out
```

```python
import math
from contextlib import ExitStack

import numpy as np

import concourse.bass as bass
from concourse import mybir

P = 128
D = 1024
T = 512
KT = D // P
NR = T // P
F = 4 * D
RW = 512
HP = RW // P
HEADS = 8
HD = 64
CH = 64
NCH = T // CH
SC = T // P
WD_AD = 3 * RW
GD = WD_AD + P
GR = 160
AB = 3 * RW + P + GR + 3 * RW
PB = 3 * RW + P + GR
ALPHA = 4 ** 0.25
LN_EPS = 1e-5
GN_EPS = 64e-5
KAPPA = -math.exp(-0.5)
NEG = -1e30
GROUPS = 3
BAND = 9
BW = 256

F32 = mybir.dt.float32
ALU = mybir.AluOpType
ACT = mybir.ActivationFunctionType
AX = mybir.AxisListType

PAR = {}
_row = 0
for _name, _n in (("c", 8), ("ln_g", 32), ("ln_b", 32), ("mu", 15), ("w0", 4), ("a0", 4), ("k_k", 4), ("k_a", 4),
                  ("r_k", 4), ("lnx_g", 4), ("lnx_b", 4), ("conv", 12)):
    PAR[_name] = _row
    _row += _n
SH1, SC1, G1, SH2, SC2, G2 = range(6)


def build_plan():
    plan = [(("F", i), "act") for i in range(5)]
    plan += [(("par",), "dve")] + [(("mod", 0, k), "dve") for k in range(8)]
    plan += [(("x", d), "act" if d % 2 else "dve") for d in range(KT)]
    plan += [(("p", i), "dve") for i in range(15)]
    plan += [((n, i), "act") for n in ("w", "a", "g") for i in range(HP)]
    plan += [((n, i), "act") for n in ("h", "b") for i in range(HP)]
    plan += [(("nrm", i), "act") for i in range(HP)]
    plan += [(("c", i), "dve") for i in range(HP)]
    plan += [(("gate", 0, 0, n), "act") for n in range(2)] + [(("mod", 0, 8 + k), "act") for k in range(8)]
    plan += [(("gate", 0, 1, n), "act") for n in range(2)]
    plan += [(("bonus", i), "dve") for i in range(HP)]
    for s in range(SC):
        plan += [((n, s), "act") for n in ("trK", "trB", "trA", "trV")]
        plan += [((n, s, i), "dve") for i in range(HP) for n in ("UB", "UK")]
        plan += [(("LL", s, q), "dve") for q in range(2)]
        for n, e in (("D2", "act"), ("D2T", "act"), ("D4", "act"), ("P2", "dve"), ("D4T", "act"), ("D8T", "act"),
                     ("P4", "dve"), ("P8", "dve"), ("P8T", "act"), ("Y1", "act"), ("Pa", "dve"), ("PaT", "act"),
                     ("Y2", "act"), ("Pb", "dve")):
            plan += [((n, s, q), e) for q in range(2)]
        plan += [(("LakV", s), "act"), (("WT", s), "act"), (("U", s), "act")]
        for c in (2 * s, 2 * s + 1):
            plan += [(("SA", c), "dve")] + ([(("DS", c), "dve")] if c < NCH - 1 else []) + [(("Y", c), "act")]
    plan += [(("mean", i), "dve") for i in range(HP)]
    plan += [(("var", i), "act") for i in range(HP)]
    for l in range(2):
        if l:
            for g in range(GROUPS):
                plan += [(("q", g, i), "act") for i in range(HP)] + [(("k", g, i), "dve") for i in range(HP)]
                plan += [(("v", g, r), "act") for r in range(NR)]
            n = HEADS * NR
            for i in range(n + 1):
                if i < n:
                    plan += [(("S0", i), "dve"), (("S1", i), "dve")]
                if i:
                    plan += [(("PT0", i - 1), "act"), (("PT1", i - 1), "dve"), (("O", i - 1), "dve")]
            plan += [(("oT", r), "act") for r in range(NR)]
        plan += [(("y", l, 0, n, r), "dve") for n in range(2) for r in range(NR)]
        plan += [(("nT", l, 0, r, n), "act" if n else "dve") for r in range(NR) for n in range(2)]
        for f in range(F // P):
            plan += [(("f", l, f), "act")]
            if l == 0 and f % 2:
                plan += [(("mod", 1, f // 2), "act")]
        if l == 0:
            plan += [(("gate", 1, g, n), "act") for g in range(2) for n in range(2)]
        plan += [(("y", l, 1, n, r), "dve") for n in range(2) for r in range(NR)]
        if l == 0:
            plan += [(("nT", l, 1, r, n), "act" if n else "dve") for r in range(NR) for n in range(2)]
    return plan


def panel_list():
    out = [("ada", 0, k) for k in range(8)]
    out += [("in", k) for k in range(8)] + [("in", 8 + k) for k in range(6)]
    out += [("adg", 0, 0, n, k) for n in range(2) for k in range(2)]
    out += [("ada", 0, 8 + k) for k in range(8)]
    out += [("adg", 0, 1, n, k) for n in range(2) for k in range(2)]
    out += [("wo", n, k) for n in range(2) for k in range(2)]
    for l in range(2):
        if l:
            for g in range(GROUPS):
                out += [("qkv", g, k) for k in range(4)] + [("wv", g, k) for k in range(2)]
            out += [("do", n) for n in range(2)]
        for k in range(16):
            out += [("w1", l, k)] + ([("ada", 1, k)] if l == 0 else [])
        if l == 0:
            out += [("adg", 1, g, n, k) for g in range(2) for n in range(2) for k in range(2)]
        out += [("w2", l, n, k) for n in range(2) for k in range(8)]
    return out


def last_product(p):
    kind = p[0]
    if kind == "ada":
        return ("mod", p[1], p[2])
    if kind == "adg":
        return ("gate", p[1], p[2], p[3])
    if kind == "in":
        k = p[1]
        return ("p", min(2 * k + 1, 14)) if k < 8 else ("hbc"[(k - 8) // 2], 2 * (k % 2) + 1)
    if kind == "qkv":
        return ("q" if p[2] < 2 else "k", p[1], 2 * (p[2] % 2) + 1)
    if kind == "wv":
        return ("v", p[1], NR - 1)
    if kind in ("wo", "do"):
        return ("y", int(kind == "do"), 0, p[1], NR - 1)
    if kind == "w1":
        return ("f", p[1], 2 * p[2] + 1)
    return ("y", p[1], 1, p[2], NR - 1) if p[3] >= 6 else None


RING = 5


def trunk(nc, x, c, ada_w, ada_b, ln_g, ln_b, ab_w_in, rw_mu, rw_w0, rw_w_up, rw_a0, rw_a_up, rw_g_up, rw_k_k,
          rw_k_a, rw_r_k, rw_lnx_g, rw_lnx_b, sc_conv_w, ab_w_out, dil_w_qkv, dil_w_out, rel_bias, mlp_w1, mlp_w2,
          identity, masks, buckets, out, band_dram, skew_dram):
    plan = build_plan()
    number, freed_count, counts = {}, {}, {"act": 0, "dve": 0}
    for j, (name, reader) in enumerate(plan):
        counts[reader] += 1
        number[name] = j
        freed_count[name] = counts[reader]
    reader_of = dict(plan)
    panels = panel_list()
    panel_no = {p: i for i, p in enumerate(panels)}

    with ExitStack() as ctx:
        def sb(name, shape):
            return ctx.enter_context(nc.sbuf_tensor(name, shape, F32))

        def sem(name):
            return ctx.enter_context(nc.semaphore(name))

        bank = [ctx.enter_context(nc.psum_tensor(f"bank{i}", [P, 512], F32)) for i in range(8)]

        ident = sb("ident", [P, P])
        block_ones = sb("block_ones", [P, P])
        block_mean = sb("block_mean", [P, P])
        par = sb("par", [P, P])
        adab = sb("adab", [P, 96])
        cond = sb("cond", [P, 8])
        condrep = sb("condrep", [P, 8, P])
        mod = sb("mod", [P, 2, 32])
        tiny = sb("tiny", [P, 256])
        mask = sb("mask", [P, 7, P])
        arena = sb("arena", [P, 194 * 256])
        assert masks.shape[1] == 7

        def at(kib, *shape):
            n = int(np.prod(shape))
            v = arena[:, int(kib * 256):int(kib * 256) + n]
            if len(shape) == 1:
                return v
            names = "abcd"[:len(shape)]
            return v.rearrange(f"p ({' '.join(names)}) -> p {' '.join(names)}", **dict(zip(names, shape)))

        ring = [at(8 * i, 2048) for i in range(RING)]
        gate = [at(40 + 4 * i, D) for i in range(3)]
        X0 = 52
        rT, kT_, aT, bT = (at(X0 + 8 * i, HP, T) for i in range(4))
        vT, bonus, gt, ybT = (at(X0 + 32 + 8 * i, HP, T) for i in range(4))
        W0 = X0 + 64
        t8, t9, t10, t11 = (at(W0 + 8 * i, HP, T) for i in range(4))
        xin = at(W0, NR, D)
        uT0 = at(W0 + 32, KT, T)
        lr = at(W0 + 48, 4, RW)
        low = at(W0 + 56, 3, T)
        rawpar = at(X0, 3, P)
        wconst = at(X0 + 4, BAND * BW)
        bandv = at(X0 + 16, BAND * BW)
        relb = at(X0 + 2, GROUPS * HEADS)
        MB = at(W0, HEADS, 2, P)
        MK = at(W0 + 8, HEADS, 2, P)
        m0, m1, m2, m3, m4, m5, m6 = (at(W0 + 16 + 4 * i, HEADS, P) for i in range(7))
        arz = at(W0 + 44, HP, 2, 2, P)
        tokK, tokB, tokA, tokV = (at(W0 + 52 + 2 * i, HP, P) for i in range(4))
        vz = at(W0 + 60, 2, HP, P)
        saz = at(W0 + 64, 2, HP, P)
        lakv, uu, wt = (at(W0 + 68 + 2 * i, HP, P) for i in range(3))
        state = at(W0 + 74, 2, HP, P)
        xp = at(X0 + 64, NR, D)
        nrm = at(X0 + 80, NR, D)
        uT = at(X0 + 96, KT, T)
        grow, brow = at(X0 + 112, D), at(X0 + 116, D)
        hT = at(X0, F // P, T)
        qT = at(X0, GROUPS, HP, T)
        kT = at(X0 + 24, GROUPS, HP, T)
        v_at = [at(X0 + 48, NR, RW), at(X0 + 56, NR, RW), at(X0 + 80, NR, RW)]
        otok = at(X0 + 88, NR, RW)
        oT = at(X0, HP, T)
        qpad = at(X0 + 96, 2, GROUPS, T)
        tab = [at(X0 + 120 + 4.5 * i, BAND * P) for i in range(2)]
        sS = at(X0 + 129, 2, 6 * P)
        pT = at(X0 + 135, 2, 6, P)
        assert X0 + 142 <= 194

        eps_ln, eps_gn = tiny[:, 0:1], tiny[:, 1:2]
        omm = tiny[:, 2:17]
        omka = tiny[:, 17:21]
        csum_end = tiny[:, 24:56]
        rho = tiny[:, 56:84]
        stats = tiny[:, 96:96 + 4 * 12]
        mv = tiny[:, 144:152]
        rstd = tiny[:, 152:156]
        nmr = tiny[:, 156:160]
        scl = tiny[:, 160:168]
        shf = tiny[:, 168:176]
        nmax = tiny[:, 176:180]
        den = tiny[:, 180:184]
        sg_c = tiny[:, 184:192]
        mx = tiny[:, 192:196]

        mm_done = sem("mm_done")
        freed = {"act": sem("read_by_act"), "dve": sem("read_by_dve")}
        slot_landed = [sem(f"slot_landed{i}") for i in range(RING)]
        panel_used = sem("panel_used")
        act_step, dve_step, pool_step = sem("act_step"), sem("dve_step"), sem("pool_step")
        consts_in, params_in, x_in, band_in = sem("consts_in"), sem("params_in"), sem("x_in"), sem("band_in")
        lowrank_in, xp_in, rows_in, tab_in = sem("lowrank_in"), sem("xp_in"), sem("rows_in"), [sem("tab_in0"), sem("tab_in1")]
        band_out, skewed = sem("band_out"), sem("skewed")
        raw_zero, cond_ready, block_ready = sem("raw_zero"), sem("cond_ready"), sem("block_ready")
        sig_c, mod_ready = sem("sig_c"), sem("mod_ready")
        low_ready, sq_ready, norm_root, cs_ready = sem("low_ready"), sem("sq_ready"), sem("norm_root"), sem("cs_ready")
        exps_ready, rk_ready, prods_ready = sem("exps_ready"), sem("rk_ready"), sem("prods_ready")
        arz_ready, vz_ready, p_ready, arz_zero = sem("arz_ready"), sem("vz_ready"), sem("p_ready"), sem("arz_zero")
        state_ready, chunk_done = sem("state_ready"), sem("chunk_done")
        gn_sq, gn_in, gn_root, ya_ready = sem("gn_sq"), sem("gn_in"), sem("gn_root"), sem("ya_ready")
        var_ready, root_ready, scale_ready, normed, resid_ready = (sem("var_ready"), sem("root_ready"), sem("scale_ready"),
                                                                    sem("normed"), sem("resid_ready"))
        h_squared, relu_ready = sem("h_squared"), sem("relu_ready")
        q_padded, max_ready, exp_ready = sem("q_padded"), sem("max_ready"), sem("exp_ready")
        out_stored = sem("out_stored")

        def product_ready(eng, name):
            eng.wait_ge(mm_done, number[name] + 1)
            return bank[number[name] % 8]

        def read(eng, *names):
            need = {}
            for n in names:
                need[reader_of[n]] = max(need.get(reader_of[n], 0), freed_count[n])
            for e, v in need.items():
                eng.wait_ge(freed[e], v)

        def panel_ap(p):
            kind = p[0]
            if kind == "ada":
                l, k = p[1], p[2]
                col = (0, 1, 3, 4)[k // 4] * D + (k % 4) * 256
                return ada_w[l][:, col:col + 256].rearrange("(t p) n -> p t n", p=P)
            if kind == "adg":
                l, g, n, k = p[1:]
                col = (2, 5)[g] * D + n * 512
                return ada_w[l][512 * k:512 * k + 512, col:col + 512].rearrange("(t p) n -> p t n", p=P)
            if kind == "in":
                k = p[1]
                lo = 256 * k if k < 8 else PB + 256 * (k - 8)
                hi = min(lo + 256, PB) if k < 8 else lo + 256
                return ab_w_in[0][:, lo:hi].rearrange("(t p) n -> p t n", p=P)
            if kind == "wo":
                n, k = p[1:]
                return ab_w_out[0][512 * k:512 * k + 512, n * 512:n * 512 + 512].rearrange("(t p) n -> p t n", p=P)
            if kind == "qkv":
                g, k = p[1:]
                col = g * 1536 + 256 * k
                return dil_w_qkv[0][:, col:col + 256].rearrange("(t p) n -> p t n", p=P)
            if kind == "wv":
                g, k = p[1:]
                return dil_w_qkv[0][512 * k:512 * k + 512, g * 1536 + 1024:g * 1536 + 1536].rearrange("(t p) n -> p t n", p=P)
            if kind == "do":
                return dil_w_out[0][:, p[1] * 512:p[1] * 512 + 512].rearrange("(t p) n -> p t n", p=P)
            if kind == "w1":
                l, k = p[1:]
                return mlp_w1[l][:, 256 * k:256 * k + 256].rearrange("(t p) n -> p t n", p=P)
            l, n, k = p[1:]
            return mlp_w2[l][512 * k:512 * k + 512, n * 512:n * 512 + 512].rearrange("(t p) n -> p t n", p=P)

        def panel_tile(p):
            src = panel_ap(p)
            t, n = src.shape[1], src.shape[2]
            return ring[panel_no[p] % RING][:, 0:t * n].rearrange("p (t n) -> p t n", t=t), src

        block = ctx.enter_context(nc.Block())

        @block.sync
        def _(sp):
            sp.dma_start(ident[:, :], identity).then_inc(consts_in, 16)
            sp.dma_start(mask[:, :, :], masks).then_inc(consts_in, 16)
            sp.dma_start(wconst[0:33, :], buckets).then_inc(band_in, 16)
            sp.dma_start(relb[0:32, :], rel_bias).then_inc(band_in, 16)
            sp.wait_ge(raw_zero, 1)

            def rows(name, n, src):
                sp.dma_start(rawpar[PAR[name]:PAR[name] + n, 0, :], src).then_inc(params_in, 16)

            rows("c", 8, c[0].rearrange("(r j) -> r j", j=P))
            rows("ln_g", 32, ln_g.rearrange("a b (r j) -> (a b r) j", j=P))
            rows("ln_b", 32, ln_b.rearrange("a b (r j) -> (a b r) j", j=P))
            rows("mu", 14, rw_mu[0, 0:14 * P].rearrange("(r j) -> r j", j=P))
            sp.dma_start(rawpar[PAR["mu"] + 14:PAR["mu"] + 15, 0, 0:32],
                         rw_mu[:, 14 * P:PB]).then_inc(params_in, 16)
            for name, v in (("w0", rw_w0), ("a0", rw_a0), ("k_k", rw_k_k), ("k_a", rw_k_a), ("lnx_g", rw_lnx_g),
                            ("lnx_b", rw_lnx_b)):
                rows(name, 4, v[0].rearrange("(r j) -> r j", j=P))
            sp.dma_start(rawpar[PAR["r_k"]:PAR["r_k"] + 4, 0, :],
                         rw_r_k[0].rearrange("(r e) j -> r (e j)", e=2)).then_inc(params_in, 16)
            rows("conv", 12, sc_conv_w[0].rearrange("k (r j) -> (k r) j", j=P))
            sp.dma_start(rawpar[0:96, 1, :], ada_b.rearrange("l (r j) -> (l r) j", j=P)).then_inc(params_in, 16)
            xr = x[0].rearrange("(l r) d -> r l d", r=NR)
            for i in range(len(panels)):
                if i == 4:
                    for r in range(NR):
                        sp.dma_start(xin[:, r, :], xr[r]).then_inc(x_in, 16)
                    sp.dma_start(lr[0:64, 0, :], rw_w_up[0]).then_inc(lowrank_in, 16)
                    sp.dma_start(lr[64:128, 1, :], rw_a_up[0]).then_inc(lowrank_in, 16)
                    sp.dma_start(lr[:, 2, :], rw_g_up[0, 0:P]).then_inc(lowrank_in, 16)
                    sp.dma_start(lr[0:32, 3, :], rw_g_up[0, P:GR]).then_inc(lowrank_in, 16)
                dst, src = panel_tile(panels[i])
                if i >= RING:
                    name = last_product(panels[i - RING])
                    if name:
                        sp.wait_ge(mm_done, number[name] + 1)
                    else:
                        sp.wait_ge(panel_used, sum(not last_product(p) for p in panels[:i - RING + 1]))
                sp.dma_start(dst, src).then_inc(slot_landed[i % RING], 16)

        @block.gpsimd
        def _(pool):
            steps = [0]

            def step(ins):
                steps[0] += 1
                ins.then_inc(pool_step, 1)
                pool.wait_ge(pool_step, steps[0])

            g = nc.gpsimd
            g.memset(rawpar[:, :, :], 0.0).then_inc(raw_zero, 1)
            pool.wait_ge(raw_zero, 1)
            g.memset(relb[32:33, :], 1.0).then_inc(raw_zero, 1)
            pool.wait_ge(raw_zero, 2)
            step(g.memset(eps_ln, LN_EPS))
            step(g.memset(eps_gn, GN_EPS))
            for t, value in ((block_ones, 1.0), (block_mean, 1.0 / HD)):
                step(g.memset(t[:, :], 0.0))
                step(g.memset(t[0:64, 0:64], value))
                step(g.memset(t[64:128, 64:128], value))
            step(g.memset(lr[64:128, 0, :], 0.0))
            g.memset(lr[0:64, 1, :], 0.0).then_inc(block_ready, 1)
            pool.wait_ge(block_ready, 1)
            read(pool, ("F", 4))
            g.dma_start(band_dram, bandv[0:HEADS, :]).then_inc(band_out, 16)
            pool.wait_ge(band_out, 16)
            for h in range(HEADS):
                src = bass.AP(tensor=band_dram.tensor, offset=band_dram.offset + h * BAND * BW,
                              ap=[[0, P], [1, BAND * BW]])
                g.dma_start(skew_dram[h], src).then_inc(skewed, 16)

            pool.wait_ge(arz_zero, 1)
            step(g.memset(arz[:, :, :, :, :], 0.0))
            step(g.memset(vz[:, :, :, :], 0.0))
            step(g.memset(saz[:, :, :, :], 0.0))
            g.memset(state[:, :, :, :], 0.0).then_inc(state_ready, 1)
            pool.wait_ge(state_ready, 1)
            for s in range(SC):
                if s:
                    pool.wait_ge(mm_done, number[("LL", s - 1, 1)] + 1)
                for e in range(2):
                    h = slice(64 * e, 64 * e + 64)
                    step(g.tensor_copy(arz[h, :, e, 0, :], aT[h, :, P * s:P * s + P]))
                    g.tensor_copy(arz[h, :, e, 1, :], rT[h, :, P * s:P * s + P]).then_inc(arz_ready, 1)
                    pool.wait_ge(arz_ready, 2 * s + e + 1)
                read(pool, ("trV", s))
                if s:
                    pool.wait_ge(mm_done, number[("Y", 2 * s - 1)] + 1)
                for e in range(2):
                    h = slice(64 * e, 64 * e + 64)
                    g.tensor_copy(vz[h, e, :, :], tokV[h, :, :]).then_inc(vz_ready, 1)
                    pool.wait_ge(vz_ready, 2 * s + e + 1)
            pool.wait_ge(mm_done, number[("Y", NCH - 1)] + 1)
            xr = x[0].rearrange("(l r) d -> r l d", r=NR)
            g.dma_start(xp, xr.rearrange("r l d -> l r d")).then_inc(xp_in, 16)

            for l in range(2):
                if l:
                    pool.wait_ge(mm_done, number[("v", GROUPS - 1, NR - 1)] + 1)
                    step(g.memset(qpad[:, :, :, :], 0.0))
                    for h in range(HEADS):
                        e, hp = h % 2, h // 2
                        rows_ = slice(64 * e, 64 * e + 64)
                        if h >= 2:
                            pool.wait_ge(mm_done, number[("S1", (h - 1) * NR - 1)] + 1)
                            read(pool, ("S1", (h - 1) * NR - 1))
                        elif h == 0:
                            pool.wait_ge(skewed, 16 * HEADS)
                            read(pool, ("q", 2, 3))
                        src = bass.AP(tensor=skew_dram.tensor, offset=skew_dram.offset + h * P * BAND * BW + P - 1,
                                      ap=[[BAND * BW - 1, P], [BW, BAND], [1, P]])
                        g.dma_start(tab[e].rearrange("p (b k) -> p b k", b=BAND), src).then_inc(tab_in[e], 16)
                        g.tensor_copy(qpad[rows_, e, :, :], qT[rows_, :, hp, :]).then_inc(q_padded, 1)
                        pool.wait_ge(q_padded, h + 1)
                for j in range(2):
                    if l or j:
                        pool.wait_ge(resid_ready, 4 * (2 * l + j))
                    for dst, v in ((grow, ln_g), (brow, ln_b)):
                        g.dma_start(dst, v[l, j:j + 1, :].partition_broadcast(P)
                                    if False else bass.AP(tensor=v.tensor, offset=v.offset + (2 * l + j) * D,
                                                          ap=[[0, P], [1, D]])).then_inc(rows_in, 16)
                    pool.wait_ge(rows_in, 32 * (2 * l + j + 1))
                    for r in range(NR):
                        pool.wait_ge(normed, 4 * (2 * l + j) + r + 1)
                        step(g.tensor_tensor(xp[:, r, :], nrm[:, r, :], grow, ALU.mult))
                        g.tensor_tensor(xp[:, r, :], xp[:, r, :], brow, ALU.add).then_inc(resid_ready, 1)
                        pool.wait_ge(resid_ready, 4 * (2 * l + j) + r + 1)
            outr = out[0].rearrange("(l r) d -> r l d", r=NR)
            for r in range(NR):
                pool.wait_ge(resid_ready, 12 + r + 1)
                g.dma_start(outr[r], xp[:, r, :]).then_inc(out_stored, 16)
            pool.wait_ge(out_stored, 64)

        @block.scalar
        def _(act):
            steps = [0]
            a = nc.scalar

            def step(ins):
                steps[0] += 1
                ins.then_inc(act_step, 1)
                act.wait_ge(act_step, steps[0])

            def done(ins):
                ins.then_inc(freed["act"], 1)

            for i in range(5):
                b = product_ready(act, ("F", i))
                w = min(512, BAND * BW - 512 * i)
                if i == 3:
                    a.copy(bandv[0:HEADS, 1536:1792], b[0:HEADS, 0:256])
                    ins = a.copy(bandv[0:HEADS, 1792:2048], b[0:HEADS, 256:512])
                else:
                    ins = a.copy(bandv[0:HEADS, 512 * i:512 * i + w], b[0:HEADS, 0:w])
                done(ins)
            read(act, ("par",))
            a.activation(sg_c, par[:, 0:8], ACT.Sigmoid).then_inc(sig_c, 1)

            for d in range(1, KT, 2):
                b = product_ready(act, ("x", d))
                act.wait_ge(mod_ready, 1)
                done(a.activation(uT0[:, d, :].rearrange("p (l r) -> p r l", r=NR),
                                  b[:, :].rearrange("p (r l) -> p r l", r=NR), ACT.Identity,
                                  scale=mod[:, 0, 8 + d:9 + d], bias=mod[:, 0, d:d + 1]))
            read(act, ("p", 14))
            a.activation(low[0:64, 0, :], low[0:64, 0, :], ACT.Tanh)
            a.activation(low[:, 1, :], low[:, 1, :], ACT.Sigmoid)
            a.activation(low[0:32, 2, :], low[0:32, 2, :], ACT.Sigmoid).then_inc(low_ready, 1)
            act.wait_ge(band_out, 16)
            for i in range(HP):
                b = product_ready(act, ("w", i))
                done(a.activation(aT[:, i, :], b[:, :], ACT.Sigmoid, bias=par[:, PAR["w0"] + i:PAR["w0"] + i + 1]))
            for i in range(HP):
                b = product_ready(act, ("a", i))
                done(a.activation(bT[:, i, :], b[:, :], ACT.Sigmoid, bias=par[:, PAR["a0"] + i:PAR["a0"] + i + 1]))
            for i in range(HP):
                b = product_ready(act, ("g", i))
                done(a.copy(gt[:, i, :], b[:, :]))
            for i in range(HP):
                b = product_ready(act, ("h", i))
                done(a.copy(bonus[:, i, :], b[:, :]))
            for i in range(HP):
                b = product_ready(act, ("b", i))
                done(a.copy(ybT[:, i, :], b[:, :]))
            for i in range(HP):
                b = product_ready(act, ("nrm", i))
                done(a.activation(t9[:, i, :], b[:, :], ACT.Sqrt))
            act.wait_ge(cs_ready, 1)
            a.activation(t11, t10, ACT.Exp, scale=-KAPPA).then_inc(exps_ready, 1)
            a.activation(t10, t10, ACT.Exp, scale=KAPPA).then_inc(exps_ready, 1)
            a.activation(aT, aT, ACT.Exp, scale=KAPPA).then_inc(exps_ready, 1)
            a.activation(rho, rho, ACT.Exp, scale=KAPPA / 2).then_inc(exps_ready, 1)
            for n in range(2):
                b = product_ready(act, ("gate", 0, 0, n))
                done(a.activation(gate[0][:, 512 * n:512 * n + 512], b[:, :], ACT.Identity, bias=1.0))
            for k in range(8, 16):
                b = product_ready(act, ("mod", 0, k))
                done(a.copy(mod[:, 0, 2 * k:2 * k + 2], b[:, 0:2]))
            for n in range(2):
                b = product_ready(act, ("gate", 0, 1, n))
                done(a.activation(gate[1][:, 512 * n:512 * n + 512], b[:, :], ACT.Identity, bias=1.0))

            for s in range(SC):
                if s:
                    act.wait_ge(mm_done, number[("Y", 2 * s - 1)] + 1)
                if s == 0:
                    act.wait_ge(arz_zero, 1)
                for n, dst in (("trK", tokK), ("trB", tokB), ("trA", tokA), ("trV", tokV)):
                    b = product_ready(act, (n, s))
                    done(a.copy(dst, b[:, :].rearrange("p (h k) -> p h k", h=HP)))
                where = {"D2": m3, "D2T": m0, "D4": m4, "D4T": m5, "D8T": m3, "P8T": m0, "Y1": m4, "PaT": m5, "Y2": m3}
                for n in ("D2", "D2T", "D4", "D4T", "D8T", "P8T", "Y1", "PaT", "Y2"):
                    for q in range(2):
                        b = product_ready(act, (n, s, q))
                        done(a.copy(where[n][:, 4 * q:4 * q + 4, :], b[:, :].rearrange("p (m k) -> p m k", m=4)))
                for n, dst in (("LakV", lakv), ("WT", wt), ("U", uu)):
                    b = product_ready(act, (n, s))
                    done(a.copy(dst, b[:, :].rearrange("p (h k) -> p h k", h=HP)))
                for c_ in (2 * s, 2 * s + 1):
                    b = product_ready(act, ("Y", c_))
                    done(a.copy(rT[:, :, CH * c_:CH * c_ + CH], b[:, 0:256].rearrange("p (h t) -> p h t", h=HP)))
            for i in range(HP):
                act.wait_ge(gn_in, i + 1)
                a.activation(t10[:, i, :], rT[:, i, :], ACT.Square).then_inc(gn_sq, 1)
            for i in range(HP):
                b = product_ready(act, ("var", i))
                done(a.activation(t10[:, i, :], b[:, :], ACT.Sqrt, bias=eps_gn))

            def norm(l, j):
                last = l == 1 and j == 1
                for r in range(NR):
                    n = 4 * (2 * l + j) + r
                    act.wait_ge(var_ready, n + 1)
                    a.activation(rstd[:, r:r + 1], mv[:, 2 * r + 1:2 * r + 2], ACT.Sqrt, bias=eps_ln).then_inc(root_ready, 1)
                    act.wait_ge(scale_ready, n + 1)
                    a.activation(nrm[:, r, :], nrm[:, r, :], ACT.Identity, scale=rstd[:, r:r + 1],
                                 bias=nmr[:, r:r + 1]).then_inc(normed, 1)
                if last:
                    return
                for r in range(NR):
                    b = product_ready(act, ("nT", l, j, r, 1))
                    for d in range(4, 8):
                        ins = a.activation(uT[:, d, P * r:P * r + P], b[:, P * (d - 4):P * (d - 3)], ACT.Identity,
                                           scale=scl[:, d:d + 1], bias=shf[:, d:d + 1])
                    done(ins)

            def relus(l):
                for f in range(F // P):
                    b = product_ready(act, ("f", l, f))
                    done(a.activation(hT[:, f, :], b[:, :], ACT.Relu))
                    if l == 0 and f % 2:
                        k = f // 2
                        b = product_ready(act, ("mod", 1, k))
                        done(a.copy(mod[:, 1, 2 * k:2 * k + 2], b[:, 0:2]))

            for l in range(2):
                if l:
                    for g in range(GROUPS):
                        for i in range(HP):
                            b = product_ready(act, ("q", g, i))
                            done(a.mul(qT[:, g, i, :], b[:, :], HD ** -0.5))
                        if g == 2:
                            act.wait_ge(resid_ready, 8)
                        for r in range(NR):
                            b = product_ready(act, ("v", g, r))
                            done(a.copy(v_at[g][:, r, :], b[:, :]))
                    n = HEADS * NR
                    for i in range(n + 1):
                        if i < n:
                            act.wait_ge(max_ready, i + 1)
                            a.activation(sS[:, i % 2, :], sS[:, i % 2, :], ACT.Exp, bias=nmax[:, i % 4:i % 4 + 1],
                                         accum_out=den[:, i % 4:i % 4 + 1]).then_inc(exp_ready, 1)
                        if i:
                            b = product_ready(act, ("PT0", i - 1))
                            done(a.copy(pT[:, (i - 1) % 2, 0:4, :], b[:, :].rearrange("p (m k) -> p m k", m=4)))
                    for r in range(NR):
                        b = product_ready(act, ("oT", r))
                        done(a.copy(oT[:, :, P * r:P * r + P], b[:, :].rearrange("p (h t) -> p h t", h=HP)))
                norm(l, 0)
                relus(l)
                if l == 0:
                    for g in range(2):
                        for n in range(2):
                            b = product_ready(act, ("gate", 1, g, n))
                            done(a.activation(gate[2 * g][:, 512 * n:512 * n + 512], b[:, :], ACT.Identity, bias=1.0))
                norm(l, 1)

        @block.vector
        def _(dve):
            steps = [0]
            v = nc.vector

            def step(ins):
                steps[0] += 1
                ins.then_inc(dve_step, 1)
                dve.wait_ge(dve_step, steps[0])

            def done(ins):
                ins.then_inc(freed["dve"], 1)

            b = product_ready(dve, ("par",))
            v.tensor_copy(par[:, :], b[:, 0:P])
            done(v.tensor_copy(adab[:, :], b[:, P:P + 96]))
            read(dve, ("par",))
            v.tensor_scalar(omm, par[:, PAR["mu"]:PAR["mu"] + 15], -1.0, 1.0, ALU.mult, ALU.add)
            v.tensor_scalar(omka, par[:, PAR["k_a"]:PAR["k_a"] + 4], -1.0, 1.0, ALU.mult, ALU.add)
            dve.wait_ge(sig_c, 1)
            step(v.tensor_tensor(cond[:, :], sg_c, par[:, 0:8], ALU.mult))
            v.tensor_copy(condrep[:, :, :], cond[:, :].unsqueeze(2).broadcast_to((P, 8, P))).then_inc(cond_ready, 1)
            for k in range(8):
                b = product_ready(dve, ("mod", 0, k))
                done(v.scalar_tensor_tensor(mod[:, 0, 2 * k:2 * k + 2], b[:, 0:2], float(k >= 4),
                                            adab[:, 2 * k:2 * k + 2], ALU.add, ALU.add))
            read(dve, ("mod", 0, 7))
            v.tensor_copy(tiny[:, 203:204], mod[:, 0, 0:1]).then_inc(mod_ready, 1)
            for d in range(0, KT, 2):
                b = product_ready(dve, ("x", d))
                done(v.tensor_scalar(uT0[:, d, :].rearrange("p (l r) -> p r l", r=NR),
                                     b[:, :].rearrange("p (r l) -> p r l", r=NR), mod[:, 0, 8 + d:9 + d],
                                     mod[:, 0, d:d + 1], ALU.mult, ALU.add))
            for i in range(15):
                b = product_ready(dve, ("p", i))
                rows_ = 32 if i == 14 else P
                dst = (rT, kT_, vT)[i // 4][:, i % 4, :] if i < 12 else low[:, i - 12, :]
                dst = dst[0:rows_]
                step(v.tensor_scalar(dst, b[0:rows_, :], omm[0:rows_, i:i + 1], None, ALU.mult))
                done(v.scalar_tensor_tensor(dst[:, 1:T], b[0:rows_, 0:T - 1], par[0:rows_, PAR["mu"] + i:PAR["mu"] + i + 1],
                                            dst[:, 1:T], ALU.mult, ALU.add))
            read(dve, ("p", 14))
            for i in range(HP):
                step(v.tensor_scalar(t8[:, i, :], kT_[:, i, :], par[:, PAR["k_k"] + i:PAR["k_k"] + i + 1], None, ALU.mult))
            v.tensor_tensor(t9, t8, t8, ALU.mult).then_inc(sq_ready, 1)
            dve.wait_ge(sq_ready, 1)
            read(dve, ("a", 3))
            for i in range(HP):
                step(v.tensor_scalar(t10[:, i, :], bT[:, i, :], par[:, PAR["k_a"] + i:PAR["k_a"] + i + 1],
                                     omka[:, i:i + 1], ALU.mult, ALU.add))
            step(v.tensor_tensor(kT_, kT_, t10, ALU.mult))
            def chunks(t):
                return t.rearrange("p h (c s) -> p (h c) s", s=CH)

            src, spare = aT, [t10, t11]
            for n, sh in enumerate((1, 2, 4, 8, 16, 32)):
                dst = spare[n % 2]
                v.tensor_copy(chunks(dst)[:, :, 0:sh], chunks(src)[:, :, 0:sh])
                step(v.tensor_tensor(chunks(dst)[:, :, sh:], chunks(src)[:, :, sh:], chunks(src)[:, :, :CH - sh], ALU.add))
                src = dst
            ends = chunks(t11)[:, :, CH - 1]
            step(v.tensor_copy(csum_end, ends))
            ce = csum_end.rearrange("p (h c) -> p h c", c=NCH)
            step(v.tensor_tensor(rho.rearrange("p (h c) -> p h c", c=NCH - 1), ce[:, :, 0:NCH - 1], ce[:, :, 1:NCH], ALU.add))
            step(v.tensor_scalar(csum_end, csum_end, 0.5, None, ALU.mult))
            step(v.tensor_tensor(chunks(t10), chunks(t11), csum_end.unsqueeze(2).broadcast_to((P, HP * NCH, CH)), ALU.subtract))
            v.tensor_tensor(aT, t10, aT, ALU.subtract).then_inc(cs_ready, 1)
            read(dve, ("nrm", 3))
            step(v.tensor_scalar(t9, t9, 1e-12, None, ALU.max))
            step(v.reciprocal(t9, t9))
            step(v.tensor_tensor(t8, t8, t9, ALU.mult))
            for i in range(HP):
                step(v.scalar_tensor_tensor(t9[:, i, :], rT[:, i, :], par[:, PAR["r_k"] + i:PAR["r_k"] + i + 1],
                                            kT_[:, i, :], ALU.mult, ALU.mult))
            v.tensor_copy(tiny[:, 200:201], t9[:, 0, 0:1]).then_inc(rk_ready, 1)
            dve.wait_ge(exps_ready, 4)
            step(v.scalar_tensor_tensor(aT, t8, -1.0, aT, ALU.mult, ALU.mult))
            step(v.tensor_tensor(bT, bT, t8, ALU.mult))
            step(v.tensor_tensor(bT, bT, t11, ALU.mult))
            step(v.tensor_tensor(kT_, kT_, t11, ALU.mult))
            v.tensor_tensor(rT, rT, t10, ALU.mult).then_inc(prods_ready, 1)
            dve.wait_ge(prods_ready, 1)
            for i in range(HP):
                b = product_ready(dve, ("c", i))
                read(dve, ("b", 3))
                done(v.tensor_tensor(t8[:, i, :], b[:, :], bonus[:, i, :], ALU.mult))
                read(dve, ("c", i))

                def tap(k):
                    return par[:, PAR["conv"] + 4 * k + i:PAR["conv"] + 4 * k + i + 1]

                step(v.tensor_scalar(t10[:, i, :], t8[:, i, :], tap(2), None, ALU.mult))
                step(v.scalar_tensor_tensor(t10[:, i, 1:T], t8[:, i, 0:T - 1], tap(1), t10[:, i, 1:T], ALU.mult, ALU.add))
                step(v.scalar_tensor_tensor(t10[:, i, 2:T], t8[:, i, 0:T - 2], tap(0), t10[:, i, 2:T], ALU.mult, ALU.add))
                step(v.tensor_tensor(ybT[:, i, :], ybT[:, i, :], t10[:, i, :], ALU.mult))
            for i in range(HP):
                b = product_ready(dve, ("bonus", i))
                done(v.tensor_tensor(bonus[:, i, :], b[:, :], vT[:, i, :], ALU.mult))
            read(dve, ("bonus", 3))
            v.tensor_copy(tiny[:, 201:202], tiny[:, 0:1]).then_inc(arz_zero, 1)
            read(dve, ("mod", 0, 15))
            v.tensor_tensor(mod[:, 0, 16:24], mod[:, 0, 16:24], adab[:, 24:32], ALU.add)
            step(v.scalar_tensor_tensor(mod[:, 0, 24:32], mod[:, 0, 24:32], 1.0, adab[:, 32:40], ALU.add, ALU.add))

            def msk(lo, n, *shape):
                m = mask[:, lo:lo + n, :]
                return m if n > 1 else mask[:, lo, :]

            for s in range(SC):
                for i in range(HP):
                    for n, dst, lo in (("UB", MB, 0), ("UK", MK, 2)):
                        b = product_ready(dve, (n, s, i))
                        m = mask[:, lo:lo + 2, :].rearrange("p a k -> p (a k)").unsqueeze(1).broadcast_to((P, 2, 2 * P))
                        done(v.tensor_tensor(dst[:, 2 * i:2 * i + 2, :, :].rearrange("p m a k -> p m (a k)"),
                                             b[:, :].rearrange("p (m k) -> p m k", m=2), m, ALU.mult))
                for q in range(2):
                    b = product_ready(dve, ("LL", s, q))
                    for j, dst in ((4, m0), (5, m1), (6, m2)):
                        m = mask[:, j, :].unsqueeze(1).broadcast_to((P, 4, P))
                        ins = v.tensor_tensor(dst[:, 4 * q:4 * q + 4, :], b[:, :].rearrange("p (m k) -> p m k", m=4), m,
                                              ALU.mult)
                    done(ins)
                read(dve, ("LL", s, 1))
                v.tensor_tensor(m6, MB[:, :, 0, :], ident[:, :].unsqueeze(1).broadcast_to((P, HEADS, P)), ALU.add)\
                    .then_inc(p_ready, 1)
                dve.wait_ge(p_ready, s + 1)
                for n in ("P2", "P4", "P8", "Pa", "Pb"):
                    for q in range(2):
                        b = product_ready(dve, (n, s, q))
                        done(v.tensor_tensor(m6[:, 4 * q:4 * q + 4, :], b[:, :].rearrange("p (m k) -> p m k", m=4),
                                             m6[:, 4 * q:4 * q + 4, :], ALU.add))
                    read(dve, (n, s, 1))
                for c_ in (2 * s, 2 * s + 1):
                    p_ = c_ % 2
                    h = slice(64 * p_, 64 * p_ + 64)
                    b = product_ready(dve, ("SA", c_))
                    read(dve, ("U", s))
                    if c_ == 0:
                        dve.wait_ge(state_ready, 1)
                    done(v.tensor_tensor(saz[h, p_, :, :], b[h, :].rearrange("p (h k) -> p h k", h=HP), uu[h, :, :], ALU.add))
                    if c_ == NCH - 1:
                        continue
                    b = product_ready(dve, ("DS", c_))
                    old, new = state[:, c_ % 2, :, :], state[:, (c_ + 1) % 2, :, :]
                    rc = rho.rearrange("p (h c) -> p h c", c=NCH - 1)[:, :, c_]
                    bb = b[:, :].rearrange("p (h k) -> p h k", h=HP)
                    if c_:
                        product_ready(dve, ("Y", c_ - 1))
                    for e in range(2):
                        g = slice(64 * e, 64 * e + 64)
                        k = slice(64 * e, 64 * e + 64)
                        ins = v.tensor_tensor(new[g, :, k], bb[g, :, k], old[g, :, k], ALU.add)
                    step(ins)
                    for e in range(2):
                        g = slice(64 * e, 64 * e + 64)
                        k = slice(64 * e, 64 * e + 64)
                        ins = v.tensor_tensor(new[g, :, k], new[g, :, k],
                                              rc[g].unsqueeze(2).broadcast_to((64, HP, 64)), ALU.mult)
                    done(ins)
            for i in range(HP):
                b = product_ready(dve, ("mean", i))
                v.tensor_tensor(rT[:, i, :], rT[:, i, :], b[:, :], ALU.subtract).then_inc(freed["dve"], 1)
                read(dve, ("mean", i))
                v.tensor_copy(tiny[:, 202:203], rT[:, i, 0:1]).then_inc(gn_in, 1)
            for i in range(HP):
                read(dve, ("var", i))
                step(v.reciprocal(t10[:, i, :], t10[:, i, :]))
                step(v.tensor_tensor(rT[:, i, :], rT[:, i, :], t10[:, i, :], ALU.mult))
                step(v.tensor_scalar(rT[:, i, :], rT[:, i, :], par[:, PAR["lnx_g"] + i:PAR["lnx_g"] + i + 1],
                                     par[:, PAR["lnx_b"] + i:PAR["lnx_b"] + i + 1], ALU.mult, ALU.add))
                step(v.tensor_tensor(rT[:, i, :], rT[:, i, :], bonus[:, i, :], ALU.add))
                v.tensor_tensor(rT[:, i, :], rT[:, i, :], gt[:, i, :], ALU.mult).then_inc(ya_ready, 1)
            dve.wait_ge(ya_ready, HP)

            def norm(l, j):
                last = l == 1 and j == 1
                gr = gate[(0, 1, 0, 2)[2 * l + j]]
                if not last:
                    l2, o = (l, 16) if j == 0 else (1, 0)
                    base = (2 * l + j) * 8
                    step(v.tensor_tensor(scl, par[:, PAR["ln_g"] + base:PAR["ln_g"] + base + 8], mod[:, l2, o + 8:o + 16], ALU.mult))
                    step(v.tensor_tensor(shf, par[:, PAR["ln_b"] + base:PAR["ln_b"] + base + 8], mod[:, l2, o + 8:o + 16], ALU.mult))
                    step(v.tensor_tensor(shf, shf, mod[:, l2, o:o + 8], ALU.add))
                for n in range(2):
                    cols = slice(512 * n, 512 * n + 512)
                    for r in range(NR):
                        b = product_ready(dve, ("y", l, j, n, r))
                        if n == 0 and r == 0 and l == 0 and j == 0:
                            dve.wait_ge(xp_in, 16)
                        if l or j:
                            dve.wait_ge(resid_ready, 4 * (2 * l + j - 1) + r + 1)
                        done(v.tensor_tensor(nrm[:, r, cols], b[:, :], gr[:, cols], ALU.mult))
                        read(dve, ("y", l, j, n, r))
                        step(v.scalar_tensor_tensor(nrm[:, r, cols], xp[:, r, cols], ALPHA, nrm[:, r, cols], ALU.mult, ALU.add))
                        step(v.bn_stats(stats[:, 12 * r + 6 * n:12 * r + 6 * n + 6], nrm[:, r, cols]))
                        if n == 1:
                            k = 4 * (2 * l + j) + r
                            v.bn_aggr(mv[:, 2 * r:2 * r + 2], stats[:, 12 * r:12 * r + 12]).then_inc(var_ready, 1)
                            dve.wait_ge(root_ready, k + 1)
                            step(v.reciprocal(rstd[:, r:r + 1], rstd[:, r:r + 1]))
                            v.scalar_tensor_tensor(nmr[:, r:r + 1], mv[:, 2 * r:2 * r + 1], -1.0, rstd[:, r:r + 1],
                                                   ALU.mult, ALU.mult).then_inc(scale_ready, 1)
                if last:
                    return
                for r in range(NR):
                    b = product_ready(dve, ("nT", l, j, r, 0))
                    for d in range(4):
                        ins = v.tensor_scalar(uT[:, d, P * r:P * r + P], b[:, P * d:P * d + P], scl[:, d:d + 1],
                                              shf[:, d:d + 1], ALU.mult, ALU.add)
                    done(ins)

            for l in range(2):
                if l:
                    for g in range(GROUPS):
                        for i in range(HP):
                            b = product_ready(dve, ("k", g, i))
                            done(v.tensor_copy(kT[:, g, i, :], b[:, :]))
                    n = HEADS * NR
                    for i in range(n + 1):
                        if i < n:
                            h, r = i // NR, i % NR
                            if r == 0:
                                dve.wait_ge(tab_in[h % 2], 16 * (h // 2 + 1))
                            if i >= 2:
                                dve.wait_ge(mm_done, number[("PT1", i - 2)] + 1)
                            t = tab[h % 2]
                            b = product_ready(dve, ("S0", i))
                            done(v.tensor_tensor(sS[:, i % 2, 0:512], b[:, :], t[:, (3 - r) * P:(7 - r) * P], ALU.add))
                            b = product_ready(dve, ("S1", i))
                            done(v.tensor_tensor(sS[:, i % 2, 512:768], b[:, 0:256], t[:, 7 * P:9 * P], ALU.add))
                            read(dve, ("S1", i))
                            if i >= 4:
                                dve.wait_ge(exp_ready, i - 3)
                            step(v.tensor_reduce(mx[:, i % 4:i % 4 + 1], sS[:, i % 2, :], AX.X, ALU.max))
                            v.tensor_scalar(nmax[:, i % 4:i % 4 + 1], mx[:, i % 4:i % 4 + 1], -1.0, None,
                                            ALU.mult).then_inc(max_ready, 1)
                        if i:
                            k = i - 1
                            h, r = k // NR, k % NR
                            b = product_ready(dve, ("PT1", k))
                            done(v.tensor_copy(pT[:, k % 2, 4:6, :], b[:, 0:256].rearrange("p (m k) -> p m k", m=2)))
                            dve.wait_ge(exp_ready, k + 1)
                            step(v.reciprocal(mx[:, k % 4:k % 4 + 1], den[:, k % 4:k % 4 + 1]))
                            b = product_ready(dve, ("O", k))
                            done(v.tensor_scalar(otok[:, r, HD * h:HD * h + HD], b[:, 0:HD], mx[:, k % 4:k % 4 + 1], None,
                                                 ALU.mult))
                norm(l, 0)
                for f in range(F // P):
                    read(dve, ("f", l, f))
                    v.tensor_tensor(hT[:, f, :], hT[:, f, :], hT[:, f, :], ALU.mult).then_inc(h_squared, 1)
                if l == 0:
                    read(dve, ("mod", 1, 15))
                    a1 = 48
                    v.tensor_tensor(mod[:, 1, 0:8], mod[:, 1, 0:8], adab[:, a1:a1 + 8], ALU.add)
                    v.tensor_tensor(mod[:, 1, 16:24], mod[:, 1, 16:24], adab[:, a1 + 24:a1 + 32], ALU.add)
                    v.scalar_tensor_tensor(mod[:, 1, 8:16], mod[:, 1, 8:16], 1.0, adab[:, a1 + 8:a1 + 16], ALU.add, ALU.add)
                    step(v.scalar_tensor_tensor(mod[:, 1, 24:32], mod[:, 1, 24:32], 1.0, adab[:, a1 + 32:a1 + 40], ALU.add, ALU.add))
                norm(l, 1)

        @block.tensor
        def _(pe):
            at_job, at_panel = [0], [0]

            def start(name, offset=0):
                j = at_job[0]
                assert plan[j][0] == name, (plan[j], name)
                at_job[0] += 1
                if j >= 8:
                    read(pe, plan[j - 8][0])
                return bank[j % 8]

            def finish(ins):
                ins.then_inc(mm_done, 1)

            def panel(p):
                i = at_panel[0]
                assert panels[i] == p, (panels[i], p)
                at_panel[0] += 1
                pe.wait_ge(slot_landed[i % RING], 16 * (i // RING + 1))
                return panel_tile(p)[0]

            mm = pe.matmul

            def transpose4(b, parts):
                for i, src in enumerate(parts):
                    ins = pe.transpose(b[:, P * i:P * i + P], src, ident[:, :])
                return ins

            pe.wait_ge(band_in, 32)
            pe.wait_ge(raw_zero, 2)
            for i in range(5):
                b = start(("F", i))
                if i < 3:
                    ins = mm(b[0:HEADS, :], relb[0:33, 0:8], wconst[0:33, 512 * i:512 * i + 512], start=True, stop=True)
                elif i == 3:
                    mm(b[0:HEADS, 0:256], relb[0:33, 0:8], wconst[0:33, 1536:1792], start=True, stop=True)
                    ins = mm(b[0:HEADS, 256:512], relb[0:33, 8:16], wconst[0:33, 1792:2048], start=True, stop=True)
                else:
                    ins = mm(b[0:HEADS, 0:256], relb[0:33, 16:24], wconst[0:33, 2048:2304], start=True, stop=True)
                finish(ins)
            pe.wait_ge(params_in, 16 * 14)
            pe.wait_ge(consts_in, 32)
            b = start(("par",))
            pe.transpose(b[:, 0:P], rawpar[:, 0, :], ident[:, :])
            finish(pe.transpose(b[:, P:2 * P], rawpar[:, 1, :], ident[:, :]))
            pe.wait_ge(cond_ready, 1)

            def mod_cols(l, k):
                w = panel(("ada", l, k))
                b = start(("mod", l, k))
                for n in range(2):
                    for t in range(KT):
                        ins = mm(b[:, n:n + 1], w[:, t, P * n:P * n + P], cond[:, t:t + 1],
                                 start=(t == 0), stop=(t == KT - 1))
                finish(ins)

            def mod_row(l, g, n):
                b = start(("gate", l, g, n))
                for i in range(4):
                    col = 48 * l + (2, 5)[g] * 8 + 4 * n + i
                    mm(b[:, P * i:P * i + P], adab[:, col:col + 1].broadcast_to((P, P)), ident[:, :], start=(i == 0),
                       stop=False, skip_group_check=True)
                for k in range(2):
                    w = panel(("adg", l, g, n, k))
                    for t in range(4):
                        ins = mm(b[:, :], condrep[:, 4 * k + t, :], w[:, t, :], start=False, stop=(k + t == 4),
                                 skip_group_check=True)
                finish(ins)

            for k in range(8):
                mod_cols(0, k)
            pe.wait_ge(x_in, 64)
            for d in range(KT):
                b = start(("x", d))
                finish(transpose4(b, [xin[:, r, P * d:P * d + P] for r in range(NR)]))

            def feature_tile(b, w, n, act_t, m=P):
                for t in range(KT):
                    ins = mm(b[0:m, :], w[:, t, P * n:P * n + m], act_t[:, t, :], start=(t == 0), stop=(t == KT - 1))
                return ins

            read(pe, ("x", 6), ("x", 7))

            for k in range(8):
                w = panel(("in", k))
                for n in range(2 if k < 7 else 1):
                    b = start(("p", 2 * k + n))
                    finish(feature_tile(b, w, n, uT0, P if k < 7 else 32))
            pe.wait_ge(lowrank_in, 64)
            pe.wait_ge(block_ready, 1)
            pe.wait_ge(low_ready, 1)
            for n, j in (("w", 0), ("a", 1)):
                for i in range(HP):
                    b = start((n, i))
                    finish(mm(b[:, :], lr[:, j, P * i:P * i + P], low[:, 0, :], start=True, stop=True))
            for i in range(HP):
                b = start(("g", i))
                mm(b[:, :], lr[:, 2, P * i:P * i + P], low[:, 1, :], start=True, stop=False)
                finish(mm(b[:, :], lr[0:32, 3, P * i:P * i + P], low[0:32, 2, :], start=False, stop=True))
            for k in range(6):
                w = panel(("in", 8 + k))
                if k == 4:
                    pe.wait_ge(sq_ready, 1)
                    for i in range(HP):
                        b = start(("nrm", i))
                        finish(mm(b[:, :], block_ones[:, :], t9[:, i, :], start=True, stop=True))
                for n in range(2):
                    b = start(("hbc"[k // 2], 2 * (k % 2) + n))
                    finish(feature_tile(b, w, n, uT0))
            for n in range(2):
                mod_row(0, 0, n)
            for k in range(8, 16):
                mod_cols(0, k)
            for n in range(2):
                mod_row(0, 1, n)
            pe.wait_ge(rk_ready, 1)
            for i in range(HP):
                b = start(("bonus", i))
                finish(mm(b[:, :], block_ones[:, :], t9[:, i, :], start=True, stop=True))

            pe.wait_ge(prods_ready, 1)
            for s in range(SC):
                tk = slice(P * s, P * s + P)
                for n, src in (("trK", kT_), ("trB", bT), ("trA", aT), ("trV", vT)):
                    b = start((n, s))
                    finish(transpose4(b, [src[:, i, tk] for i in range(HP)]))
                pe.wait_ge(arz_ready, 2 * s + 2)
                for i in range(HP):
                    for n, src in (("UB", bT), ("UK", kT_)):
                        b = start((n, s, i))
                        for e in range(2):
                            ins = mm(b[:, 256 * e:256 * e + 256], src[:, i, tk],
                                     arz[:, i, e, :, :].rearrange("p a k -> p (a k)"), start=True, stop=True)
                        finish(ins)
                for q in range(2):
                    b = start(("LL", s, q))
                    for j in range(4):
                        h = 4 * q + j
                        ins = mm(b[:, P * j:P * j + P], arz[:, h // 2, h % 2, 0, :], bT[:, h // 2, tk], start=True, stop=True)
                    finish(ins)
                pe.wait_ge(p_ready, s + 1)

                def each(name, left, right, *after):
                    for q in range(2):
                        b = start((name, s, q))
                        for a_ in after:
                            read(pe, (a_, s, q))
                        for j in range(4):
                            ins = mm(b[:, P * j:P * j + P], left(4 * q + j), right(4 * q + j), start=True, stop=True)
                        finish(ins)

                def turned(name, src, after):
                    for q in range(2):
                        b = start((name, s, q))
                        read(pe, (after, s, q))
                        finish(transpose4(b, [src[:, 4 * q + j, :] for j in range(4)]))

                each("D2", lambda h: m0[:, h, :], lambda h: MB[:, h, 0, :])
                turned("D2T", m3, "D2")
                each("D4", lambda h: m0[:, h, :], lambda h: m3[:, h, :], "D2T")
                each("P2", lambda h: m0[:, h, :], lambda h: m6[:, h, :], "D2T")
                turned("D4T", m4, "D4")
                each("D8T", lambda h: m4[:, h, :], lambda h: m5[:, h, :], "D4T")
                each("P4", lambda h: m5[:, h, :], lambda h: m6[:, h, :], "P2")
                each("P8", lambda h: m3[:, h, :], lambda h: m6[:, h, :], "D8T", "P4")
                turned("P8T", m6, "P8")
                each("Y1", lambda h: m1[:, h, :], lambda h: m6[:, h, :], "P8T")
                each("Pa", lambda h: m0[:, h, :], lambda h: m4[:, h, :], "Y1")
                turned("PaT", m6, "Pa")
                each("Y2", lambda h: m2[:, h, :], lambda h: m6[:, h, :], "PaT")
                each("Pb", lambda h: m5[:, h, :], lambda h: m3[:, h, :], "Y2")
                b = start(("LakV", s))
                for h in range(HEADS):
                    ins = mm(b[:, HD * h:HD * h + HD], MK[:, h, 0, :], tokV[:, h // 2, HD * (h % 2):HD * (h % 2) + HD],
                             start=True, stop=True)
                finish(ins)
                b = start(("WT", s))
                read(pe, ("Pb", s, 1))
                for h in range(HEADS):
                    e = h % 2
                    ins = mm(b[64 * e:64 * e + 64, P * (h // 2):P * (h // 2) + P],
                             tokA[:, h // 2, HD * e:HD * e + HD], m6[:, h, :], start=True, stop=True)
                finish(ins)
                b = start(("U", s))
                read(pe, ("LakV", s))
                for h in range(HEADS):
                    ins = mm(b[:, HD * h:HD * h + HD], m6[:, h, :], lakv[:, h // 2, HD * (h % 2):HD * (h % 2) + HD],
                             start=True, stop=True)
                finish(ins)
                read(pe, ("WT", s))
                pe.wait_ge(vz_ready, 2 * s + 2)
                for c_ in (2 * s, 2 * s + 1):
                    p_ = c_ % 2
                    S = state[:, c_ % 2, :, :]
                    b = start(("SA", c_))
                    if c_:
                        read(pe, ("DS", c_ - 1))
                    else:
                        pe.wait_ge(state_ready, 1)
                    for i in range(HP):
                        ins = mm(b[64 * p_:64 * p_ + 64, P * i:P * i + P], wt[:, i, 64 * p_:64 * p_ + 64], S[:, i, :],
                                 start=True, stop=True)
                    finish(ins)
                    if c_ < NCH - 1:
                        b = start(("DS", c_))
                        read(pe, ("SA", c_))
                        for i in range(HP):
                            mm(b[:, P * i:P * i + P], tokK[:, i, :], vz[:, p_, i, :], start=True, stop=False)
                            ins = mm(b[:, P * i:P * i + P], tokB[:, i, :], saz[:, p_, i, :], start=False, stop=True)
                        finish(ins)
                    b = start(("Y", c_))
                    read(pe, ("SA", c_))
                    ct = slice(64 * p_, 64 * p_ + 64)
                    for i in range(HP):
                        for e in range(2):
                            o = b[64 * e:64 * e + 64, CH * i:CH * i + CH]
                            mm(o, saz[:, p_, i, HD * e:HD * e + HD], MB[:, 2 * i + e, 1, ct], start=True, stop=False,
                               skip_group_check=True)
                            mm(o, vz[:, p_, i, HD * e:HD * e + HD], MK[:, 2 * i + e, 1, ct], start=False, stop=False,
                               skip_group_check=True)
                        ins = mm(b[:, CH * i:CH * i + CH], S[:, i, :], rT[:, i, CH * c_:CH * c_ + CH], start=False,
                                 stop=True, skip_group_check=True)
                    finish(ins)
            read(pe, ("Y", NCH - 1))
            for i in range(HP):
                b = start(("mean", i))
                finish(mm(b[:, :], block_mean[:, :], rT[:, i, :], start=True, stop=True))
            for i in range(HP):
                b = start(("var", i))
                pe.wait_ge(gn_sq, i + 1)
                finish(mm(b[:, :], block_mean[:, :], t10[:, i, :], start=True, stop=True))

            def out_half(l, j, n, left, kinds):
                banks = [start(("y", l, j, n, r)) for r in range(NR)]
                last = min(2, len(kinds))
                k0 = len(kinds) - last
                for k in range(k0):
                    w = panel(kinds[k])
                    for t in range(4):
                        for r in range(NR):
                            ins = mm(banks[r][:, :], left(4 * k + t, r), w[:, t, :], start=(k + t == 0), stop=False)
                    ins.then_inc(panel_used, 1)
                ws = [panel(p) for p in kinds[k0:]]
                for r in range(NR):
                    for k, w in enumerate(ws):
                        for t in range(4):
                            ins = mm(banks[r][:, :], left(4 * (k0 + k) + t, r), w[:, t, :], start=(k0 + k + t == 0),
                                     stop=(k == last - 1 and t == 3))
                    finish(ins)

            def norm_turns(l, j):
                for r in range(NR):
                    pe.wait_ge(normed, 4 * (2 * l + j) + r + 1)
                    for n in range(2):
                        b = start(("nT", l, j, r, n))
                        finish(transpose4(b, [nrm[:, r, P * d:P * d + P] for d in range(4 * n, 4 * n + 4)]))
                read(pe, ("nT", l, j, NR - 1, 0), ("nT", l, j, NR - 1, 1))

            for l in range(2):
                if l == 0:
                    pe.wait_ge(ya_ready, HP)

                    def left(k, r):
                        src = rT if k < 4 else ybT
                        return src[:, k % 4, r:T:NR]

                    for n in range(2):
                        out_half(0, 0, n, left, [("wo", n, k) for k in range(2)])
                else:
                    for g in range(GROUPS):
                        for k in range(4):
                            w = panel(("qkv", g, k))
                            for n in range(2):
                                i = 2 * (k % 2) + n
                                b = start(("q" if k < 2 else "k", g, i))
                                finish(feature_tile(b, w, n, uT))
                        ws = [panel(("wv", g, k)) for k in range(2)]
                        for r in range(NR):
                            b = start(("v", g, r))
                            for k in range(2):
                                for t in range(4):
                                    ins = mm(b[:, :], uT[:, 4 * k + t, P * r:P * r + P], ws[k][:, t, :],
                                             start=(k + t == 0), stop=(k + t == 4))
                            finish(ins)
                    read(pe, ("q", 2, 3), ("k", 2, 3))
                    read(pe, ("v", 2, 3))
                    n = HEADS * NR
                    for i in range(n + 1):
                        if i < n:
                            h, r = i // NR, i % NR
                            e, hp = h % 2, h // 2
                            pe.wait_ge(q_padded, h + 1)
                            b = start(("S0", i))
                            finish(mm(b[:, :], qpad[:, e, 0, P * r:P * r + P], kT[:, 0, hp, :], start=True, stop=True))
                            b = start(("S1", i))
                            for g in (1, 2):
                                ins = mm(b[:, P * (g - 1):P * g], qpad[:, e, g, P * r:P * r + P],
                                         kT[:, g, hp, P * r:P * r + P], start=True, stop=True)
                            finish(ins)
                        if i:
                            k = i - 1
                            h, r = k // NR, k % NR
                            pe.wait_ge(exp_ready, k + 1)
                            b = start(("PT0", k))
                            finish(transpose4(b, [sS[:, k % 2, P * m:P * m + P] for m in range(4)]))
                            b = start(("PT1", k))
                            finish(transpose4(b, [sS[:, k % 2, P * m:P * m + P] for m in range(4, 6)]))
                            b = start(("O", k))
                            read(pe, ("PT0", k), ("PT1", k))
                            for m in range(6):
                                vs = v_at[0][:, m, :] if m < 4 else v_at[m - 3][:, r, :]
                                ins = mm(b[:, 0:HD], pT[:, k % 2, m, :], vs[:, HD * h:HD * h + HD], start=(m == 0),
                                         stop=(m == 5))
                            finish(ins)
                    read(pe, ("O", n - 1))
                    for r in range(NR):
                        b = start(("oT", r))
                        finish(transpose4(b, [otok[:, r, P * i:P * i + P] for i in range(HP)]))
                    read(pe, ("oT", NR - 1))
                    for n in range(2):
                        out_half(1, 0, n, lambda k, r: oT[:, k, P * r:P * r + P], [("do", n)])
                norm_turns(l, 0)
                for k in range(16):
                    w = panel(("w1", l, k))
                    for n in range(2):
                        b = start(("f", l, 2 * k + n))
                        finish(feature_tile(b, w, n, uT))
                    if l == 0:
                        mod_cols(1, k)
                if l == 0:
                    for g in range(2):
                        for n in range(2):
                            mod_row(1, g, n)
                pe.wait_ge(h_squared, 32 * (l + 1))
                for n in range(2):
                    out_half(l, 1, n, lambda k, r: hT[:, k, P * r:P * r + P], [("w2", l, n, k) for k in range(8)])
                if l == 0:
                    norm_turns(0, 1)
            assert at_job[0] == len(plan) and at_panel[0] == len(panels)


_INS = ['x', 'c', 'ada_w', 'ada_b', 'ln_g', 'ln_b', 'ab_w_in', 'rw_mu', 'rw_w0', 'rw_w_up', 'rw_a0', 'rw_a_up', 'rw_g_up',
        'rw_k_k', 'rw_k_a', 'rw_r_k', 'rw_lnx_g', 'rw_lnx_b', 'sc_conv_w', 'ab_w_out', 'dil_w_qkv', 'dil_w_out',
        'rel_bias', 'mlp_w1', 'mlp_w2']


def shape_constants():
    i, j = np.arange(P)[:, None], np.arange(P)[None, :]

    def same(n):
        return i // n == j // n

    masks = np.stack([same(16) & (i < j), same(64) & (i <= j), same(64) & (i < j), same(64) & (i <= j),
                      same(16) & (i > j), same(32) & ~same(16) & (i > j), same(64) & ~same(32) & (i > j)], axis=1)
    n = np.arange(BW)
    steps = P - 1 - n
    buckets = np.zeros((33, BAND, BW), np.float32)
    for b in range(BAND):
        if b < 7:
            dist = 4 * steps + 3 - b
            valid = (dist >= 0) & (dist <= 128)
        elif b == 7:
            dist = 4 * steps
            valid = steps >= 0
        else:
            dist = 4 * steps
            valid = (steps >= 0) & (steps % 4 == 0)
        d = np.where(valid, dist, 0)
        exact = 16
        far = exact + (np.log(np.maximum(d, 1) / exact) / np.log(2048 / exact) * exact).astype(np.int64)
        bucket = np.where(d < exact, d, np.minimum(far, 31))
        buckets[bucket[valid], b, n[valid]] = 1.0
        buckets[32, b, ~valid] = NEG
    return np.eye(P, dtype=np.float32), masks.astype(np.float32), buckets.reshape(33, BAND * BW)


def kernel(**inputs):
    import concourse.bacc as bacc
    from concourse.bass_utils import run_bass_kernel_spmd

    nc = bacc.Bacc("TRN2", target_bir_lowering=False, num_devices=1)
    arrays, args = {}, []
    for name in _INS:
        arrays[f"in_{name}"] = np.ascontiguousarray(inputs[name])
    for name, value in zip(("identity", "masks", "buckets"), shape_constants()):
        arrays[f"in_{name}"] = value
    for name, value in arrays.items():
        args.append(nc.dram_tensor(name, value.shape, F32, kind="ExternalInput").ap())
    args.append(nc.dram_tensor("out", (1, T, D), F32, kind="ExternalOutput").ap())
    args.append(nc.dram_tensor("band", (HEADS, BAND * BW), F32).ap())
    args.append(nc.dram_tensor("skew", (HEADS, P, BAND * BW), F32).ap())
    trunk(nc, *args)
    r = run_bass_kernel_spmd(nc, [arrays], core_ids=[0])
    return r.results[0]["out"]
```

```python
import math
from contextlib import ExitStack

import numpy as np

import concourse.bass as bass
from concourse import mybir

P = 128
D = 1024
T = 512
KT = D // P
NR = T // P
F = 4 * D
RW = 512
HP = RW // P
HEADS = 8
HD = 64
CH = 64
NCH = T // CH
SC = T // P
WD_AD = 3 * RW
GD = WD_AD + P
GR = 160
AB = 3 * RW + P + GR + 3 * RW
PB = 3 * RW + P + GR
ALPHA = 4 ** 0.25
LN_EPS = 1e-5
GN_EPS = 64e-5
KAPPA = -math.exp(-0.5)
NEG = -1e30
GROUPS = 3
BAND = 9
BW = 256

F32 = mybir.dt.float32
F32R = mybir.dt.float32r
ALU = mybir.AluOpType
ACT = mybir.ActivationFunctionType
AX = mybir.AxisListType

PAR = {}
_row = 0
for _name, _n in (("c", 8), ("ln_g", 32), ("ln_b", 32), ("mu", 15), ("w0", 4), ("a0", 4), ("k_k", 4), ("k_a", 4),
                  ("r_k", 4), ("lnx_g", 4), ("lnx_b", 4), ("conv", 12)):
    PAR[_name] = _row
    _row += _n
SH1, SC1, G1, SH2, SC2, G2 = range(6)


FH = F // P // 2
ADA_COLS = (0, 1, 2, 3, 6, 7, 8, 9)
ADA_ROWS = (4, 5, 10, 11)
ADA_REST = (4, 5, 6, 7, 8, 9, 10, 11)


def ada_product(l, cg):
    return ("gate", l, int(cg > 5), cg % 2) if cg in ADA_ROWS else ("mod", l, cg)


def build_plan():
    plan = [(("F", i), "act") for i in range(5)]
    plan += [(("par",), "dve")] + [(("mod", 0, cg), "dve") for cg in range(4)]
    plan += [(("x", d), "act" if d % 2 else "dve") for d in range(KT)]
    tiles = [("p", i) for i in range(15)]
    for t in tiles:
        plan += [(t, "dve")] + [(ada_product(0, cg), "act") for i, cg in ((5, 4), (9, 5), (13, 6)) if t[1] == i]
    plan += [((n, i), "act") for n in ("w", "a", "g") for i in range(HP)]
    plan += [(("h", i), "act") for i in range(HP)] + [(ada_product(0, 7), "act")]
    plan += [(("b", i), "act") for i in range(HP)] + [(ada_product(0, 8), "act")]
    plan += [(("nrm", i), "act") for i in range(HP)]
    plan += [(("c", i), "dve") for i in range(HP)]
    plan += [(ada_product(0, cg), "act") for cg in (9, 10, 11)]
    plan += [(("bonus", i), "dve") for i in range(HP)]
    for s in range(SC):
        plan += [((n, s), "act") for n in ("trK", "trB", "trA", "trV")]
        plan += [((n, s, i), "dve") for i in range(HP) for n in ("UB", "UK")]
        plan += [(("LL", s, q), "dve") for q in range(2)]
        for n, e in (("D2", "act"), ("D2T", "act"), ("D4", "act"), ("P2", "dve"), ("D4T", "act"), ("D8T", "act"),
                     ("P4", "dve"), ("P8", "dve"), ("P8T", "act"), ("Y1", "act"), ("Pa", "dve"), ("PaT", "act"),
                     ("Y2", "act"), ("Pb", "dve")):
            plan += [((n, s, q), e) for q in range(2)]
        plan += [(("LakV", s), "act"), (("WT", s), "act"), (("U", s), "act")]
        for c in (2 * s, 2 * s + 1):
            plan += [(("SA", c), "dve")] + ([(("DS", c), "dve")] if c < NCH - 1 else []) + [(("Y", c), "act")]
    plan += [(("mean", i), "dve") for i in range(HP)]
    plan += [(("var", i), "act") for i in range(HP)]
    for l in range(2):
        if l:
            for g in range(GROUPS):
                plan += [(("q", g, i), "act") for i in range(HP)] + [(("k", g, i), "dve") for i in range(HP)]
                plan += [(("v", g, r), "act") for r in range(NR)]
            n = HEADS * NR
            for i in range(n + 2):
                if i < n:
                    plan += [(("S0", i), "dve"), (("S1", i), "dve")]
                if 1 <= i <= n:
                    plan += [(("PT0", i - 1), "act"), (("PT1", i - 1), "dve")]
                if i >= 2:
                    plan += [(("O", i - 2), "dve")]
            plan += [(("oT", r), "act") for r in range(NR)]
        plan += [(("y", l, 0, 0, n, r), "dve") for n in range(2) for r in range(NR)]
        plan += [(("nT", l, 0, r, n), "act" if n else "dve") for r in range(NR) for n in range(2)]
        for a in range(2):
            for f in range(FH):
                plan += [(("f", l, FH * a + f), "act")]
                if l == 0 and (FH * a + f) in ADA_AFTER:
                    plan += [(ada_product(1, ADA_AFTER[FH * a + f]), "act")]
            plan += [(("y", l, 1, a, n, r), "dve") for n in range(2) for r in range(NR)]
        if l == 0:
            plan += [(("nT", l, 1, r, n), "act" if n else "dve") for r in range(NR) for n in range(2)]
    return plan


ADA_AFTER = {2: 0, 4: 1, 6: 2, 8: 3, 10: 4, 12: 5, 18: 6, 20: 7, 22: 8, 24: 9, 26: 10, 28: 11}


def panel_list():
    out = [("ada", 0, cg, k) for cg in range(4) for k in range(2)]
    ada = [("ada", 0, cg, k) for cg in ADA_REST for k in range(2)]
    for k in range(14):
        out += [("in", k)]
        if k < 6:
            out += [ada.pop(0)]
        elif k >= 8:
            out += [ada.pop(0)] + ([ada.pop(0)] if k >= 10 else [])
    assert not ada
    out += [("wo", n, 1 - k) for n in range(2) for k in range(2)]
    for l in range(2):
        if l:
            for g in range(GROUPS):
                out += [("qkv", g, k) for k in range(4)] + [("wv", g, k) for k in range(2)]
            out += [("do", n) for n in range(2)]
        for a in range(2):
            later = [("ada", 1, cg, k) for cg in range(6 * a, 6 * a + 6) for k in range(2)] if l == 0 else []
            for k in range(8):
                out += [("w1", l, 8 * a + k)]
                for _ in range(2 if k < 6 else 0):
                    if later:
                        out += [later.pop(0)]
            assert not later
            out += [("w2", l, a, n, k) for n in range(2) for k in range(4)]
    return out


def half_panels(panels, number):
    out = []
    for i, p in enumerate(panels):
        kind = p[0]
        if kind == "ada":
            continue
        if kind in ("in", "qkv", "w1"):
            for n in range(1 if p == ("in", 7) else 2):
                if kind == "in":
                    k = p[1]
                    name = ("p", 2 * k + n) if k < 8 else ("hbc"[(k - 8) // 2], 2 * (k % 2) + n)
                elif kind == "qkv":
                    name = ("q" if p[2] < 2 else "k", p[1], 2 * (p[2] % 2) + n)
                else:
                    name = ("f", p[1], 2 * p[2] + n)
                out.append((i, n, name, name))
            continue
        if kind == "wv":
            group, last = ("v", p[1]), p[2] == 1
        elif kind == "wo":
            group, last = ("y", 0, 0, 0, p[1]), p[2] == 0
        elif kind == "do":
            group, last = ("y", 1, 0, 0, p[1]), True
        else:
            group, last = ("y", p[1], 1, p[2], p[3]), p[4] == 3
        for n in range(2):
            out.append((i, n, group + (NR - 1,) if last else None, group + (0,)))
    return out


ARENA = 200
RING = 3
SPLIT = 3


def trunk(nc, x, c, ada_w, ada_b, ln_g, ln_b, ab_w_in, rw_mu, rw_w0, rw_w_up, rw_a0, rw_a_up, rw_g_up, rw_k_k,
          rw_k_a, rw_r_k, rw_lnx_g, rw_lnx_b, sc_conv_w, ab_w_out, dil_w_qkv, dil_w_out, rel_bias, mlp_w1, mlp_w2,
          identity, masks, buckets, out, band_dram, skew_dram):
    plan = build_plan()
    number, freed_count, counts = {}, {}, {"act": 0, "dve": 0}
    for j, (name, reader) in enumerate(plan):
        counts[reader] += 1
        number[name] = j
        freed_count[name] = counts[reader]
    reader_of = dict(plan)
    panels = panel_list()
    halves = half_panels(panels, number)
    panel_no = {p: i for i, p in enumerate(panels)}

    with ExitStack() as ctx:
        def sb(name, shape):
            return ctx.enter_context(nc.sbuf_tensor(name, shape, F32))

        def sem(name):
            return ctx.enter_context(nc.semaphore(name))

        bank = [ctx.enter_context(nc.psum_tensor(f"bank{i}", [P, 512], F32)) for i in range(8)]

        ident = sb("ident", [P, P])
        block_ones = sb("block_ones", [P, P])
        block_mean = sb("block_mean", [P, P])
        ones_sq = sb("ones_sq", [P, P])[:, :]
        ones_col = ones_sq[:, 0:1]
        par = sb("par", [P, P])
        adab = sb("adab", [P, 96])
        cond = sb("cond", [P, 8])
        mod = sb("mod", [P, 2, 32])
        tiny = sb("tiny", [P, 216])
        mask = sb("mask", [P, 7, P])
        arena_at = (nc.sbuf_usable_end - ARENA * 1024) // 32 * 32
        assert arena_at >= nc.sbuf_base
        placed = [0]

        def rounded(name, kib, *shape):
            return nc.alloc_sbuf_tensor_at(name, [P, *shape], F32R, offset=arena_at + int(kib * 1024))

        assert masks.shape[1] == 7

        def at(kib, *shape):
            placed[0] += 1
            assert kib * 1024 + 4 * int(np.prod(shape)) <= ARENA * 1024
            t = nc.alloc_sbuf_tensor_at(f"part{placed[0]}", [P, *shape], F32, offset=arena_at + int(kib * 1024))
            return t[(slice(None),) * (1 + len(shape))]

        ring = [at(8 * i, 2048) for i in range(RING)]
        w_hi = [rounded(f"w_hi{i}", 24 + 8 * i, 1024) for i in range(SPLIT)]
        w_lo = [rounded(f"w_lo{i}", 28 + 8 * i, 1024) for i in range(SPLIT)]
        X0 = 56
        gate = [at(48, D), at(52, D), at(X0 + 120, D)]
        acc = [[gate[1][:, 0:512], gate[1][:, 512:1024]], [gate[2][:, 0:512], gate[2][:, 512:1024]]]
        rT, kT_, aT, bT = (at(X0 + 8 * i, HP, T) for i in range(4))
        vT, bonus, gt, ybT = (at(X0 + 32 + 8 * i, HP, T) for i in range(4))
        W0 = X0 + 64
        t8, t9, t10, t11 = (at(W0 + 8 * i, HP, T) for i in range(4))
        xin = at(W0, NR, D)
        ut_val = at(W0 + 16, KT, T)
        u0_hi, u0_lo = rounded("u0_hi", W0 + 32, KT, T), rounded("u0_lo", W0 + 48, KT, T)
        lr = at(W0 + 64, 4, RW)
        low = at(W0 + 72, 3, T)
        rawpar = at(X0, 3, P)
        wconst = at(X0 + 4, BAND * BW)
        bandv = at(X0 + 16, BAND * BW)
        relb = at(X0 + 2, GROUPS * HEADS)
        MB = at(W0, HEADS, 2, P)
        MK = at(W0 + 8, HEADS, 2, P)
        m0, m1, m2, m3, m4, m5, m6 = (at(W0 + 16 + 4 * i, HEADS, P) for i in range(7))
        arz = at(W0 + 44, HP, 2, 2, P)
        tokK, tokB, tokA, tokV = (at(W0 + 52 + 2 * i, HP, P) for i in range(4))
        vz = at(W0 + 60, 2, HP, P)
        saz = at(W0 + 64, 2, HP, P)
        lakv, uu, wt = (at(W0 + 68 + 2 * i, HP, P) for i in range(3))
        state = at(W0 + 74, 2, HP, P)
        xp = at(X0 + 64, NR, D)
        mix_hi, mix_lo = rounded("mix_hi", X0 + 80, 8, T), rounded("mix_lo", X0 + 96, 8, T)
        u_hi, u_lo = rounded("u_hi", X0 + 80, KT, T), rounded("u_lo", X0 + 96, KT, T)
        grow, brow = at(X0 + 112, D), at(X0 + 116, D)
        h_hi, h_lo = rounded("h_hi", X0, FH, T), rounded("h_lo", X0 + 32, FH, T)
        h_val = at(X0 + 124, 4, T)
        gn = at(X0 + 124, HP, T)
        u_val = at(X0 + 132, 2, T)
        ytmp = at(X0 + 136, 2, T)
        qT = at(X0, GROUPS, HP, T)
        kT = at(X0 + 24, GROUPS, HP, T)
        v_at = [at(X0 + 48, NR, RW), at(X0 + 56, NR, RW), at(X0 + 124, NR, RW)]
        otok = at(X0 + 112, NR, RW)
        o_hi, o_lo = rounded("o_hi", X0, HP, T), rounded("o_lo", X0 + 8, HP, T)
        oT = at(X0 + 16, HP, T)
        qpad = at(X0 + 80, 2, GROUPS, T)
        tab = [at(X0 + 92 + 4.5 * i, BAND * P) for i in range(2)]
        sS = at(X0 + 101, 3, 6 * P)
        pT = at(X0 + 132, 2, 6, P)
        assert X0 + 144 <= ARENA

        eps_ln, eps_gn = tiny[:, 0:1], tiny[:, 1:2]
        omm = tiny[:, 2:17]
        omka = tiny[:, 17:21]
        csum_end = tiny[:, 24:56]
        rho = tiny[:, 56:84]
        stats = tiny[:, 96:96 + 4 * 12]
        mv = tiny[:, 144:152]
        rstd = tiny[:, 152:156]
        nmr = tiny[:, 156:160]
        scl = tiny[:, 160:168]
        shf = tiny[:, 168:176]
        nmax = tiny[:, 176:180]
        den = tiny[:, 180:184]
        sg_c = tiny[:, 184:192]
        mx = tiny[:, 192:196]
        rden = tiny[:, 208:212]

        mm_done = sem("mm_done")
        freed = {"act": sem("read_by_act"), "dve": sem("read_by_dve")}
        slot_landed = [sem(f"slot_landed{i}") for i in range(RING)]
        raw_used = sem("raw_used")
        hi_ready, lo_ready = sem("hi_ready"), sem("lo_ready")
        half_used = sem("half_used")
        acc_ready = sem("acc_ready")
        u_value, u_hi_ready, u_lo_ready = sem("u_value"), sem("u_hi_ready"), sem("u_lo_ready")
        h_value, h_hi_ready, h_lo_ready = sem("h_value"), sem("h_hi_ready"), sem("h_lo_ready")
        o_hi_ready, o_lo_ready = sem("o_hi_ready"), sem("o_lo_ready")
        act_step, dve_step, pool_step = sem("act_step"), sem("dve_step"), sem("pool_step")
        consts_in, params_in, x_in, band_in = sem("consts_in"), sem("params_in"), sem("x_in"), sem("band_in")
        lowrank_in, xp_in, rows_in, tab_in = sem("lowrank_in"), sem("xp_in"), sem("rows_in"), [sem("tab_in0"), sem("tab_in1")]
        band_out, skewed = sem("band_out"), sem("skewed")
        raw_zero, cond_ready, block_ready = sem("raw_zero"), sem("cond_ready"), sem("block_ready")
        sig_c, mod_ready = sem("sig_c"), sem("mod_ready")
        low_ready, sq_ready, norm_root, cs_ready = sem("low_ready"), sem("sq_ready"), sem("norm_root"), sem("cs_ready")
        exps_ready, rk_ready, prods_ready = sem("exps_ready"), sem("rk_ready"), sem("prods_ready")
        arz_ready, vz_ready, p_ready, arz_zero = sem("arz_ready"), sem("vz_ready"), sem("p_ready"), sem("arz_zero")
        state_ready, chunk_done = sem("state_ready"), sem("chunk_done")
        gn_sq, gn_in, gn_root, ya_ready = sem("gn_sq"), sem("gn_in"), sem("gn_root"), sem("ya_ready")
        var_ready, root_ready, scale_ready, normed, resid_ready = (sem("var_ready"), sem("root_ready"), sem("scale_ready"),
                                                                    sem("normed"), sem("resid_ready"))
        x_split_hi, x_split_lo = sem("x_split_hi"), sem("x_split_lo")
        mix_hi_ready, mix_lo_ready = sem("mix_hi_ready"), sem("mix_lo_ready")
        q_padded, max_ready, exp_ready = sem("q_padded"), sem("max_ready"), sem("exp_ready")
        rden_ready = sem("rden_ready")
        out_stored = sem("out_stored")

        def wait_product(eng, name):
            eng.wait_ge(mm_done, number[name] + 1)
            return bank[number[name] % 8]

        def read(eng, *names):
            need = {}
            for n in names:
                need[reader_of[n]] = max(need.get(reader_of[n], 0), freed_count[n])
            for e, v in need.items():
                eng.wait_ge(freed[e], v)

        def panel_ap(p):
            kind = p[0]
            if kind == "ada":
                l, cg, k = p[1:]
                src = ada_w[l][512 * k:512 * k + 512, 512 * cg:512 * cg + 512]
            elif kind == "in":
                k = p[1]
                lo = 256 * k if k < 8 else PB + 256 * (k - 8)
                src = ab_w_in[0][:, lo:lo + (P if k == 7 else 256)]
            elif kind == "qkv":
                g, k = p[1:]
                src = dil_w_qkv[0][:, g * 1536 + 256 * k:g * 1536 + 256 * k + 256]
            elif kind == "w1":
                l, k = p[1:]
                src = mlp_w1[l][:, 256 * k:256 * k + 256]
            elif kind == "wo":
                n, k = p[1:]
                src = ab_w_out[0][512 * k:512 * k + 512, n * 512:n * 512 + 512]
            elif kind == "wv":
                g, k = p[1:]
                src = dil_w_qkv[0][512 * k:512 * k + 512, g * 1536 + 1024:g * 1536 + 1536]
            elif kind == "do":
                src = dil_w_out[0][:, p[1] * 512:p[1] * 512 + 512]
            else:
                l, a, n, k = p[1:]
                row = 512 * (4 * a + k)
                src = mlp_w2[l][row:row + 512, n * 512:n * 512 + 512]
            return src.rearrange("(t p) n -> p t n", p=P)

        def panel_tile(i):
            src = panel_ap(panels[i])
            t, n = src.shape[1], src.shape[2]
            return ring[i % RING][:, 0:t * n].rearrange("p (t n) -> p t n", t=t), src

        def half_of(h):
            i, n = halves[h][0:2]
            w = panel_tile(i)[0]
            if w.shape[1] == KT:
                return w[:, :, P * n:P * n + P]
            return w[:, 2 * n:2 * n + 2, :]

        def part(t, h):
            n = KT if half_of(h).shape[1] == KT else 2
            return t[h % SPLIT][:, :].rearrange("p (t n) -> p t n", t=n)

        def wait_landed(eng, i):
            eng.wait_ge(slot_landed[i % RING], 16 * (i // RING + 1))

        def wait_half_free(eng, h):
            if h >= SPLIT:
                end = halves[h - SPLIT][2]
                if end:
                    eng.wait_ge(mm_done, number[end] + 1)
                else:
                    eng.wait_ge(half_used, sum(not x[2] for x in halves[:h - SPLIT + 1]))

        def due(h):
            if h < SPLIT:
                return number[("x", 0)]
            end, first = halves[h - SPLIT][2:]
            return number[end or first]

        block = ctx.enter_context(nc.Block())

        @block.sync
        def _(sp):
            sp.dma_start(ident[:, :], identity).then_inc(consts_in, 16)
            sp.dma_start(mask[:, :, :], masks).then_inc(consts_in, 16)
            sp.dma_start(wconst[0:33, :], buckets).then_inc(band_in, 16)
            sp.dma_start(relb[0:32, :], rel_bias).then_inc(band_in, 16)
            sp.wait_ge(raw_zero, 1)

            def rows(name, n, src):
                sp.dma_start(rawpar[PAR[name]:PAR[name] + n, 0, :], src).then_inc(params_in, 16)

            rows("c", 8, c[0].rearrange("(r j) -> r j", j=P))
            rows("ln_g", 32, ln_g.rearrange("a b (r j) -> (a b r) j", j=P))
            rows("ln_b", 32, ln_b.rearrange("a b (r j) -> (a b r) j", j=P))
            rows("mu", 14, rw_mu[0, 0:14 * P].rearrange("(r j) -> r j", j=P))
            sp.dma_start(rawpar[PAR["mu"] + 14:PAR["mu"] + 15, 0, 0:32],
                         rw_mu[:, 14 * P:PB]).then_inc(params_in, 16)
            for name, v in (("w0", rw_w0), ("a0", rw_a0), ("k_k", rw_k_k), ("k_a", rw_k_a), ("lnx_g", rw_lnx_g),
                            ("lnx_b", rw_lnx_b)):
                rows(name, 4, v[0].rearrange("(r j) -> r j", j=P))
            sp.dma_start(rawpar[PAR["r_k"]:PAR["r_k"] + 4, 0, :],
                         rw_r_k[0].rearrange("(r e) j -> r (e j)", e=2)).then_inc(params_in, 16)
            rows("conv", 12, sc_conv_w[0].rearrange("k (r j) -> (k r) j", j=P))
            sp.dma_start(rawpar[0:96, 1, :], ada_b.rearrange("l (r j) -> (l r) j", j=P)).then_inc(params_in, 16)
            xr = x[0].rearrange("(l r) d -> r l d", r=NR)
            for r in range(NR):
                sp.dma_start(xin[:, r, :], xr[r]).then_inc(x_in, 16)
            for i in range(len(panels)):
                if i == 8:
                    sp.dma_start(lr[0:64, 0, :], rw_w_up[0]).then_inc(lowrank_in, 16)
                    sp.dma_start(lr[64:128, 1, :], rw_a_up[0]).then_inc(lowrank_in, 16)
                    sp.dma_start(lr[:, 2, :], rw_g_up[0, 0:P]).then_inc(lowrank_in, 16)
                    sp.dma_start(lr[0:32, 3, :], rw_g_up[0, P:GR]).then_inc(lowrank_in, 16)
                dst, src = panel_tile(i)
                if i >= RING:
                    sp.wait_ge(raw_used, i - RING + 1)
                sp.dma_start(dst, src).then_inc(slot_landed[i % RING], 16)

        @block.gpsimd
        def _(pool):
            steps = [0]

            def step(ins):
                steps[0] += 1
                ins.then_inc(pool_step, 1)
                pool.wait_ge(pool_step, steps[0])

            g = nc.gpsimd
            g.memset(rawpar[:, :, :], 0.0).then_inc(raw_zero, 1)
            pool.wait_ge(raw_zero, 1)
            g.memset(relb[32:33, :], 1.0).then_inc(raw_zero, 1)
            pool.wait_ge(raw_zero, 2)
            step(g.memset(eps_ln, LN_EPS))
            step(g.memset(eps_gn, GN_EPS))
            step(g.memset(ones_sq, 1.0))
            for t, value in ((block_ones, 1.0), (block_mean, 1.0 / HD)):
                step(g.memset(t[:, :], 0.0))
                step(g.memset(t[0:64, 0:64], value))
                step(g.memset(t[64:128, 64:128], value))
            step(g.memset(lr[64:128, 0, :], 0.0))
            g.memset(lr[0:64, 1, :], 0.0).then_inc(block_ready, 1)
            pool.wait_ge(block_ready, 1)
            read(pool, ("F", 4))
            g.dma_start(band_dram, bandv[0:HEADS, :]).then_inc(band_out, 16)
            pool.wait_ge(band_out, 16)
            for h in range(HEADS):
                src = bass.AP(tensor=band_dram.tensor, offset=band_dram.offset + h * BAND * BW,
                              ap=[[0, P], [1, BAND * BW]])
                g.dma_start(skew_dram[h], src).then_inc(skewed, 16)

            pool.wait_ge(arz_zero, 1)
            step(g.memset(arz[:, :, :, :, :], 0.0))
            step(g.memset(vz[:, :, :, :], 0.0))
            step(g.memset(saz[:, :, :, :], 0.0))
            g.memset(state[:, :, :, :], 0.0).then_inc(state_ready, 1)
            pool.wait_ge(state_ready, 1)
            for s in range(SC):
                if s:
                    pool.wait_ge(mm_done, number[("LL", s - 1, 1)] + 1)
                for e in range(2):
                    h = slice(64 * e, 64 * e + 64)
                    step(g.tensor_copy(arz[h, :, e, 0, :], aT[h, :, P * s:P * s + P]))
                    g.tensor_copy(arz[h, :, e, 1, :], rT[h, :, P * s:P * s + P]).then_inc(arz_ready, 1)
                    pool.wait_ge(arz_ready, 2 * s + e + 1)
                read(pool, ("trV", s))
                if s:
                    pool.wait_ge(mm_done, number[("Y", 2 * s - 1)] + 1)
                for e in range(2):
                    h = slice(64 * e, 64 * e + 64)
                    g.tensor_copy(vz[h, e, :, :], tokV[h, :, :]).then_inc(vz_ready, 1)
                    pool.wait_ge(vz_ready, 2 * s + e + 1)
            pool.wait_ge(mm_done, number[("Y", NCH - 1)] + 1)
            xr = x[0].rearrange("(l r) d -> r l d", r=NR)
            g.dma_start(xp, xr.rearrange("r l d -> l r d")).then_inc(xp_in, 16)

            for l in range(2):
                if l:
                    pool.wait_ge(mm_done, number[("v", GROUPS - 1, NR - 1)] + 1)
                    step(g.memset(qpad[:, :, :, :], 0.0))
                    for h in range(HEADS):
                        e, hp = h % 2, h // 2
                        rows_ = slice(64 * e, 64 * e + 64)
                        if h >= 2:
                            pool.wait_ge(mm_done, number[("S1", (h - 1) * NR - 1)] + 1)
                            read(pool, ("S1", (h - 1) * NR - 1))
                        elif h == 0:
                            pool.wait_ge(skewed, 16 * HEADS)
                            read(pool, ("q", 2, 3))
                        src = bass.AP(tensor=skew_dram.tensor, offset=skew_dram.offset + h * P * BAND * BW + P - 1,
                                      ap=[[BAND * BW - 1, P], [BW, BAND], [1, P]])
                        g.dma_start(tab[e].rearrange("p (b k) -> p b k", b=BAND), src).then_inc(tab_in[e], 16)
                        g.tensor_copy(qpad[rows_, e, :, :], qT[rows_, :, hp, :]).then_inc(q_padded, 1)
                        pool.wait_ge(q_padded, h + 1)
                for j in range(2):
                    if l and not j:
                        pool.wait_ge(mm_done, number[("oT", NR - 1)] + 1)
                    for dst, v in ((grow, ln_g), (brow, ln_b)):
                        src = bass.AP(tensor=v.tensor, offset=v.offset + (2 * l + j) * D, ap=[[0, P], [1, D]])
                        g.dma_start(dst, src).then_inc(rows_in, 16)
                    pool.wait_ge(rows_in, 32 * (2 * l + j + 1))
                    for r in range(NR):
                        if l and j:
                            pool.wait_ge(normed, 12 + r + 1)
                        else:
                            pool.wait_ge(mm_done, number[("nT", l, j, r, 1)] + 1)
                        step(g.tensor_tensor(xp[:, r, :], xp[:, r, :], grow, ALU.mult))
                        g.tensor_tensor(xp[:, r, :], xp[:, r, :], brow, ALU.add).then_inc(resid_ready, 1)
                        pool.wait_ge(resid_ready, 4 * (2 * l + j) + r + 1)
            outr = out[0].rearrange("(l r) d -> r l d", r=NR)
            for r in range(NR):
                pool.wait_ge(resid_ready, 12 + r + 1)
                g.dma_start(outr[r], xp[:, r, :]).then_inc(out_stored, 16)
            pool.wait_ge(out_stored, 64)

        @block.scalar
        def _(act):
            steps = [0]
            a = nc.scalar

            def step(ins):
                steps[0] += 1
                ins.then_inc(act_step, 1)
                act.wait_ge(act_step, steps[0])

            def done(ins):
                ins.then_inc(freed["act"], 1)

            at_half = [0]

            def product_ready(eng, name):
                while at_half[0] < len(halves) and due(at_half[0]) <= number[name]:
                    h = at_half[0]
                    at_half[0] += 1
                    wait_landed(act, halves[h][0])
                    wait_half_free(act, h)
                    a.copy(part(w_hi, h), half_of(h)).then_inc(hi_ready, 1)
                return wait_product(eng, name)

            for i in range(5):
                b = product_ready(act, ("F", i))
                w = min(512, BAND * BW - 512 * i)
                if i == 3:
                    a.copy(bandv[0:HEADS, 1536:1792], b[0:HEADS, 0:256])
                    ins = a.copy(bandv[0:HEADS, 1792:2048], b[0:HEADS, 256:512])
                else:
                    ins = a.copy(bandv[0:HEADS, 512 * i:512 * i + w], b[0:HEADS, 0:w])
                done(ins)
            read(act, ("par",))
            a.activation(sg_c, par[:, 0:8], ACT.Sigmoid).then_inc(sig_c, 1)

            for d in range(1, KT, 2):
                b = product_ready(act, ("x", d))
                act.wait_ge(mod_ready, 1)
                done(a.activation(ut_val[:, d, :].rearrange("p (l r) -> p r l", r=NR),
                                  b[:, :].rearrange("p (r l) -> p r l", r=NR), ACT.Identity,
                                  scale=mod[:, 0, 8 + d:9 + d], bias=mod[:, 0, d:d + 1]))
                for e in (d - 1, d):
                    read(act, ("x", e))
                    a.copy(u0_hi[:, e, :], ut_val[:, e, :]).then_inc(x_split_hi, 1)
            def ada_out(l, cg):
                name = ada_product(l, cg)
                b = product_ready(act, name)
                if name[0] == "mod":
                    k = ADA_COLS.index(cg)
                    done(a.copy(mod[:, l, 4 * k:4 * k + 4], b[:, 0:4]))
                else:
                    g, n = name[2:]
                    done(a.activation(gate[(0, 1, 0, 2)[2 * l + g]][:, 512 * n:512 * n + 512], b[:, :], ACT.Identity,
                                      bias=1.0))

            for cg in (4, 5, 6):
                ada_out(0, cg)
            product_ready(act, ("p", 14))
            read(act, ("p", 14))
            a.activation(low[0:64, 0, :], low[0:64, 0, :], ACT.Tanh)
            a.activation(low[:, 1, :], low[:, 1, :], ACT.Sigmoid)
            a.activation(low[0:32, 2, :], low[0:32, 2, :], ACT.Sigmoid).then_inc(low_ready, 1)
            act.wait_ge(band_out, 16)
            for i in range(HP):
                b = product_ready(act, ("w", i))
                done(a.activation(aT[:, i, :], b[:, :], ACT.Sigmoid, bias=par[:, PAR["w0"] + i:PAR["w0"] + i + 1]))
            for i in range(HP):
                b = product_ready(act, ("a", i))
                done(a.activation(bT[:, i, :], b[:, :], ACT.Sigmoid, bias=par[:, PAR["a0"] + i:PAR["a0"] + i + 1]))
            for i in range(HP):
                b = product_ready(act, ("g", i))
                done(a.copy(gt[:, i, :], b[:, :]))
            for i in range(HP):
                b = product_ready(act, ("h", i))
                done(a.copy(bonus[:, i, :], b[:, :]))
            ada_out(0, 7)
            for i in range(HP):
                b = product_ready(act, ("b", i))
                done(a.copy(ybT[:, i, :], b[:, :]))
            ada_out(0, 8)
            for i in range(HP):
                b = product_ready(act, ("nrm", i))
                done(a.activation(t9[:, i, :], b[:, :], ACT.Sqrt))
            act.wait_ge(cs_ready, 1)
            a.activation(t11, t10, ACT.Exp, scale=-KAPPA).then_inc(exps_ready, 1)
            a.activation(t10, t10, ACT.Exp, scale=KAPPA).then_inc(exps_ready, 1)
            a.activation(aT, aT, ACT.Exp, scale=KAPPA).then_inc(exps_ready, 1)
            a.activation(rho, rho, ACT.Exp, scale=KAPPA / 2).then_inc(exps_ready, 1)
            for cg in (9, 10, 11):
                ada_out(0, cg)

            for s in range(SC):
                if s:
                    act.wait_ge(mm_done, number[("Y", 2 * s - 1)] + 1)
                if s == 0:
                    act.wait_ge(arz_zero, 1)
                for n, dst in (("trK", tokK), ("trB", tokB), ("trA", tokA), ("trV", tokV)):
                    b = product_ready(act, (n, s))
                    done(a.copy(dst, b[:, :].rearrange("p (h k) -> p h k", h=HP)))
                where = {"D2": m3, "D2T": m0, "D4": m4, "D4T": m5, "D8T": m3, "P8T": m0, "Y1": m4, "PaT": m5, "Y2": m3}
                for n in ("D2", "D2T", "D4", "D4T", "D8T", "P8T", "Y1", "PaT", "Y2"):
                    for q in range(2):
                        b = product_ready(act, (n, s, q))
                        done(a.copy(where[n][:, 4 * q:4 * q + 4, :], b[:, :].rearrange("p (m k) -> p m k", m=4)))
                for n, dst in (("LakV", lakv), ("WT", wt), ("U", uu)):
                    b = product_ready(act, (n, s))
                    done(a.copy(dst, b[:, :].rearrange("p (h k) -> p h k", h=HP)))
                for c_ in (2 * s, 2 * s + 1):
                    b = product_ready(act, ("Y", c_))
                    done(a.copy(rT[:, :, CH * c_:CH * c_ + CH], b[:, 0:256].rearrange("p (h t) -> p h t", h=HP)))
            for i in range(HP):
                act.wait_ge(gn_in, i + 1)
                a.activation(gn[:, i, :], rT[:, i, :], ACT.Square).then_inc(gn_sq, 1)
            for i in range(HP):
                b = product_ready(act, ("var", i))
                done(a.activation(gn[:, i, :], b[:, :], ACT.Sqrt, bias=eps_gn))

            for i in range(HP):
                a.copy(mix_hi[:, i, :], ybT[:, i, :]).then_inc(mix_hi_ready, 1)
            for i in range(HP):
                act.wait_ge(ya_ready, i + 1)
                a.copy(mix_hi[:, 4 + i, :], rT[:, i, :]).then_inc(mix_hi_ready, 1)

            def norm(l, j):
                last = l == 1 and j == 1
                product_ready(act, ("y", l, j, j, 1, 0))
                for r in range(NR):
                    n = 4 * (2 * l + j) + r
                    act.wait_ge(var_ready, n + 1)
                    a.activation(rstd[:, r:r + 1], mv[:, 2 * r + 1:2 * r + 2], ACT.Sqrt, bias=eps_ln).then_inc(root_ready, 1)
                    act.wait_ge(scale_ready, n + 1)
                    a.activation(xp[:, r, :], xp[:, r, :], ACT.Identity, scale=rstd[:, r:r + 1],
                                 bias=nmr[:, r:r + 1]).then_inc(normed, 1)
                if last:
                    return
                for r in range(NR):
                    k = 8 * (2 * l + j) + 2 * r
                    b = product_ready(act, ("nT", l, j, r, 1))
                    if k:
                        act.wait_ge(u_lo_ready, k)
                    for d in range(4, 8):
                        ins = a.activation(u_val[:, 1, P * (d - 4):P * (d - 3)], b[:, P * (d - 4):P * (d - 3)],
                                           ACT.Identity, scale=scl[:, d:d + 1], bias=shf[:, d:d + 1])
                    done(ins)
                    for n in range(2):
                        read(act, ("nT", l, j, r, n))
                        a.copy(u_hi[:, 4 * n:4 * n + 4, P * r:P * r + P],
                               u_val[:, n, :].rearrange("p (d l) -> p d l", d=4)).then_inc(u_hi_ready, 1)

            def hidden_hi(k):
                act.wait_ge(h_value, k + 1)
                a.copy(h_hi[:, k % FH, :], h_val[:, k % 4, :]).then_inc(h_hi_ready, 1)

            def mlp(l):
                for a_ in range(2):
                    for f in range(FH * a_, FH * a_ + FH):
                        k = 2 * FH * l + f
                        b = product_ready(act, ("f", l, f))
                        if k >= 4:
                            act.wait_ge(h_lo_ready, k - 3)
                        done(a.activation(h_val[:, k % 4, :], b[:, :], ACT.Relu))
                        if f % FH:
                            hidden_hi(k - 1)
                        if l == 0 and f in ADA_AFTER:
                            ada_out(1, ADA_AFTER[f])
                    hidden_hi(k)
                    for n in range(2):
                        product_ready(act, ("y", l, 1, a_, n, 0))

            for l in range(2):
                if l:
                    for g in range(GROUPS):
                        for i in range(HP):
                            b = product_ready(act, ("q", g, i))
                            done(a.mul(qT[:, g, i, :], b[:, :], HD ** -0.5))
                        product_ready(act, ("k", g, 0))
                        for i in range(HP):
                            product_ready(act, ("k", g, i))
                        for r in range(NR):
                            b = product_ready(act, ("v", g, r))
                            done(a.copy(v_at[g][:, r, :], b[:, :]))
                    n = HEADS * NR
                    for i in range(n + 2):
                        if i < n:
                            act.wait_ge(max_ready, i + 1)
                            a.activation(sS[:, i % 3, :], sS[:, i % 3, :], ACT.Exp, bias=nmax[:, i % 4:i % 4 + 1],
                                         accum_out=den[:, i % 4:i % 4 + 1]).then_inc(exp_ready, 1)
                        if 1 <= i <= n:
                            b = product_ready(act, ("PT0", i - 1))
                            done(a.copy(pT[:, (i - 1) % 2, 0:4, :], b[:, :].rearrange("p (m k) -> p m k", m=4)))
                    for r in range(NR):
                        b = product_ready(act, ("oT", r))
                        done(a.copy(oT[:, :, P * r:P * r + P], b[:, :].rearrange("p (h t) -> p h t", h=HP)))
                        read(act, ("oT", r))
                        a.copy(o_hi[:, :, P * r:P * r + P], oT[:, :, P * r:P * r + P]).then_inc(o_hi_ready, 1)
                product_ready(act, ("y", l, 0, 0, 0, 0))
                norm(l, 0)
                mlp(l)
                norm(l, 1)

        @block.vector
        def _(dve):
            steps = [0]
            v = nc.vector

            def step(ins):
                steps[0] += 1
                ins.then_inc(dve_step, 1)
                dve.wait_ge(dve_step, steps[0])

            def done(ins):
                ins.then_inc(freed["dve"], 1)

            at_half, at_panel = [0], [0]

            def sum_panel(p):
                l, cg, k = p[1:]
                i = at_panel[0]
                wait_landed(dve, i)
                w, dst = panel_tile(i)[0], acc[l][cg % 2]
                if k == 0 and cg >= 2:
                    dve.wait_ge(mm_done, number[ada_product(l, cg - 2)] + 1)
                for t in range(4):
                    s = cond[:, 4 * k + t:4 * k + t + 1]
                    if k + t == 0:
                        step(v.tensor_scalar(dst, w[:, t, :], s, None, ALU.mult))
                    elif t < 3:
                        step(v.scalar_tensor_tensor(dst, w[:, t, :], s, dst, ALU.mult, ALU.add))
                v.scalar_tensor_tensor(dst, w[:, 3, :], s, dst, ALU.mult, ALU.add).then_inc(raw_used, 1)
                dve.wait_ge(raw_used, i + 1)
                if k:
                    v.tensor_copy(tiny[:, 204:205], dst[:, 0:1]).then_inc(acc_ready, 1)
                at_panel[0] += 1

            def sum_panels():
                while at_panel[0] < len(panels) and panels[at_panel[0]][0] == "ada":
                    sum_panel(panels[at_panel[0]])

            def keep_up(name):
                while at_half[0] < len(halves) and due(at_half[0]) <= number[name]:
                    h = at_half[0]
                    at_half[0] += 1
                    sum_panels()
                    i = halves[h][0]
                    assert i == at_panel[0]
                    dve.wait_ge(hi_ready, h + 1)
                    ins = v.tensor_tensor(part(w_lo, h), half_of(h), part(w_hi, h).bitcast(F32), ALU.subtract)
                    if h + 1 < len(halves) and halves[h + 1][0] == i:
                        ins.then_inc(lo_ready, 1)
                    else:
                        ins.then_inc(lo_ready, 1)
                        dve.wait_ge(lo_ready, h + 1)
                        v.tensor_copy(tiny[:, 205:206], tiny[:, 0:1]).then_inc(raw_used, 1)
                        at_panel[0] += 1

            def product_ready(eng, name):
                keep_up(name)
                return wait_product(eng, name)

            b = product_ready(dve, ("par",))
            v.tensor_copy(par[:, :], b[:, 0:P])
            done(v.tensor_copy(adab[:, :], b[:, P:P + 96]))
            read(dve, ("par",))
            v.tensor_scalar(omm, par[:, PAR["mu"]:PAR["mu"] + 15], -1.0, 1.0, ALU.mult, ALU.add)
            v.tensor_scalar(omka, par[:, PAR["k_a"]:PAR["k_a"] + 4], -1.0, 1.0, ALU.mult, ALU.add)
            dve.wait_ge(sig_c, 1)
            step(v.tensor_tensor(cond[:, :], sg_c, par[:, 0:8], ALU.mult))
            sum_panels()
            for k in range(4):
                b = product_ready(dve, ("mod", 0, k))
                done(v.scalar_tensor_tensor(mod[:, 0, 4 * k:4 * k + 4], b[:, 0:4], float(k >= 2),
                                            adab[:, 4 * k:4 * k + 4], ALU.add, ALU.add))
            read(dve, ("mod", 0, 3))
            v.tensor_copy(tiny[:, 203:204], mod[:, 0, 0:1]).then_inc(mod_ready, 1)
            for d in range(0, KT, 2):
                b = product_ready(dve, ("x", d))
                done(v.tensor_scalar(ut_val[:, d, :].rearrange("p (l r) -> p r l", r=NR),
                                     b[:, :].rearrange("p (r l) -> p r l", r=NR), mod[:, 0, 8 + d:9 + d],
                                     mod[:, 0, d:d + 1], ALU.mult, ALU.add))
            for d in range(KT):
                dve.wait_ge(x_split_hi, d + 1)
                v.tensor_tensor(u0_lo[:, d, :], ut_val[:, d, :], u0_hi[:, d, :].bitcast(F32), ALU.subtract)\
                    .then_inc(x_split_lo, 1)
            for i in range(15):
                b = product_ready(dve, ("p", i))
                rows_ = 32 if i == 14 else P
                dst = (rT, kT_, vT)[i // 4][:, i % 4, :] if i < 12 else low[:, i - 12, :]
                dst = dst[0:rows_]
                step(v.tensor_scalar(dst, b[0:rows_, :], omm[0:rows_, i:i + 1], None, ALU.mult))
                done(v.scalar_tensor_tensor(dst[:, 1:T], b[0:rows_, 0:T - 1], par[0:rows_, PAR["mu"] + i:PAR["mu"] + i + 1],
                                            dst[:, 1:T], ALU.mult, ALU.add))
            read(dve, ("p", 14))
            for i in range(HP):
                step(v.tensor_scalar(t8[:, i, :], kT_[:, i, :], par[:, PAR["k_k"] + i:PAR["k_k"] + i + 1], None, ALU.mult))
            v.tensor_tensor(t9, t8, t8, ALU.mult).then_inc(sq_ready, 1)
            dve.wait_ge(sq_ready, 1)
            keep_up(("h", 0))
            read(dve, ("a", 3))
            for i in range(HP):
                step(v.tensor_scalar(t10[:, i, :], bT[:, i, :], par[:, PAR["k_a"] + i:PAR["k_a"] + i + 1],
                                     omka[:, i:i + 1], ALU.mult, ALU.add))
            step(v.tensor_tensor(kT_, kT_, t10, ALU.mult))
            keep_up(("h", 1))
            def chunks(t):
                return t.rearrange("p h (c s) -> p (h c) s", s=CH)

            src, spare = aT, [t10, t11]
            for n, sh in enumerate((1, 2, 4, 8, 16, 32)):
                dst = spare[n % 2]
                v.tensor_copy(chunks(dst)[:, :, 0:sh], chunks(src)[:, :, 0:sh])
                step(v.tensor_tensor(chunks(dst)[:, :, sh:], chunks(src)[:, :, sh:], chunks(src)[:, :, :CH - sh], ALU.add))
                src = dst
                keep_up((("h", 2), ("h", 3), ("b", 0), ("b", 1), ("b", 2), ("b", 2))[n])
            ends = chunks(t11)[:, :, CH - 1]
            step(v.tensor_copy(csum_end, ends))
            ce = csum_end.rearrange("p (h c) -> p h c", c=NCH)
            step(v.tensor_tensor(rho.rearrange("p (h c) -> p h c", c=NCH - 1), ce[:, :, 0:NCH - 1], ce[:, :, 1:NCH], ALU.add))
            step(v.tensor_scalar(csum_end, csum_end, 0.5, None, ALU.mult))
            step(v.tensor_tensor(chunks(t10), chunks(t11), csum_end.unsqueeze(2).broadcast_to((P, HP * NCH, CH)), ALU.subtract))
            v.tensor_tensor(aT, t10, aT, ALU.subtract).then_inc(cs_ready, 1)
            keep_up(("b", 3))
            read(dve, ("nrm", 3))
            step(v.tensor_scalar(t9, t9, 1e-12, None, ALU.max))
            step(v.reciprocal(t9, t9))
            step(v.tensor_tensor(t8, t8, t9, ALU.mult))
            for i in range(HP):
                step(v.scalar_tensor_tensor(t9[:, i, :], rT[:, i, :], par[:, PAR["r_k"] + i:PAR["r_k"] + i + 1],
                                            kT_[:, i, :], ALU.mult, ALU.mult))
            v.tensor_copy(tiny[:, 200:201], t9[:, 0, 0:1]).then_inc(rk_ready, 1)
            dve.wait_ge(exps_ready, 4)
            step(v.scalar_tensor_tensor(aT, t8, -1.0, aT, ALU.mult, ALU.mult))
            step(v.tensor_tensor(bT, bT, t8, ALU.mult))
            step(v.tensor_tensor(bT, bT, t11, ALU.mult))
            step(v.tensor_tensor(kT_, kT_, t11, ALU.mult))
            v.tensor_tensor(rT, rT, t10, ALU.mult).then_inc(prods_ready, 1)
            dve.wait_ge(prods_ready, 1)
            for i in range(HP):
                b = product_ready(dve, ("c", i))
                read(dve, ("b", 3))
                done(v.tensor_tensor(t8[:, i, :], b[:, :], bonus[:, i, :], ALU.mult))
                read(dve, ("c", i))

                def tap(k):
                    return par[:, PAR["conv"] + 4 * k + i:PAR["conv"] + 4 * k + i + 1]

                step(v.tensor_scalar(t10[:, i, :], t8[:, i, :], tap(2), None, ALU.mult))
                step(v.scalar_tensor_tensor(t10[:, i, 1:T], t8[:, i, 0:T - 1], tap(1), t10[:, i, 1:T], ALU.mult, ALU.add))
                step(v.scalar_tensor_tensor(t10[:, i, 2:T], t8[:, i, 0:T - 2], tap(0), t10[:, i, 2:T], ALU.mult, ALU.add))
                step(v.tensor_tensor(ybT[:, i, :], ybT[:, i, :], t10[:, i, :], ALU.mult))
            for i in range(HP):
                b = product_ready(dve, ("bonus", i))
                done(v.tensor_tensor(bonus[:, i, :], b[:, :], vT[:, i, :], ALU.mult))
            read(dve, ("bonus", 3))
            v.tensor_copy(tiny[:, 201:202], tiny[:, 0:1]).then_inc(arz_zero, 1)
            read(dve, ada_product(0, 11))
            v.tensor_tensor(mod[:, 0, 16:24], mod[:, 0, 16:24], adab[:, 24:32], ALU.add)
            step(v.scalar_tensor_tensor(mod[:, 0, 24:32], mod[:, 0, 24:32], 1.0, adab[:, 32:40], ALU.add, ALU.add))

            def msk(lo, n, *shape):
                m = mask[:, lo:lo + n, :]
                return m if n > 1 else mask[:, lo, :]

            for s in range(SC):
                for i in range(HP):
                    for n, dst, lo in (("UB", MB, 0), ("UK", MK, 2)):
                        b = product_ready(dve, (n, s, i))
                        m = mask[:, lo:lo + 2, :].rearrange("p a k -> p (a k)").unsqueeze(1).broadcast_to((P, 2, 2 * P))
                        done(v.tensor_tensor(dst[:, 2 * i:2 * i + 2, :, :].rearrange("p m a k -> p m (a k)"),
                                             b[:, :].rearrange("p (m k) -> p m k", m=2), m, ALU.mult))
                for q in range(2):
                    b = product_ready(dve, ("LL", s, q))
                    for j, dst in ((4, m0), (5, m1), (6, m2)):
                        m = mask[:, j, :].unsqueeze(1).broadcast_to((P, 4, P))
                        ins = v.tensor_tensor(dst[:, 4 * q:4 * q + 4, :], b[:, :].rearrange("p (m k) -> p m k", m=4), m,
                                              ALU.mult)
                    done(ins)
                read(dve, ("LL", s, 1))
                v.tensor_tensor(m6, MB[:, :, 0, :], ident[:, :].unsqueeze(1).broadcast_to((P, HEADS, P)), ALU.add)\
                    .then_inc(p_ready, 1)
                dve.wait_ge(p_ready, s + 1)
                for n in ("P2", "P4", "P8", "Pa", "Pb"):
                    for q in range(2):
                        b = product_ready(dve, (n, s, q))
                        done(v.tensor_tensor(m6[:, 4 * q:4 * q + 4, :], b[:, :].rearrange("p (m k) -> p m k", m=4),
                                             m6[:, 4 * q:4 * q + 4, :], ALU.add))
                    read(dve, (n, s, 1))
                for c_ in (2 * s, 2 * s + 1):
                    p_ = c_ % 2
                    h = slice(64 * p_, 64 * p_ + 64)
                    b = product_ready(dve, ("SA", c_))
                    read(dve, ("U", s))
                    if c_ == 0:
                        dve.wait_ge(state_ready, 1)
                    done(v.tensor_tensor(saz[h, p_, :, :], b[h, :].rearrange("p (h k) -> p h k", h=HP), uu[h, :, :], ALU.add))
                    if c_ == NCH - 1:
                        continue
                    b = product_ready(dve, ("DS", c_))
                    old, new = state[:, c_ % 2, :, :], state[:, (c_ + 1) % 2, :, :]
                    rc = rho.rearrange("p (h c) -> p h c", c=NCH - 1)[:, :, c_]
                    bb = b[:, :].rearrange("p (h k) -> p h k", h=HP)
                    if c_:
                        product_ready(dve, ("Y", c_ - 1))
                    for e in range(2):
                        g = slice(64 * e, 64 * e + 64)
                        k = slice(64 * e, 64 * e + 64)
                        ins = v.tensor_tensor(new[g, :, k], bb[g, :, k], old[g, :, k], ALU.add)
                    step(ins)
                    for e in range(2):
                        g = slice(64 * e, 64 * e + 64)
                        k = slice(64 * e, 64 * e + 64)
                        ins = v.tensor_tensor(new[g, :, k], new[g, :, k],
                                              rc[g].unsqueeze(2).broadcast_to((64, HP, 64)), ALU.mult)
                    done(ins)
            for i in range(HP):
                b = product_ready(dve, ("mean", i))
                v.tensor_tensor(rT[:, i, :], rT[:, i, :], b[:, :], ALU.subtract).then_inc(freed["dve"], 1)
                read(dve, ("mean", i))
                v.tensor_copy(tiny[:, 202:203], rT[:, i, 0:1]).then_inc(gn_in, 1)
            for i in range(HP):
                dve.wait_ge(mix_hi_ready, i + 1)
                v.tensor_tensor(mix_lo[:, i, :], ybT[:, i, :], mix_hi[:, i, :].bitcast(F32), ALU.subtract)\
                    .then_inc(mix_lo_ready, 1)
            for i in range(HP):
                read(dve, ("var", i))
                step(v.reciprocal(gn[:, i, :], gn[:, i, :]))
                step(v.tensor_tensor(rT[:, i, :], rT[:, i, :], gn[:, i, :], ALU.mult))
                step(v.tensor_scalar(rT[:, i, :], rT[:, i, :], par[:, PAR["lnx_g"] + i:PAR["lnx_g"] + i + 1],
                                     par[:, PAR["lnx_b"] + i:PAR["lnx_b"] + i + 1], ALU.mult, ALU.add))
                step(v.tensor_tensor(rT[:, i, :], rT[:, i, :], bonus[:, i, :], ALU.add))
                v.tensor_tensor(rT[:, i, :], rT[:, i, :], gt[:, i, :], ALU.mult).then_inc(ya_ready, 1)
                dve.wait_ge(mix_hi_ready, HP + i + 1)
                v.tensor_tensor(mix_lo[:, 4 + i, :], rT[:, i, :], mix_hi[:, 4 + i, :].bitcast(F32), ALU.subtract)\
                    .then_inc(mix_lo_ready, 1)

            def norm(l, j):
                if not (l == 1 and j == 1):
                    l2, o = (l, 16) if j == 0 else (1, 0)
                    base = (2 * l + j) * 8
                    step(v.tensor_tensor(scl, par[:, PAR["ln_g"] + base:PAR["ln_g"] + base + 8], mod[:, l2, o + 8:o + 16], ALU.mult))
                    step(v.tensor_tensor(shf, par[:, PAR["ln_b"] + base:PAR["ln_b"] + base + 8], mod[:, l2, o + 8:o + 16], ALU.mult))
                    step(v.tensor_tensor(shf, shf, mod[:, l2, o:o + 8], ALU.add))
                residual(l, j, j)
                if l == 1 and j == 1:
                    return
                for r in range(NR):
                    k = 8 * (2 * l + j) + 2 * r
                    b = product_ready(dve, ("nT", l, j, r, 0))
                    if k:
                        dve.wait_ge(u_lo_ready, k)
                    for d in range(4):
                        ins = v.tensor_scalar(u_val[:, 0, P * d:P * d + P], b[:, P * d:P * d + P], scl[:, d:d + 1],
                                              shf[:, d:d + 1], ALU.mult, ALU.add)
                    done(ins)
                    for n in range(2):
                        dve.wait_ge(u_hi_ready, k + n + 1)
                        t = slice(P * r, P * r + P)
                        v.tensor_tensor(u_lo[:, 4 * n:4 * n + 4, t], u_val[:, n, :].rearrange("p (d l) -> p d l", d=4),
                                        u_hi[:, 4 * n:4 * n + 4, t].bitcast(F32), ALU.subtract).then_inc(u_lo_ready, 1)

            def residual(l, j, a_):
                gr = gate[(0, 1, 0, 2)[2 * l + j]]
                for n in range(2):
                    cols = slice(512 * n, 512 * n + 512)
                    for r in range(NR):
                        if r < NR - 1 or n == 0 or a_ < j:
                            keep_up(("y", l, j, a_, n, r))
                        b = wait_product(dve, ("y", l, j, a_, n, r))
                        if a_ == 0 and n == 0:
                            if l == 0 and j == 0:
                                dve.wait_ge(xp_in, 16)
                            else:
                                dve.wait_ge(resid_ready, 4 * (2 * l + j - 1) + r + 1)
                        done(v.tensor_tensor(ytmp[:, r % 2, :], b[:, :], gr[:, cols], ALU.mult))
                        read(dve, ("y", l, j, a_, n, r))
                        step(v.scalar_tensor_tensor(xp[:, r, cols], xp[:, r, cols], 1.0 if a_ else ALPHA, ytmp[:, r % 2, :],
                                                    ALU.mult, ALU.add))
                        if a_ == j:
                            step(v.bn_stats(stats[:, 12 * r + 6 * n:12 * r + 6 * n + 6], xp[:, r, cols]))
                            if n == 1:
                                k = 4 * (2 * l + j) + r
                                v.bn_aggr(mv[:, 2 * r:2 * r + 2], stats[:, 12 * r:12 * r + 12]).then_inc(var_ready, 1)
                                dve.wait_ge(root_ready, k + 1)
                                step(v.reciprocal(rstd[:, r:r + 1], rstd[:, r:r + 1]))
                                v.scalar_tensor_tensor(nmr[:, r:r + 1], mv[:, 2 * r:2 * r + 1], -1.0, rstd[:, r:r + 1],
                                                       ALU.mult, ALU.mult).then_inc(scale_ready, 1)

            def hidden_lo(k):
                dve.wait_ge(h_hi_ready, k + 1)
                v.tensor_tensor(h_lo[:, k % FH, :], h_val[:, k % 4, :], h_hi[:, k % FH, :].bitcast(F32), ALU.subtract)\
                    .then_inc(h_lo_ready, 1)

            for l in range(2):
                if l:
                    for g in range(GROUPS):
                        for i in range(HP):
                            b = product_ready(dve, ("k", g, i))
                            done(v.tensor_copy(kT[:, g, i, :], b[:, :]))
                        keep_up(("v", g, 0))
                    n = HEADS * NR
                    for i in range(n + 2):
                        if i < n:
                            h, r = i // NR, i % NR
                            if r == 0:
                                dve.wait_ge(tab_in[h % 2], 16 * (h // 2 + 1))
                            if i >= 3:
                                dve.wait_ge(mm_done, number[("PT1", i - 3)] + 1)
                            t = tab[h % 2]
                            b = product_ready(dve, ("S0", i))
                            done(v.tensor_tensor(sS[:, i % 3, 0:512], b[:, :], t[:, (3 - r) * P:(7 - r) * P], ALU.add))
                            b = product_ready(dve, ("S1", i))
                            done(v.tensor_tensor(sS[:, i % 3, 512:768], b[:, 0:256], t[:, 7 * P:9 * P], ALU.add))
                            read(dve, ("S1", i))
                            if i >= 4:
                                dve.wait_ge(exp_ready, i - 3)
                            step(v.tensor_reduce(mx[:, i % 4:i % 4 + 1], sS[:, i % 3, :], AX.X, ALU.max))
                            v.tensor_scalar(nmax[:, i % 4:i % 4 + 1], mx[:, i % 4:i % 4 + 1], -1.0, None,
                                            ALU.mult).then_inc(max_ready, 1)
                        if 1 <= i <= n:
                            k = i - 1
                            b = product_ready(dve, ("PT1", k))
                            done(v.tensor_copy(pT[:, k % 2, 4:6, :], b[:, 0:256].rearrange("p (m k) -> p m k", m=2)))
                            dve.wait_ge(exp_ready, k + 1)
                            v.reciprocal(rden[:, k % 4:k % 4 + 1], den[:, k % 4:k % 4 + 1]).then_inc(rden_ready, 1)
                        if i >= 2:
                            k = i - 2
                            h, r = k // NR, k % NR
                            b = product_ready(dve, ("O", k))
                            dve.wait_ge(rden_ready, k + 1)
                            done(v.tensor_scalar(otok[:, r, HD * h:HD * h + HD], b[:, 0:HD], rden[:, k % 4:k % 4 + 1], None,
                                                 ALU.mult))
                    for r in range(NR):
                        dve.wait_ge(o_hi_ready, r + 1)
                        t = slice(P * r, P * r + P)
                        v.tensor_tensor(o_lo[:, :, t], oT[:, :, t], o_hi[:, :, t].bitcast(F32), ALU.subtract)\
                            .then_inc(o_lo_ready, 1)
                norm(l, 0)
                for a_ in range(2):
                    for f in range(FH * a_, FH * a_ + FH):
                        k = 2 * FH * l + f
                        product_ready(dve, ("f", l, f))
                        read(dve, ("f", l, f))
                        v.tensor_tensor(h_val[:, k % 4, :], h_val[:, k % 4, :], h_val[:, k % 4, :], ALU.mult)\
                            .then_inc(h_value, 1)
                        if f % FH:
                            hidden_lo(k - 1)
                    hidden_lo(k)
                    if a_ == 0:
                        residual(l, 1, 0)
                if l == 0:
                    read(dve, ada_product(1, 11))
                    a1 = 48
                    v.tensor_tensor(mod[:, 1, 0:8], mod[:, 1, 0:8], adab[:, a1:a1 + 8], ALU.add)
                    v.tensor_tensor(mod[:, 1, 16:24], mod[:, 1, 16:24], adab[:, a1 + 24:a1 + 32], ALU.add)
                    v.scalar_tensor_tensor(mod[:, 1, 8:16], mod[:, 1, 8:16], 1.0, adab[:, a1 + 8:a1 + 16], ALU.add, ALU.add)
                    step(v.scalar_tensor_tensor(mod[:, 1, 24:32], mod[:, 1, 24:32], 1.0, adab[:, a1 + 32:a1 + 40], ALU.add, ALU.add))
                norm(l, 1)

        @block.tensor
        def _(pe):
            at_job, at_half = [0], [0]

            def start(name, offset=0):
                j = at_job[0]
                assert plan[j][0] == name, (plan[j], name)
                at_job[0] += 1
                if j >= 8:
                    read(pe, plan[j - 8][0])
                return bank[j % 8]

            def finish(ins):
                ins.then_inc(mm_done, 1)

            def half_panel():
                h = at_half[0]
                at_half[0] += 1
                pe.wait_ge(lo_ready, h + 1)
                return part(w_hi, h), part(w_lo, h)

            mm = pe.matmul

            def mm3(out_, left, right, first, last):
                mm(out_, left[0], right[0], start=first, stop=False)
                mm(out_, left[1], right[0], start=False, stop=False)
                return mm(out_, left[0], right[1], start=False, stop=last)

            def transpose4(b, parts):
                for i, src in enumerate(parts):
                    ins = pe.transpose(b[:, P * i:P * i + P], src, ident[:, :])
                return ins

            pe.wait_ge(band_in, 32)
            pe.wait_ge(raw_zero, 2)
            for i in range(5):
                b = start(("F", i))
                if i < 3:
                    ins = mm(b[0:HEADS, :], relb[0:33, 0:8], wconst[0:33, 512 * i:512 * i + 512], start=True, stop=True)
                elif i == 3:
                    mm(b[0:HEADS, 0:256], relb[0:33, 0:8], wconst[0:33, 1536:1792], start=True, stop=True)
                    ins = mm(b[0:HEADS, 256:512], relb[0:33, 8:16], wconst[0:33, 1792:2048], start=True, stop=True)
                else:
                    ins = mm(b[0:HEADS, 0:256], relb[0:33, 16:24], wconst[0:33, 2048:2304], start=True, stop=True)
                finish(ins)
            pe.wait_ge(block_ready, 1)
            pe.wait_ge(params_in, 16 * 14)
            pe.wait_ge(consts_in, 32)
            b = start(("par",))
            pe.transpose(b[:, 0:P], rawpar[:, 0, :], ident[:, :])
            finish(pe.transpose(b[:, P:2 * P], rawpar[:, 1, :], ident[:, :]))
            ada_done = [0]

            def ada(l, cg):
                name = ada_product(l, cg)
                b = start(name)
                ada_done[0] += 1
                pe.wait_ge(acc_ready, ada_done[0])
                src = acc[l][cg % 2]
                if name[0] == "mod":
                    for n in range(4):
                        ins = mm(b[:, n:n + 1], src[:, P * n:P * n + P], ones_col, start=True, stop=True)
                else:
                    for i in range(4):
                        col = 48 * l + 4 * cg + i
                        mm(b[:, P * i:P * i + P], adab[:, col:col + 1].broadcast_to((P, P)), ident[:, :], start=(i == 0),
                           stop=False, skip_group_check=True)
                    ins = mm(b[:, :], ones_sq, src, start=False, stop=True, skip_group_check=True)
                finish(ins)

            for cg in range(4):
                ada(0, cg)
            pe.wait_ge(x_in, 64)
            for d in range(KT):
                b = start(("x", d))
                finish(transpose4(b, [xin[:, r, P * d:P * d + P] for r in range(NR)]))

            def feature_tile(name, hi, lo):
                b = start(name)
                wh, wl = half_panel()
                for t in range(KT):
                    ins = mm3(b[:, :], (wh[:, t, :], wl[:, t, :]), (hi[:, t, :], lo[:, t, :]), t == 0, t == KT - 1)
                finish(ins)

            pe.wait_ge(x_split_lo, KT)
            for i in range(15):
                feature_tile(("p", i), u0_hi, u0_lo)
                if i in (5, 9, 13):
                    ada(0, i // 4 + 3)
            pe.wait_ge(lowrank_in, 64)
            pe.wait_ge(block_ready, 1)
            pe.wait_ge(low_ready, 1)
            for n, j in (("w", 0), ("a", 1)):
                for i in range(HP):
                    b = start((n, i))
                    finish(mm(b[:, :], lr[:, j, P * i:P * i + P], low[:, 0, :], start=True, stop=True))
            for i in range(HP):
                b = start(("g", i))
                mm(b[:, :], lr[:, 2, P * i:P * i + P], low[:, 1, :], start=True, stop=False)
                finish(mm(b[:, :], lr[0:32, 3, P * i:P * i + P], low[0:32, 2, :], start=False, stop=True))
            for i in range(HP):
                feature_tile(("h", i), u0_hi, u0_lo)
            ada(0, 7)
            for i in range(HP):
                feature_tile(("b", i), u0_hi, u0_lo)
            ada(0, 8)
            pe.wait_ge(sq_ready, 1)
            for i in range(HP):
                b = start(("nrm", i))
                finish(mm(b[:, :], block_ones[:, :], t9[:, i, :], start=True, stop=True))
            for i in range(HP):
                feature_tile(("c", i), u0_hi, u0_lo)
            for cg in (9, 10, 11):
                ada(0, cg)
            pe.wait_ge(rk_ready, 1)
            for i in range(HP):
                b = start(("bonus", i))
                finish(mm(b[:, :], block_ones[:, :], t9[:, i, :], start=True, stop=True))

            pe.wait_ge(prods_ready, 1)
            for s in range(SC):
                tk = slice(P * s, P * s + P)
                for n, src in (("trK", kT_), ("trB", bT), ("trA", aT), ("trV", vT)):
                    b = start((n, s))
                    finish(transpose4(b, [src[:, i, tk] for i in range(HP)]))
                pe.wait_ge(arz_ready, 2 * s + 2)
                for i in range(HP):
                    for n, src in (("UB", bT), ("UK", kT_)):
                        b = start((n, s, i))
                        for e in range(2):
                            ins = mm(b[:, 256 * e:256 * e + 256], src[:, i, tk],
                                     arz[:, i, e, :, :].rearrange("p a k -> p (a k)"), start=True, stop=True)
                        finish(ins)
                for q in range(2):
                    b = start(("LL", s, q))
                    for j in range(4):
                        h = 4 * q + j
                        ins = mm(b[:, P * j:P * j + P], arz[:, h // 2, h % 2, 0, :], bT[:, h // 2, tk], start=True, stop=True)
                    finish(ins)
                pe.wait_ge(p_ready, s + 1)

                def each(name, left, right, *after):
                    for q in range(2):
                        b = start((name, s, q))
                        for a_ in after:
                            read(pe, (a_, s, q))
                        for j in range(4):
                            ins = mm(b[:, P * j:P * j + P], left(4 * q + j), right(4 * q + j), start=True, stop=True)
                        finish(ins)

                def turned(name, src, after):
                    for q in range(2):
                        b = start((name, s, q))
                        read(pe, (after, s, q))
                        finish(transpose4(b, [src[:, 4 * q + j, :] for j in range(4)]))

                each("D2", lambda h: m0[:, h, :], lambda h: MB[:, h, 0, :])
                turned("D2T", m3, "D2")
                each("D4", lambda h: m0[:, h, :], lambda h: m3[:, h, :], "D2T")
                each("P2", lambda h: m0[:, h, :], lambda h: m6[:, h, :], "D2T")
                turned("D4T", m4, "D4")
                each("D8T", lambda h: m4[:, h, :], lambda h: m5[:, h, :], "D4T")
                each("P4", lambda h: m5[:, h, :], lambda h: m6[:, h, :], "P2")
                each("P8", lambda h: m3[:, h, :], lambda h: m6[:, h, :], "D8T", "P4")
                turned("P8T", m6, "P8")
                each("Y1", lambda h: m1[:, h, :], lambda h: m6[:, h, :], "P8T")
                each("Pa", lambda h: m0[:, h, :], lambda h: m4[:, h, :], "Y1")
                turned("PaT", m6, "Pa")
                each("Y2", lambda h: m2[:, h, :], lambda h: m6[:, h, :], "PaT")
                each("Pb", lambda h: m5[:, h, :], lambda h: m3[:, h, :], "Y2")
                b = start(("LakV", s))
                for h in range(HEADS):
                    ins = mm(b[:, HD * h:HD * h + HD], MK[:, h, 0, :], tokV[:, h // 2, HD * (h % 2):HD * (h % 2) + HD],
                             start=True, stop=True)
                finish(ins)
                b = start(("WT", s))
                read(pe, ("Pb", s, 1))
                for h in range(HEADS):
                    e = h % 2
                    ins = mm(b[64 * e:64 * e + 64, P * (h // 2):P * (h // 2) + P],
                             tokA[:, h // 2, HD * e:HD * e + HD], m6[:, h, :], start=True, stop=True)
                finish(ins)
                b = start(("U", s))
                read(pe, ("LakV", s))
                for h in range(HEADS):
                    ins = mm(b[:, HD * h:HD * h + HD], m6[:, h, :], lakv[:, h // 2, HD * (h % 2):HD * (h % 2) + HD],
                             start=True, stop=True)
                finish(ins)
                read(pe, ("WT", s))
                pe.wait_ge(vz_ready, 2 * s + 2)
                for c_ in (2 * s, 2 * s + 1):
                    p_ = c_ % 2
                    S = state[:, c_ % 2, :, :]
                    b = start(("SA", c_))
                    if c_:
                        read(pe, ("DS", c_ - 1))
                    else:
                        pe.wait_ge(state_ready, 1)
                    for i in range(HP):
                        ins = mm(b[64 * p_:64 * p_ + 64, P * i:P * i + P], wt[:, i, 64 * p_:64 * p_ + 64], S[:, i, :],
                                 start=True, stop=True)
                    finish(ins)
                    if c_ < NCH - 1:
                        b = start(("DS", c_))
                        read(pe, ("SA", c_))
                        for i in range(HP):
                            mm(b[:, P * i:P * i + P], tokK[:, i, :], vz[:, p_, i, :], start=True, stop=False)
                            ins = mm(b[:, P * i:P * i + P], tokB[:, i, :], saz[:, p_, i, :], start=False, stop=True)
                        finish(ins)
                    b = start(("Y", c_))
                    read(pe, ("SA", c_))
                    ct = slice(64 * p_, 64 * p_ + 64)
                    for i in range(HP):
                        for e in range(2):
                            o = b[64 * e:64 * e + 64, CH * i:CH * i + CH]
                            mm(o, saz[:, p_, i, HD * e:HD * e + HD], MB[:, 2 * i + e, 1, ct], start=True, stop=False,
                               skip_group_check=True)
                            mm(o, vz[:, p_, i, HD * e:HD * e + HD], MK[:, 2 * i + e, 1, ct], start=False, stop=False,
                               skip_group_check=True)
                        ins = mm(b[:, CH * i:CH * i + CH], S[:, i, :], rT[:, i, CH * c_:CH * c_ + CH], start=False,
                                 stop=True, skip_group_check=True)
                    finish(ins)
            read(pe, ("Y", NCH - 1))
            for i in range(HP):
                b = start(("mean", i))
                finish(mm(b[:, :], block_mean[:, :], rT[:, i, :], start=True, stop=True))
            for i in range(HP):
                b = start(("var", i))
                pe.wait_ge(gn_sq, i + 1)
                finish(mm(b[:, :], block_mean[:, :], gn[:, i, :], start=True, stop=True))

            def token_tiles(names, order, left):
                banks = [start(n) for n in names]
                n = len(order)
                for k in range(0, n - 4, 2):
                    wh, wl = half_panel()
                    for t in range(2):
                        for r in range(NR):
                            ins = mm3(banks[r][:, :], left(order[k + t], r), (wh[:, t, :], wl[:, t, :]), k + t == 0, False)
                    ins.then_inc(half_used, 1)
                last = [half_panel(), half_panel()]
                for r in range(NR):
                    for m, (wh, wl) in enumerate(last):
                        for t in range(2):
                            k = n - 4 + 2 * m + t
                            ins = mm3(banks[r][:, :], left(order[k], r), (wh[:, t, :], wl[:, t, :]), k == 0, k == n - 1)
                    finish(ins)

            def norm_turns(l, j):
                for r in range(NR):
                    pe.wait_ge(normed, 4 * (2 * l + j) + r + 1)
                    for n in range(2):
                        b = start(("nT", l, j, r, n))
                        finish(transpose4(b, [xp[:, r, P * d:P * d + P] for d in range(4 * n, 4 * n + 4)]))
                pe.wait_ge(u_lo_ready, 8 * (2 * l + j + 1))

            for l in range(2):
                if l == 0:
                    def left(k, r):
                        m = (k + 4) % 8
                        if (r, m) in waits:
                            pe.wait_ge(mix_lo_ready, m + 1)
                            waits.discard((r, m))
                        return mix_hi[:, m, r:T:NR], mix_lo[:, m, r:T:NR]

                    waits = {(0, m) for m in range(8)}
                    for n in range(2):
                        token_tiles([("y", 0, 0, 0, n, r) for r in range(NR)], (4, 5, 6, 7, 0, 1, 2, 3), left)
                else:
                    def token_u(k, r):
                        return u_hi[:, k, P * r:P * r + P], u_lo[:, k, P * r:P * r + P]

                    for g in range(GROUPS):
                        for n in ("q", "k"):
                            for i in range(HP):
                                feature_tile((n, g, i), u_hi, u_lo)
                        token_tiles([("v", g, r) for r in range(NR)], range(8), token_u)
                    read(pe, ("q", 2, 3), ("k", 2, 3))
                    read(pe, ("v", 2, 3))
                    n = HEADS * NR
                    for i in range(n + 2):
                        if i < n:
                            h, r = i // NR, i % NR
                            e, hp = h % 2, h // 2
                            pe.wait_ge(q_padded, h + 1)
                            b = start(("S0", i))
                            finish(mm(b[:, :], qpad[:, e, 0, P * r:P * r + P], kT[:, 0, hp, :], start=True, stop=True))
                            b = start(("S1", i))
                            for g in (1, 2):
                                ins = mm(b[:, P * (g - 1):P * g], qpad[:, e, g, P * r:P * r + P],
                                         kT[:, g, hp, P * r:P * r + P], start=True, stop=True)
                            finish(ins)
                        if 1 <= i <= n:
                            k = i - 1
                            pe.wait_ge(exp_ready, k + 1)
                            b = start(("PT0", k))
                            finish(transpose4(b, [sS[:, k % 3, P * m:P * m + P] for m in range(4)]))
                            b = start(("PT1", k))
                            finish(transpose4(b, [sS[:, k % 3, P * m:P * m + P] for m in range(4, 6)]))
                        if i >= 2:
                            k = i - 2
                            h, r = k // NR, k % NR
                            b = start(("O", k))
                            read(pe, ("PT0", k), ("PT1", k))
                            for m in range(6):
                                vs = v_at[0][:, m, :] if m < 4 else v_at[m - 3][:, r, :]
                                ins = mm(b[:, 0:HD], pT[:, k % 2, m, :], vs[:, HD * h:HD * h + HD], start=(m == 0),
                                         stop=(m == 5))
                            finish(ins)
                    read(pe, ("O", n - 1))
                    for r in range(NR):
                        b = start(("oT", r))
                        finish(transpose4(b, [otok[:, r, P * i:P * i + P] for i in range(HP)]))
                    pe.wait_ge(o_lo_ready, NR)
                    for n in range(2):
                        token_tiles([("y", 1, 0, 0, n, r) for r in range(NR)], range(4),
                                    lambda k, r: (o_hi[:, k, P * r:P * r + P], o_lo[:, k, P * r:P * r + P]))
                norm_turns(l, 0)
                for a in range(2):
                    for f in range(FH * a, FH * a + FH):
                        feature_tile(("f", l, f), u_hi, u_lo)
                        if l == 0 and f in ADA_AFTER:
                            ada(1, ADA_AFTER[f])
                    waits = set(range(FH))

                    def hidden(k, r):
                        if k in waits:
                            pe.wait_ge(h_lo_ready, 2 * FH * l + FH * a + k + 1)
                            waits.discard(k)
                        return h_hi[:, k, P * r:P * r + P], h_lo[:, k, P * r:P * r + P]

                    for n in range(2):
                        token_tiles([("y", l, 1, a, n, r) for r in range(NR)], range(FH), hidden)
                if l == 0:
                    norm_turns(0, 1)
            assert at_job[0] == len(plan) and at_half[0] == len(halves)


_INS = ['x', 'c', 'ada_w', 'ada_b', 'ln_g', 'ln_b', 'ab_w_in', 'rw_mu', 'rw_w0', 'rw_w_up', 'rw_a0', 'rw_a_up', 'rw_g_up',
        'rw_k_k', 'rw_k_a', 'rw_r_k', 'rw_lnx_g', 'rw_lnx_b', 'sc_conv_w', 'ab_w_out', 'dil_w_qkv', 'dil_w_out',
        'rel_bias', 'mlp_w1', 'mlp_w2']


def shape_constants():
    i, j = np.arange(P)[:, None], np.arange(P)[None, :]

    def same(n):
        return i // n == j // n

    masks = np.stack([same(16) & (i < j), same(64) & (i <= j), same(64) & (i < j), same(64) & (i <= j),
                      same(16) & (i > j), same(32) & ~same(16) & (i > j), same(64) & ~same(32) & (i > j)], axis=1)
    n = np.arange(BW)
    steps = P - 1 - n
    buckets = np.zeros((33, BAND, BW), np.float32)
    for b in range(BAND):
        if b < 7:
            dist = 4 * steps + 3 - b
            valid = (dist >= 0) & (dist <= 128)
        elif b == 7:
            dist = 4 * steps
            valid = steps >= 0
        else:
            dist = 4 * steps
            valid = (steps >= 0) & (steps % 4 == 0)
        d = np.where(valid, dist, 0)
        exact = 16
        far = exact + (np.log(np.maximum(d, 1) / exact) / np.log(2048 / exact) * exact).astype(np.int64)
        bucket = np.where(d < exact, d, np.minimum(far, 31))
        buckets[bucket[valid], b, n[valid]] = 1.0
        buckets[32, b, ~valid] = NEG
    return np.eye(P, dtype=np.float32), masks.astype(np.float32), buckets.reshape(33, BAND * BW)


def kernel(**inputs):
    import concourse.bacc as bacc
    from concourse.bass_utils import run_bass_kernel_spmd

    nc = bacc.Bacc("TRN2", target_bir_lowering=False, num_devices=1)
    arrays, args = {}, []
    for name in _INS:
        arrays[f"in_{name}"] = np.ascontiguousarray(inputs[name])
    for name, value in zip(("identity", "masks", "buckets"), shape_constants()):
        arrays[f"in_{name}"] = value
    for name, value in arrays.items():
        args.append(nc.dram_tensor(name, value.shape, F32, kind="ExternalInput").ap())
    args.append(nc.dram_tensor("out", (1, T, D), F32, kind="ExternalOutput").ap())
    args.append(nc.dram_tensor("band", (HEADS, BAND * BW), F32).ap())
    args.append(nc.dram_tensor("skew", (HEADS, P, BAND * BW), F32).ap())
    trunk(nc, *args)
    r = run_bass_kernel_spmd(nc, [arrays], core_ids=[0])
    return r.results[0]["out"]
```

```python
import math
from contextlib import ExitStack

import numpy as np

import concourse.bass as bass
from concourse import mybir

P = 128
D = 1024
T = 512
KT = D // P
NR = T // P
F = 4 * D
RW = 512
HP = RW // P
HEADS = 8
HD = 64
CH = 64
NCH = T // CH
SC = T // P
WD_AD = 3 * RW
GD = WD_AD + P
GR = 160
AB = 3 * RW + P + GR + 3 * RW
PB = 3 * RW + P + GR
ALPHA = 4 ** 0.25
LN_EPS = 1e-5
GN_EPS = 64e-5
KAPPA = -math.exp(-0.5)
NEG = -1e30
GROUPS = 3
BAND = 9
BW = 256

F32 = mybir.dt.float32
F32R = mybir.dt.float32r
ALU = mybir.AluOpType
ACT = mybir.ActivationFunctionType
AX = mybir.AxisListType

PAR = {}
_row = 0
for _name, _n in (("c", 8), ("ln_g", 32), ("ln_b", 32), ("mu", 15), ("w0", 4), ("a0", 4), ("k_k", 4), ("k_a", 4),
                  ("r_k", 4), ("lnx_g", 4), ("lnx_b", 4), ("conv", 12)):
    PAR[_name] = _row
    _row += _n
SH1, SC1, G1, SH2, SC2, G2 = range(6)


BY_POOL = 2
FH = F // P // 2
ADA_COLS = (0, 1, 2, 3, 6, 7, 8, 9)
ADA_ROWS = (4, 5, 10, 11)
ADA_REST = (4, 5, 6, 7, 8, 9, 10, 11)


def ada_product(l, cg):
    return ("gate", l, int(cg > 5), cg % 2) if cg in ADA_ROWS else ("mod", l, cg)


SUPER = [("UB", 0), ("UB", 1), ("UB", 2), ("UB", 3), ("LL", 0), ("LL", 1), ("D2", 0), ("D2", 1), ("UK", 0), ("trB",),
         ("D2T", 0), ("D2T", 1), ("mean",), ("UK", 1), ("D4", 0), ("D4", 1), ("P2", 0), ("P2", 1), ("D4T", 0), ("D4T", 1),
         ("UK", 2), ("trK",), ("D8T", 0), ("D8T", 1), ("P4", 0), ("P4", 1), ("UK", 3), ("trV",), ("P8", 0), ("P8", 1),
         ("trA",), ("Y1", 0), ("Y1", 1), ("P8T", 0), ("P8T", 1), ("var",), ("LakV",), ("Pa", 0), ("Pa", 1), ("Y2", 0),
         ("Y2", 1), ("PaT", 0), ("PaT", 1), ("Pb", 0), ("Pb", 1), ("WT",), ("U",)]
SUPER_DVE = ("UB", "UK", "LL", "P2", "P4", "P8", "Pa", "Pb", "mean")
SUM_AFTER = {("UK", 0): 1, ("UK", 1): 1, ("UK", 2): 1, ("UK", 3): 1, ("P2", 1): 1, ("P4", 1): 1, ("P8", 1): 1, ("Pa", 1): 3}


CONV_BONUS = [("c", 0), ("c", 1), ("bonus", 0), ("bonus", 1), ("c", 2), ("bonus", 2), ("c", 3), ("bonus", 3)]


def super_products(s):
    for kind, *q in SUPER:
        if kind in ("mean", "var"):
            if s:
                yield kind, 0, (kind, s - 1)
        else:
            yield kind, (q or [0])[0], (kind, s, *q)


def build_plan():
    plan = [(("F", i), "act") for i in range(5)]
    plan += [(("par",), "dve")] + [(("mod", 0, cg), "dve") for cg in range(4)]
    plan += [(("x", d), "act" if d % 2 else "dve") for d in range(KT)]
    tiles = [("p", i) for i in range(15)]
    for t in tiles:
        plan += [(t, "dve")] + [(ada_product(0, cg), "act") for i, cg in ((5, 4), (9, 5), (13, 6)) if t[1] == i]
    plan += [((n, i), "act") for n in ("w", "a", "g") for i in range(HP)]
    plan += [(("h", 0), "act"), (("nrm",), "act"), (("h", 1), "act"), (("h", 2), "act")]
    plan += [(("nb", i), "dve") for i in range(HP)]
    plan += [(("h", 3), "act")] + [(("b", i), "act") for i in range(HP)]
    plan += [(name, "dve") for name in CONV_BONUS]
    for s in range(SC):
        plan += [(name, "dve" if kind in SUPER_DVE else "act") for kind, _, name in super_products(s)]
        for c in (2 * s, 2 * s + 1):
            plan += [(("SA", c), "dve")] + ([(("DS", c), "dve")] if c < NCH - 1 else []) + [(("Y", c), "act")]
        if s == SC - 1:
            plan += [(("mean", s), "dve")]
        plan += [(ada_product(0, cg), "act") for cg in SUMMED[s]]
    plan += [(("var", SC - 1), "act")]
    for l in range(2):
        if l:
            for g in range(GROUPS):
                plan += [(("q", g, i), "act") for i in range(HP)] + [(("k", g, i), "dve") for i in range(HP)]
                plan += [(("v", g, r), "act") for r in range(NR)]
            n = HEADS * NR
            for i in range(n + 3):
                if i < n:
                    plan += [(("S0", i), "dve"), (("S1", i), "dve")]
                if 2 <= i <= n + 1:
                    plan += [(("PT0", i - 2), "act"), (("PT1", i - 2), "dve")]
                if i >= 3:
                    plan += [(("O", i - 3), "dve")]
            plan += [(("oT", r), "act") for r in range(NR)]
        plan += [(("y", l, 0, 0, n, r), "dve") for n in range(2) for r in range(NR)]
        plan += [(("nT", l, 0, r, n), "act" if n else "dve") for r in range(NR) for n in range(2)]
        for a in range(2):
            for f in range(FH):
                plan += [(("f", l, FH * a + f), "act")]
                if l == 0 and (FH * a + f) in ADA_AFTER:
                    plan += [(ada_product(1, ADA_AFTER[FH * a + f]), "act")]
            plan += [(("y", l, 1, a, n, r), "dve") for n in range(2) for r in range(NR)]
        if l == 0:
            plan += [(("nT", l, 1, r, n), "act" if n else "dve") for r in range(NR) for n in range(2)]
    return plan


ADA_AFTER = {4: 0, 6: 1, 8: 2, 10: 3, 12: 4, 14: 5, 20: 6, 22: 7, 24: 8, 26: 9, 28: 10, 30: 11}
SUMMED = ((7,), (8,), (9,), (10, 11))


def panel_list():
    out = [("ada", 0, cg, k) for cg in range(4) for k in range(2)]
    ada = [("ada", 0, cg, k) for cg in ADA_REST for k in range(2)]
    for k in range(14):
        out += [("in", k)]
        if k < 6:
            out += [ada.pop(0)]
    out += ada
    out += [("wo", n, 1 - k) for n in range(2) for k in range(2)]
    for l in range(2):
        if l:
            for g in range(GROUPS):
                out += [("qkv", g, k) for k in range(4)] + [("wv", g, k) for k in range(2)]
            out += [("do", n) for n in range(2)]
        for a in range(2):
            later = [("ada", 1, cg, k) for cg in range(6 * a, 6 * a + 6) for k in range(2)] if l == 0 else []
            for k in range(8):
                out += [("w1", l, 8 * a + k)]
                for _ in range(2 if 1 <= k < 7 else 0):
                    if later:
                        out += [later.pop(0)]
            assert not later
            out += [("w2", l, a, n, k) for n in range(2) for k in range(4)]
    return out


def half_panels(panels, number):
    out = []
    for i, p in enumerate(panels):
        kind = p[0]
        if kind == "ada":
            continue
        if kind in ("in", "qkv", "w1"):
            for n in range(1 if p == ("in", 7) else 2):
                if kind == "in":
                    k = p[1]
                    name = ("p", 2 * k + n) if k < 8 else ("hbc"[(k - 8) // 2], 2 * (k % 2) + n)
                elif kind == "qkv":
                    name = ("q" if p[2] < 2 else "k", p[1], 2 * (p[2] % 2) + n)
                else:
                    name = ("f", p[1], 2 * p[2] + n)
                out.append((i, n, name, name))
            continue
        if kind == "wv":
            group, last = ("v", p[1]), p[2] == 1
        elif kind == "wo":
            group, last = ("y", 0, 0, 0, p[1]), p[2] == 0
        elif kind == "do":
            group, last = ("y", 1, 0, 0, p[1]), True
        else:
            group, last = ("y", p[1], 1, p[2], p[3]), p[4] == 3
        for n in range(2):
            out.append((i, n, group + (NR - 1,) if last else None, group + (0,)))
    return out


ARENA = 200
RING = 3
SPLIT = 3


def trunk(nc, x, c, ada_w, ada_b, ln_g, ln_b, ab_w_in, rw_mu, rw_w0, rw_w_up, rw_a0, rw_a_up, rw_g_up, rw_k_k,
          rw_k_a, rw_r_k, rw_lnx_g, rw_lnx_b, sc_conv_w, ab_w_out, dil_w_qkv, dil_w_out, rel_bias, mlp_w1, mlp_w2,
          identity, masks, heads_of, buckets, out, band_dram, skew_dram):
    plan = build_plan()
    number, freed_count, counts = {}, {}, {"act": 0, "dve": 0}
    for j, (name, reader) in enumerate(plan):
        counts[reader] += 1
        number[name] = j
        freed_count[name] = counts[reader]
    reader_of = dict(plan)
    panels = panel_list()
    halves = half_panels(panels, number)
    panel_no = {p: i for i, p in enumerate(panels)}

    with ExitStack() as ctx:
        def sb(name, shape):
            return ctx.enter_context(nc.sbuf_tensor(name, shape, F32))

        def sem(name):
            return ctx.enter_context(nc.semaphore(name))

        bank = [ctx.enter_context(nc.psum_tensor(f"bank{i}", [P, 512], F32)) for i in range(8)]

        ident = sb("ident", [P, P])
        block_ones = sb("block_ones", [P, P])
        block_mean = sb("block_mean", [P, P])
        ones_sq = sb("ones_sq", [P, P])[:, :]
        ones_col = ones_sq[:, 0:1]
        par = sb("par", [P, P])
        adab = sb("adab", [P, 96])
        cond = sb("cond", [P, 8])
        mod = sb("mod", [P, 2, 32])
        tiny = sb("tiny", [P, 216])
        mask = sb("mask", [P, 7, P])
        head_cols = sb("head_cols", [P, HP, HEADS])
        arena_at = (nc.sbuf_usable_end - ARENA * 1024) // 32 * 32
        assert arena_at >= nc.sbuf_base
        placed = [0]

        def rounded(name, kib, *shape):
            return nc.alloc_sbuf_tensor_at(name, [P, *shape], F32R, offset=arena_at + int(kib * 1024))

        assert masks.shape[1] == 7

        def at(kib, *shape):
            placed[0] += 1
            assert kib * 1024 + 4 * int(np.prod(shape)) <= ARENA * 1024
            t = nc.alloc_sbuf_tensor_at(f"part{placed[0]}", [P, *shape], F32, offset=arena_at + int(kib * 1024))
            return t[(slice(None),) * (1 + len(shape))]

        ring = [at(8 * i, 2048) for i in range(RING)]
        w_hi = [rounded(f"w_hi{i}", 24 + 8 * i, 1024) for i in range(SPLIT)]
        w_lo = [rounded(f"w_lo{i}", 28 + 8 * i, 1024) for i in range(SPLIT)]
        X0 = 56
        gate = [at(48, D), at(52, D), at(X0 + 120, D)]
        acc = [[gate[1][:, 0:512], gate[1][:, 512:1024]], [gate[2][:, 0:512], gate[2][:, 512:1024]]]
        rT, kT_, aT, bT = (at(X0 + 8 * i, HP, T) for i in range(4))
        vT, bonus, gt, ybT = (at(X0 + 32 + 8 * i, HP, T) for i in range(4))
        head_rows = at(X0 + 46, HP, P)[0:HEADS]
        W0 = X0 + 64
        t8, t9, t10, t11 = (at(W0 + 8 * i, HP, T) for i in range(4))
        xin = at(W0, NR, D)
        ut_val = at(W0 + 16, KT, T)
        u0_hi, u0_lo = rounded("u0_hi", W0 + 32, KT, T), rounded("u0_lo", W0 + 48, KT, T)
        lr = at(W0 + 64, 4, RW)
        low = at(W0 + 72, 3, T)
        rawpar = at(X0, 3, P)
        wconst = at(X0 + 4, BAND * BW)
        bandv = at(X0 + 16, BAND * BW)
        relb = at(X0 + 2, GROUPS * HEADS)
        MB = at(W0, HEADS, 2, P)
        MK = at(W0 + 8, HEADS, 2, P)
        m0, m1, m2, m3, m4, m5, m6 = (at(W0 + 16 + 4 * i, HEADS, P) for i in range(7))
        arz = at(W0 + 44, HP, 2, 2, P)
        tokK, tokB, tokA, tokV = (at(W0 + 52 + 2 * i, HP, P) for i in range(4))
        vz = at(W0 + 60, 2, HP, P)
        saz = at(W0 + 64, 2, HP, P)
        lakv, uu, wt = (at(W0 + 68 + 2 * i, HP, P) for i in range(3))
        state = at(W0 + 74, 2, HP, P)
        gn = at(W0 + 78, HP, P)
        norms = at(W0 + 78, T)[0:HEADS]
        xp = at(X0 + 64, NR, D)
        mix_hi, mix_lo = rounded("mix_hi", X0 + 80, 8, T), rounded("mix_lo", X0 + 96, 8, T)
        u_hi, u_lo = rounded("u_hi", X0 + 80, KT, T), rounded("u_lo", X0 + 96, KT, T)
        grow, brow = at(X0 + 112, D), at(X0 + 116, D)
        h_hi, h_lo = rounded("h_hi", X0, FH, T), rounded("h_lo", X0 + 32, FH, T)
        h_val = at(X0 + 124, 4, T)
        u_val = [at(X0 + 132, 2, T), at(X0 + 140, 2, T)]
        ytmp = at(X0 + 136, 2, T)
        qT = at(X0, GROUPS, HP, T)
        kT = at(X0 + 24, GROUPS, HP, T)
        v_at = [at(X0 + 48, NR, RW), at(X0 + 56, NR, RW), at(X0 + 124, NR, RW)]
        otok = at(X0 + 112, NR, RW)
        o_hi, o_lo = rounded("o_hi", X0, HP, T), rounded("o_lo", X0 + 8, HP, T)
        oT = at(X0 + 16, HP, T)
        qpad = at(X0 + 80, 2, GROUPS, T)
        tab = [at(X0 + 92 + 4.5 * i, BAND * P) for i in range(2)]
        sS = [at(X0 + 101 + 3 * i, 6 * P) for i in range(3)] + [at(X0 + 140, 6 * P)]
        pT = at(X0 + 132, 2, 6, P)
        assert X0 + 144 <= ARENA

        eps_ln, eps_gn = tiny[:, 0:1], tiny[:, 1:2]
        omm = tiny[:, 2:17]
        omka = tiny[:, 17:21]
        csum_end = tiny[:, 24:56]
        rho = tiny[:, 56:84]
        stats = tiny[:, 96:96 + 4 * 12]
        mv = tiny[:, 144:152]
        rstd = tiny[:, 152:156]
        nmr = tiny[:, 156:160]
        scl = tiny[:, 160:168]
        shf = tiny[:, 168:176]
        nmax = tiny[:, 176:180]
        den = tiny[:, 180:184]
        sg_c = tiny[:, 184:192]
        mx = tiny[:, 192:196]
        rden = tiny[:, 208:212]

        mm_done = sem("mm_done")
        freed = {"act": sem("read_by_act"), "dve": sem("read_by_dve")}
        slot_landed = [sem(f"slot_landed{i}") for i in range(RING)]
        raw_used = sem("raw_used")
        hi_ready, lo_ready = sem("hi_ready"), sem("lo_ready")
        half_used = sem("half_used")
        acc_ready = sem("acc_ready")
        u_hi_ready, u_lo_ready = sem("u_hi_ready"), sem("u_lo_ready")
        h_value, h_hi_ready, h_lo_ready = sem("h_value"), sem("h_hi_ready"), sem("h_lo_ready")
        o_hi_ready, o_lo_ready = sem("o_hi_ready"), sem("o_lo_ready")
        act_step, dve_step, pool_step = sem("act_step"), sem("dve_step"), sem("pool_step")
        ident_in = sem("ident_in")
        consts_in, params_in, x_in, band_in = sem("consts_in"), sem("params_in"), sem("x_in"), sem("band_in")
        lowrank_in, xp_in, rows_in, tab_in = sem("lowrank_in"), sem("xp_in"), sem("rows_in"), [sem("tab_in0"), sem("tab_in1")]
        band_out, skewed = sem("band_out"), sem("skewed")
        raw_zero, cond_ready, block_ready = sem("raw_zero"), sem("cond_ready"), sem("block_ready")
        sig_c, mod_ready = sem("sig_c"), sem("mod_ready")
        low_ready, sq_ready, cs_ready = sem("low_ready"), sem("sq_ready"), sem("cs_ready")
        exps_ready, rk_ready, prods_ready = sem("exps_ready"), sem("rk_ready"), sem("prods_ready")
        arz_ready, vz_ready, p_ready = sem("arz_ready"), sem("vz_ready"), sem("p_ready")
        gn_sq, gn_in, ya_ready = sem("gn_sq"), sem("gn_in"), sem("ya_ready")
        kkr_ready, affine_ready, kh_ready, kki_ready, kr_ready = (sem("kkr_ready"), sem("affine_ready"), sem("kh_ready"),
                                                                  sem("kki_ready"), sem("kr_ready"))
        kk_ready, pads_zero = sem("kk_ready"), sem("pads_zero")
        q_first, q_first_zero = sem("q_first"), sem("q_first_zero")
        d_ready, gn_root = sem("d_ready"), sem("gn_root")
        norm_ready, rp_ready, arz_zero, conv_done = sem("norm_ready"), sem("rp_ready"), sem("arz_zero"), sem("conv_done")
        var_ready, root_ready, scale_ready, normed, resid_ready = (sem("var_ready"), sem("root_ready"), sem("scale_ready"),
                                                                    sem("normed"), sem("resid_ready"))
        x_split_hi, x_split_lo = sem("x_split_hi"), sem("x_split_lo")
        mix_hi_ready, yb_lo_ready, ya_lo_ready = sem("mix_hi_ready"), sem("yb_lo_ready"), sem("ya_lo_ready")
        q_padded, max_ready, exp_ready = sem("q_padded"), sem("max_ready"), sem("exp_ready")
        rden_ready = sem("rden_ready")
        out_stored, out_ready = sem("out_stored"), sem("out_ready")

        def wait_product(eng, name):
            eng.wait_ge(mm_done, number[name] + 1)
            return bank[number[name] % 8]

        def read(eng, *names):
            need = {}
            for n in names:
                need[reader_of[n]] = max(need.get(reader_of[n], 0), freed_count[n])
            for e, v in need.items():
                eng.wait_ge(freed[e], v)

        def panel_ap(p):
            kind = p[0]
            if kind == "ada":
                l, cg, k = p[1:]
                src = ada_w[l][512 * k:512 * k + 512, 512 * cg:512 * cg + 512]
            elif kind == "in":
                k = p[1]
                lo = 256 * k if k < 8 else PB + 256 * (k - 8)
                src = ab_w_in[0][:, lo:lo + (P if k == 7 else 256)]
            elif kind == "qkv":
                g, k = p[1:]
                src = dil_w_qkv[0][:, g * 1536 + 256 * k:g * 1536 + 256 * k + 256]
            elif kind == "w1":
                l, k = p[1:]
                src = mlp_w1[l][:, 256 * k:256 * k + 256]
            elif kind == "wo":
                n, k = p[1:]
                src = ab_w_out[0][512 * k:512 * k + 512, n * 512:n * 512 + 512]
            elif kind == "wv":
                g, k = p[1:]
                src = dil_w_qkv[0][512 * k:512 * k + 512, g * 1536 + 1024:g * 1536 + 1536]
            elif kind == "do":
                src = dil_w_out[0][:, p[1] * 512:p[1] * 512 + 512]
            else:
                l, a, n, k = p[1:]
                row = 512 * (4 * a + k)
                src = mlp_w2[l][row:row + 512, n * 512:n * 512 + 512]
            return src.rearrange("(t p) n -> p t n", p=P)

        def panel_tile(i):
            src = panel_ap(panels[i])
            t, n = src.shape[1], src.shape[2]
            return ring[i % RING][:, 0:t * n].rearrange("p (t n) -> p t n", t=t), src

        def half_of(h):
            i, n = halves[h][0:2]
            w = panel_tile(i)[0]
            if w.shape[1] == KT:
                return w[:, :, P * n:P * n + P]
            return w[:, 2 * n:2 * n + 2, :]

        def part(t, h):
            n = KT if half_of(h).shape[1] == KT else 2
            return t[h % SPLIT][:, :].rearrange("p (t n) -> p t n", t=n)

        def wait_landed(eng, i):
            eng.wait_ge(slot_landed[i % RING], 16 * (i // RING + 1))

        def wait_half_free(eng, h):
            if h >= SPLIT:
                end = halves[h - SPLIT][2]
                if end:
                    eng.wait_ge(mm_done, number[end] + 1)
                else:
                    eng.wait_ge(half_used, sum(not x[2] for x in halves[:h - SPLIT + 1]))

        def due(h):
            if h < SPLIT:
                return number[("p", 0) if h else ("x", 0)]
            end, first = halves[h - SPLIT][2:]
            if halves[h][0] > panel_no["ada", 0, ADA_REST[-1], 1]:
                return max(number[end or first], number[ada_product(0, SUMMED[-1][0])])
            return number[end or first]

        parameter_rows = [("c", 8, c[0].rearrange("(r j) -> r j", j=P)),
                          ("ln_g", 32, ln_g.rearrange("a b (r j) -> (a b r) j", j=P)),
                          ("ln_b", 32, ln_b.rearrange("a b (r j) -> (a b r) j", j=P)),
                          ("mu", 14, rw_mu[0, 0:14 * P].rearrange("(r j) -> r j", j=P)),
                          ("w0", 4, rw_w0[0].rearrange("(r j) -> r j", j=P)),
                          ("a0", 4, rw_a0[0].rearrange("(r j) -> r j", j=P)),
                          ("k_k", 4, rw_k_k[0].rearrange("(r j) -> r j", j=P)),
                          ("k_a", 4, rw_k_a[0].rearrange("(r j) -> r j", j=P)),
                          ("lnx_g", 4, rw_lnx_g[0].rearrange("(r j) -> r j", j=P)),
                          ("lnx_b", 4, rw_lnx_b[0].rearrange("(r j) -> r j", j=P)),
                          ("r_k", 4, rw_r_k[0].rearrange("(r e) j -> r (e j)", e=2)),
                          ("conv", 12, sc_conv_w[0].rearrange("k (r j) -> (k r) j", j=P))]

        def load_rows(eng, part_no):
            eng.wait_ge(raw_zero, 1)
            for name, n, src in parameter_rows[part_no::2]:
                eng.dma_start(rawpar[PAR[name]:PAR[name] + n, 0, :], src).then_inc(params_in, 16)
            if part_no:
                eng.dma_start(rawpar[PAR["mu"] + 14:PAR["mu"] + 15, 0, 0:32], rw_mu[:, 14 * P:PB]).then_inc(params_in, 16)
            else:
                eng.dma_start(rawpar[0:96, 1, :], ada_b.rearrange("l (r j) -> (l r) j", j=P)).then_inc(params_in, 16)

        block = ctx.enter_context(nc.Block())

        @block.sync
        def _(sp):
            sp.dma_start(wconst[0:33, :], buckets).then_inc(band_in, 16)
            sp.dma_start(relb[0:32, :], rel_bias).then_inc(band_in, 16)
            sp.dma_start(ident[:, :], identity).then_inc(ident_in, 16)
            for i in range(len(panels)):
                if i == RING:
                    xr = x[0].rearrange("(l r) d -> r l d", r=NR)
                    for r in range(NR):
                        sp.dma_start(xin[:, r, :], xr[r]).then_inc(x_in, 16)
                if i == 12:
                    sp.dma_start(mask[:, :, :], masks).then_inc(consts_in, 16)
                    sp.dma_start(head_cols[:, :, :], heads_of[:, 0:HP * HEADS].rearrange("p (i h) -> p i h", i=HP))\
                        .then_inc(consts_in, 16)
                    sp.dma_start(head_rows, heads_of[0:HEADS, HP * HEADS:].rearrange("p (i c) -> p i c", i=HP))\
                        .then_inc(consts_in, 16)
                    sp.dma_start(lr[0:64, 0, :], rw_w_up[0]).then_inc(lowrank_in, 16)
                    sp.dma_start(lr[64:128, 1, :], rw_a_up[0]).then_inc(lowrank_in, 16)
                    sp.dma_start(lr[:, 2, :], rw_g_up[0, 0:P]).then_inc(lowrank_in, 16)
                    sp.dma_start(lr[0:32, 3, :], rw_g_up[0, P:GR]).then_inc(lowrank_in, 16)
                dst, src = panel_tile(i)
                if i >= RING:
                    sp.wait_ge(raw_used, i - RING + 1)
                sp.dma_start(dst, src).then_inc(slot_landed[i % RING], 16)
                if i == 0:
                    load_rows(sp, 1)
            outr = out[0].rearrange("(l r) d -> r l d", r=NR)
            for r in range(NR):
                if r < BY_POOL:
                    sp.wait_ge(resid_ready, 4 * 3 + r + 1)
                else:
                    sp.wait_ge(out_ready, r - BY_POOL + 1)
                sp.dma_start(outr[r], xp[:, r, :]).then_inc(out_stored, 16)
            sp.wait_ge(out_stored, 16 * NR)

        @block.gpsimd
        def _(pool):
            steps = [0]

            def step(ins):
                steps[0] += 1
                ins.then_inc(pool_step, 1)
                pool.wait_ge(pool_step, steps[0])

            g = nc.gpsimd
            g.memset(rawpar[:, :, :], 0.0).then_inc(raw_zero, 1)
            pool.wait_ge(raw_zero, 1)
            g.memset(relb[32:33, :], 1.0).then_inc(raw_zero, 1)
            pool.wait_ge(raw_zero, 2)
            step(g.memset(eps_ln, LN_EPS))
            step(g.memset(eps_gn, GN_EPS))
            step(g.memset(ones_sq, 1.0))
            for t, value in ((block_ones, 1.0), (block_mean, 1.0 / HD)):
                step(g.memset(t[:, :], 0.0))
                step(g.memset(t[0:64, 0:64], value))
                step(g.memset(t[64:128, 64:128], value))
            step(g.memset(lr[64:128, 0, :], 0.0))
            g.memset(lr[0:64, 1, :], 0.0).then_inc(block_ready, 1)
            pool.wait_ge(block_ready, 1)
            read(pool, ("F", 4))
            g.dma_start(band_dram, bandv[0:HEADS, :]).then_inc(band_out, 16)

            pool.wait_ge(affine_ready, HP)
            pool.wait_ge(kkr_ready, HP)
            g.tensor_tensor(kT_, kT_, t10, ALU.mult).then_inc(kh_ready, 1)
            pool.wait_ge(kh_ready, 1)
            pool.wait_ge(kk_ready, 1)
            g.tensor_tensor(bT, bT, t8, ALU.mult).then_inc(kki_ready, 1)
            pool.wait_ge(kki_ready, 1)
            pool.wait_ge(exps_ready, 4)
            pool.wait_ge(rk_ready, 1)
            g.tensor_tensor(rT, rT, t10, ALU.mult).then_inc(rp_ready, 1)
            pool.wait_ge(rp_ready, 1)
            g.tensor_tensor(kT_, kT_, t11, ALU.mult).then_inc(kr_ready, 1)
            pool.wait_ge(kr_ready, 1)
            pool.wait_ge(mm_done, number[("c", HP - 1)] + 1)
            g.memset(arz[:, :, :, :, :], 0.0).then_inc(arz_zero, 1)
            pool.wait_ge(arz_zero, 1)
            step(g.memset(vz[:, :, :, :], 0.0))
            step(g.memset(saz[:, :, :, :], 0.0))
            g.memset(state[:, :, :, :], 0.0).then_inc(pads_zero, 1)
            pool.wait_ge(pads_zero, 1)
            pool.wait_ge(prods_ready, 1)
            for s in range(SC):
                if s:
                    pool.wait_ge(mm_done, number[("LL", s - 1, 1)] + 1)
                    pool.wait_ge(arz_ready, 2 * s)
                for e in range(2 if s else 0):
                    h = slice(64 * e, 64 * e + 64)
                    step(g.tensor_copy(arz[h, :, e, 0, :], aT[h, :, P * s:P * s + P]))
                    g.tensor_copy(arz[h, :, e, 1, :], rT[h, :, P * s:P * s + P]).then_inc(arz_ready, 1)
                    pool.wait_ge(arz_ready, 2 * s + e + 1)
                if s == 0:
                    for h in range(HEADS):
                        src = bass.AP(tensor=band_dram.tensor, offset=band_dram.offset + h * BAND * BW,
                                      ap=[[0, P], [1, BAND * BW]])
                        g.dma_start(skew_dram[h], src).then_inc(skewed, 16)
                read(pool, ("trV", s))
                if s:
                    pool.wait_ge(mm_done, number[("Y", 2 * s - 1)] + 1)
                for e in range(2):
                    h = slice(64 * e, 64 * e + 64)
                    g.tensor_copy(vz[h, e, :, :], tokV[h, :, :]).then_inc(vz_ready, 1)
                    pool.wait_ge(vz_ready, 2 * s + e + 1)
            pool.wait_ge(mix_hi_ready, HP)
            g.tensor_tensor(mix_lo[:, 0:HP, :], ybT, mix_hi[:, 0:HP, :].bitcast(F32), ALU.subtract).then_inc(yb_lo_ready, 1)
            pool.wait_ge(yb_lo_ready, 1)
            pool.wait_ge(mm_done, number[("Y", NCH - 1)] + 1)
            xr = x[0].rearrange("(l r) d -> r l d", r=NR)
            g.dma_start(xp, xr.rearrange("r l d -> l r d")).then_inc(xp_in, 16)

            for l in range(2):
                if l:
                    pool.wait_ge(mm_done, number[("v", GROUPS - 1, NR - 1)] + 1)
                    for h in range(HEADS):
                        e, hp = h % 2, h // 2
                        rows_ = slice(64 * e, 64 * e + 64)
                        if h >= 2:
                            pool.wait_ge(mm_done, number[("S1", (h - 1) * NR - 1)] + 1)
                            read(pool, ("S1", (h - 1) * NR - 1))
                        elif h == 0:
                            pool.wait_ge(skewed, 16 * HEADS)
                            read(pool, ("q", 2, 3))
                        src = bass.AP(tensor=skew_dram.tensor, offset=skew_dram.offset + h * P * BAND * BW + P - 1,
                                      ap=[[BAND * BW - 1, P], [BW, BAND], [1, P]])
                        g.dma_start(tab[e].rearrange("p (b k) -> p b k", b=BAND), src).then_inc(tab_in[e], 16)
                        if h == 0:
                            continue
                        if h == 1:
                            step(g.memset(qpad[0:64, 1, :, :], 0.0))
                        g.tensor_copy(qpad[rows_, e, :, :], qT[rows_, :, hp, :]).then_inc(q_padded, 1)
                        pool.wait_ge(q_padded, h)
                for j in range(2):
                    if l and not j:
                        pool.wait_ge(mm_done, number[("oT", NR - 1)] + 1)
                    for dst, v in ((grow, ln_g), (brow, ln_b)):
                        src = bass.AP(tensor=v.tensor, offset=v.offset + (2 * l + j) * D, ap=[[0, P], [1, D]])
                        g.dma_start(dst, src).then_inc(rows_in, 16)
                    pool.wait_ge(rows_in, 32 * (2 * l + j + 1))
                    for r in range(BY_POOL if l and j else NR):
                        if l and j:
                            pool.wait_ge(normed, 4 * (2 * l + j) + r + 1)
                        else:
                            pool.wait_ge(mm_done, number[("nT", l, j, r, 1)] + 1)
                        step(g.tensor_tensor(xp[:, r, :], xp[:, r, :], grow, ALU.mult))
                        g.tensor_tensor(xp[:, r, :], xp[:, r, :], brow, ALU.add).then_inc(resid_ready, 1)
                        pool.wait_ge(resid_ready, 4 * (2 * l + j) + r + 1)

        @block.scalar
        def _(act):
            steps = [0]
            a = nc.scalar

            def step(ins):
                steps[0] += 1
                ins.then_inc(act_step, 1)
                act.wait_ge(act_step, steps[0])

            def done(ins):
                ins.then_inc(freed["act"], 1)

            at_half = [0]

            def keep_up(name, most=99):
                while at_half[0] < len(halves) and due(at_half[0]) <= number[name] and most:
                    most -= 1
                    h = at_half[0]
                    at_half[0] += 1
                    wait_landed(act, halves[h][0])
                    wait_half_free(act, h)
                    a.copy(part(w_hi, h), half_of(h)).then_inc(hi_ready, 1)

            def product_ready(eng, name):
                keep_up(name)
                return wait_product(eng, name)

            load_rows(act, 0)
            for i in range(5):
                b = product_ready(act, ("F", i))
                w = min(512, BAND * BW - 512 * i)
                if i == 3:
                    a.copy(bandv[0:HEADS, 1536:1792], b[0:HEADS, 0:256])
                    ins = a.copy(bandv[0:HEADS, 1792:2048], b[0:HEADS, 256:512])
                else:
                    ins = a.copy(bandv[0:HEADS, 512 * i:512 * i + w], b[0:HEADS, 0:w])
                done(ins)
            read(act, ("par",))
            a.activation(sg_c, par[:, 0:8], ACT.Sigmoid).then_inc(sig_c, 1)

            for d in range(1, KT, 2):
                b = product_ready(act, ("x", d))
                act.wait_ge(mod_ready, 1)
                done(a.activation(ut_val[:, d, :].rearrange("p (l r) -> p r l", r=NR),
                                  b[:, :].rearrange("p (r l) -> p r l", r=NR), ACT.Identity,
                                  scale=mod[:, 0, 8 + d:9 + d], bias=mod[:, 0, d:d + 1]))
                for e in (d - 1, d):
                    read(act, ("x", e))
                    a.copy(u0_hi[:, e, :], ut_val[:, e, :]).then_inc(x_split_hi, 1)
            def ada_out(l, cg):
                name = ada_product(l, cg)
                b = product_ready(act, name)
                if name[0] == "mod":
                    k = ADA_COLS.index(cg)
                    done(a.copy(mod[:, l, 4 * k:4 * k + 4], b[:, 0:4]))
                else:
                    g, n = name[2:]
                    done(a.activation(gate[(0, 1, 0, 2)[2 * l + g]][:, 512 * n:512 * n + 512], b[:, :], ACT.Identity,
                                      bias=1.0))

            for cg in (4, 5):
                ada_out(0, cg)
            product_ready(act, ("p", 12))
            read(act, ("p", 12))
            a.activation(low[0:64, 0, :], low[0:64, 0, :], ACT.Tanh).then_inc(low_ready, 1)
            product_ready(act, ("p", 13))
            read(act, ("p", 13))
            a.activation(low[:, 1, :], low[:, 1, :], ACT.Sigmoid)
            ada_out(0, 6)
            product_ready(act, ("p", 14))
            read(act, ("p", 14))
            a.activation(low[0:32, 2, :], low[0:32, 2, :], ACT.Sigmoid).then_inc(low_ready, 1)
            act.wait_ge(band_out, 16)
            for i in range(HP):
                b = product_ready(act, ("w", i))
                done(a.activation(aT[:, i, :], b[:, :], ACT.Sigmoid, bias=par[:, PAR["w0"] + i:PAR["w0"] + i + 1]))
            for i in range(HP):
                b = product_ready(act, ("a", i))
                done(a.activation(bT[:, i, :], b[:, :], ACT.Sigmoid, bias=par[:, PAR["a0"] + i:PAR["a0"] + i + 1]))
            read(act, ("a", 3))
            for i in range(HP):
                a.activation(t10[:, i, :], bT[:, i, :], ACT.Identity, scale=par[:, PAR["k_a"] + i:PAR["k_a"] + i + 1],
                             bias=omka[:, i:i + 1]).then_inc(affine_ready, 1)
            for i in range(HP):
                b = product_ready(act, ("g", i))
                done(a.copy(gt[:, i, :], b[:, :]))
            for i in range(HP):
                a.activation(t8[:, i, :], kT_[:, i, :], ACT.Identity,
                             scale=par[:, PAR["k_k"] + i:PAR["k_k"] + i + 1]).then_inc(kkr_ready, 1)
            act.wait_ge(kkr_ready, HP)
            a.activation(t9, t8, ACT.Square).then_inc(sq_ready, 1)
            for i in range(HP):
                b = product_ready(act, ("h", i))
                done(a.copy(bonus[:, i, :], b[:, :]))
                if i == 0:
                    b = product_ready(act, ("nrm",))
                    done(a.activation(norms, b[0:HEADS, :], ACT.Sqrt))
            for i in range(HP):
                b = product_ready(act, ("b", i))
                done(a.copy(ybT[:, i, :], b[:, :]))
                if i != 1:
                    continue
                act.wait_ge(cs_ready, 1)
                a.activation(t11, t10, ACT.Exp, scale=-KAPPA).then_inc(exps_ready, 1)
                a.activation(t10, t10, ACT.Exp, scale=KAPPA).then_inc(exps_ready, 1)
                a.activation(aT, aT, ACT.Exp, scale=KAPPA).then_inc(exps_ready, 1)
                a.activation(rho, rho, ACT.Exp, scale=KAPPA / 2).then_inc(exps_ready, 1)

            def group_norm_square(s):
                act.wait_ge(gn_in, s + 1)
                a.activation(gn, rT[:, :, P * s:P * s + P], ACT.Square).then_inc(gn_sq, 1)

            def group_norm_var(s):
                b = product_ready(act, ("var", s))
                done(a.activation(gn, b[:, :].rearrange("p (h t) -> p h t", h=HP), ACT.Sqrt, bias=eps_gn))

            where = {"D2": m3, "D2T": m0, "D4": m4, "D4T": m5, "D8T": m3, "P8T": m0, "Y1": m4, "PaT": m5, "Y2": m3,
                     "trK": tokK, "trB": tokB, "trA": tokA, "trV": tokV, "LakV": lakv, "WT": wt, "U": uu}
            keep_up(("bonus", HP - 1))
            act.wait_ge(arz_zero, 1)
            act.wait_ge(rp_ready, 1)
            act.wait_ge(prods_ready, 1)
            for e in range(2):
                h = slice(64 * e, 64 * e + 64)
                a.copy(arz[h, :, e, 0, :], aT[h, :, 0:P])
                a.copy(arz[h, :, e, 1, :], rT[h, :, 0:P]).then_inc(arz_ready, 1)
            act.wait_ge(conv_done, 1)
            for s in range(SC):
                for kind, q, name in super_products(s):
                    if kind in SUPER_DVE:
                        continue
                    if kind == "var":
                        group_norm_var(s - 1)
                        continue
                    b = product_ready(act, name)
                    dst = where[kind]
                    if len(name) == 3:
                        dst = dst[:, 4 * q:4 * q + 4, :]
                    done(a.copy(dst, b[:, :].rearrange("p (m k) -> p m k", m=4)))
                    if kind == "D2T" and q == 1 and s:
                        group_norm_square(s - 1)
                if s == SC - 1:
                    for i in range(HP):
                        a.copy(mix_hi[:, i, :], ybT[:, i, :]).then_inc(mix_hi_ready, 1)
                for c_ in (2 * s, 2 * s + 1):
                    b = product_ready(act, ("Y", c_))
                    done(a.copy(rT[:, :, CH * c_:CH * c_ + CH], b[:, 0:256].rearrange("p (h t) -> p h t", h=HP)))
                if s == SC - 1:
                    group_norm_square(s)
                for cg in SUMMED[s]:
                    ada_out(0, cg)
            group_norm_var(SC - 1)
            for i in range(HP):
                act.wait_ge(ya_ready, SC)
                a.copy(mix_hi[:, 4 + i, :], rT[:, i, :]).then_inc(mix_hi_ready, 1)

            def norm(l, j):
                last = l == 1 and j == 1
                product_ready(act, ("y", l, j, j, 1, 0))
                for r in range(NR):
                    n = 4 * (2 * l + j) + r
                    act.wait_ge(var_ready, n + 1)
                    a.activation(rstd[:, r:r + 1], mv[:, 2 * r + 1:2 * r + 2], ACT.Sqrt, bias=eps_ln).then_inc(root_ready, 1)
                    if last and r >= BY_POOL:
                        continue
                    act.wait_ge(scale_ready, n + 1)
                    a.activation(xp[:, r, :], xp[:, r, :], ACT.Identity, scale=rstd[:, r:r + 1],
                                 bias=nmr[:, r:r + 1]).then_inc(normed, 1)
                if last:
                    return
                for r in range(NR):
                    k = 8 * (2 * l + j) + 2 * r
                    b = wait_product(act, ("nT", l, j, r, 1))
                    if k >= 4:
                        act.wait_ge(u_lo_ready, k - 2)
                    for d in range(4, 8):
                        ins = a.activation(u_val[r % 2][:, 1, P * (d - 4):P * (d - 3)], b[:, P * (d - 4):P * (d - 3)],
                                           ACT.Identity, scale=scl[:, d:d + 1], bias=shf[:, d:d + 1])
                    done(ins)
                    for n in range(2):
                        read(act, ("nT", l, j, r, n))
                        a.copy(u_hi[:, 4 * n:4 * n + 4, P * r:P * r + P],
                               u_val[r % 2][:, n, :].rearrange("p (d l) -> p d l", d=4)).then_inc(u_hi_ready, 1)
                    if r in (1, 2):
                        keep_up(("nT", l, j, 0, 0), 1)

            def hidden_hi(k):
                act.wait_ge(h_value, k + 1)
                a.copy(h_hi[:, k % FH, :], h_val[:, k % 4, :]).then_inc(h_hi_ready, 1)

            def mlp(l):
                for a_ in range(2):
                    for f in range(FH * a_, FH * a_ + FH):
                        k = 2 * FH * l + f
                        b = product_ready(act, ("f", l, f))
                        if k >= 4:
                            act.wait_ge(h_lo_ready, k - 3)
                        done(a.activation(h_val[:, k % 4, :], b[:, :], ACT.Relu))
                        if f % FH:
                            hidden_hi(k - 1)
                        if l == 0 and f in ADA_AFTER:
                            ada_out(1, ADA_AFTER[f])
                    hidden_hi(k)
                    for n in range(2):
                        product_ready(act, ("y", l, 1, a_, n, 0))

            for l in range(2):
                if l:
                    for g in range(GROUPS):
                        for i in range(HP):
                            b = product_ready(act, ("q", g, i))
                            done(a.mul(qT[:, g, i, :], b[:, :], HD ** -0.5))
                        product_ready(act, ("k", g, 0))
                        for i in range(HP):
                            product_ready(act, ("k", g, i))
                        for r in range(NR):
                            b = product_ready(act, ("v", g, r))
                            done(a.copy(v_at[g][:, r, :], b[:, :]))
                    a.copy(qpad[0:64, 0, :, :], qT[0:64, :, 0, :]).then_inc(q_first, 1)
                    n = HEADS * NR
                    for i in range(n + 3):
                        if 2 <= i <= n + 1:
                            b = product_ready(act, ("PT0", i - 2))
                            done(a.copy(pT[:, (i - 2) % 2, 0:4, :], b[:, :].rearrange("p (m k) -> p m k", m=4)))
                        if i < n:
                            act.wait_ge(max_ready, i + 1)
                            a.activation(sS[i % 4][:, :], sS[i % 4][:, :], ACT.Exp, bias=nmax[:, i % 4:i % 4 + 1],
                                         accum_out=den[:, i % 4:i % 4 + 1]).then_inc(exp_ready, 1)
                    for r in range(NR):
                        b = product_ready(act, ("oT", r))
                        done(a.copy(oT[:, :, P * r:P * r + P], b[:, :].rearrange("p (h t) -> p h t", h=HP)))
                        read(act, ("oT", r))
                        a.copy(o_hi[:, :, P * r:P * r + P], oT[:, :, P * r:P * r + P]).then_inc(o_hi_ready, 1)
                product_ready(act, ("y", l, 0, 0, 0, 0))
                norm(l, 0)
                mlp(l)
                norm(l, 1)

        @block.vector
        def _(dve):
            steps = [0]
            v = nc.vector

            def step(ins):
                steps[0] += 1
                ins.then_inc(dve_step, 1)
                dve.wait_ge(dve_step, steps[0])

            def done(ins):
                ins.then_inc(freed["dve"], 1)

            at_half, at_panel = [0], [0]

            at_tile = [0]

            def sum_tile():
                i, t = at_panel[0], at_tile[0]
                if panels[i][0] != "ada":
                    return
                l, cg, k = panels[i][1:]
                w, dst = panel_tile(i)[0], acc[l][cg % 2]
                if t == 0:
                    wait_landed(dve, i)
                    if k == 0 and cg >= 2:
                        dve.wait_ge(mm_done, number[ada_product(l, cg - 2)] + 1)
                s = cond[:, 4 * k + t:4 * k + t + 1]
                if k + t == 0:
                    ins = v.tensor_scalar(dst, w[:, t, :], s, None, ALU.mult)
                else:
                    ins = v.scalar_tensor_tensor(dst, w[:, t, :], s, dst, ALU.mult, ALU.add)
                at_tile[0] = (t + 1) % 4
                if t < 3:
                    step(ins)
                    return
                ins.then_inc(raw_used, 1)
                at_panel[0] += 1
                dve.wait_ge(raw_used, at_panel[0])
                if k:
                    v.tensor_copy(tiny[:, 204:205], dst[:, 0:1]).then_inc(acc_ready, 1)

            def sum_panels():
                while at_panel[0] < len(panels) and panels[at_panel[0]][0] == "ada":
                    sum_tile()

            def keep_up(name, most=99):
                while at_half[0] < len(halves) and due(at_half[0]) <= number[name] and most:
                    most -= 1
                    h = at_half[0]
                    at_half[0] += 1
                    sum_panels()
                    i = halves[h][0]
                    assert i == at_panel[0]
                    dve.wait_ge(hi_ready, h + 1)
                    ins = v.tensor_tensor(part(w_lo, h), half_of(h), part(w_hi, h).bitcast(F32), ALU.subtract)
                    if h + 1 < len(halves) and halves[h + 1][0] == i:
                        ins.then_inc(lo_ready, 1)
                    else:
                        ins.then_inc(lo_ready, 1)
                        dve.wait_ge(lo_ready, h + 1)
                        v.tensor_copy(tiny[:, 205:206], tiny[:, 0:1]).then_inc(raw_used, 1)
                        at_panel[0] += 1

            def product_ready(eng, name):
                keep_up(name)
                return wait_product(eng, name)

            b = product_ready(dve, ("par",))
            v.tensor_copy(par[:, :], b[:, 0:P])
            done(v.tensor_copy(adab[:, :], b[:, P:P + 96]))
            read(dve, ("par",))
            v.tensor_scalar(omm, par[:, PAR["mu"]:PAR["mu"] + 15], -1.0, 1.0, ALU.mult, ALU.add)
            v.tensor_scalar(omka, par[:, PAR["k_a"]:PAR["k_a"] + 4], -1.0, 1.0, ALU.mult, ALU.add)
            dve.wait_ge(sig_c, 1)
            v.tensor_tensor(cond[:, :], sg_c, par[:, 0:8], ALU.mult).then_inc(cond_ready, 1)
            dve.wait_ge(cond_ready, 1)
            sum_panels()
            for k in range(4):
                b = product_ready(dve, ("mod", 0, k))
                done(v.scalar_tensor_tensor(mod[:, 0, 4 * k:4 * k + 4], b[:, 0:4], float(k >= 2),
                                            adab[:, 4 * k:4 * k + 4], ALU.add, ALU.add))
            read(dve, ("mod", 0, 3))
            v.tensor_copy(tiny[:, 203:204], mod[:, 0, 0:1]).then_inc(mod_ready, 1)

            def x_low(d):
                dve.wait_ge(x_split_hi, d + 1)
                v.tensor_tensor(u0_lo[:, d, :], ut_val[:, d, :], u0_hi[:, d, :].bitcast(F32), ALU.subtract)\
                    .then_inc(x_split_lo, 1)

            for d in range(0, KT, 2):
                b = product_ready(dve, ("x", d))
                done(v.tensor_scalar(ut_val[:, d, :].rearrange("p (l r) -> p r l", r=NR),
                                     b[:, :].rearrange("p (r l) -> p r l", r=NR), mod[:, 0, 8 + d:9 + d],
                                     mod[:, 0, d:d + 1], ALU.mult, ALU.add))
                if d:
                    x_low(d - 2)
                    x_low(d - 1)
            x_low(KT - 2)
            x_low(KT - 1)
            for i in range(15):
                b = product_ready(dve, ("p", i))
                rows_ = 32 if i == 14 else P
                dst = (rT, kT_, vT)[i // 4][:, i % 4, :] if i < 12 else low[:, i - 12, :]
                dst = dst[0:rows_]
                step(v.tensor_scalar(dst, b[0:rows_, :], omm[0:rows_, i:i + 1], None, ALU.mult))
                done(v.scalar_tensor_tensor(dst[:, 1:T], b[0:rows_, 0:T - 1], par[0:rows_, PAR["mu"] + i:PAR["mu"] + i + 1],
                                            dst[:, 1:T], ALU.mult, ALU.add))
            read(dve, ("p", 14))
            keep_up(("h", 0))
            def chunks(t):
                return t.rearrange("p h (c s) -> p (h c) s", s=CH)

            read(dve, ("w", 3))
            dve.wait_ge(kh_ready, 1)
            spare = [t10, t11]

            def doubling(n):
                src = spare[(n + 1) % 2] if n else aT
                dst, sh = spare[n % 2], 1 << n
                v.tensor_copy(chunks(dst)[:, :, 0:sh], chunks(src)[:, :, 0:sh])
                step(v.tensor_tensor(chunks(dst)[:, :, sh:], chunks(src)[:, :, sh:], chunks(src)[:, :, :CH - sh], ALU.add))

            doubling(0)
            doubling(1)
            keep_up(("h", 1))
            read(dve, ("nrm",))
            step(v.tensor_scalar(norms, norms, 1e-12, None, ALU.max))
            v.reciprocal(norms, norms).then_inc(norm_ready, 1)
            doubling(2)
            keep_up(("h", 2))
            for i in range(HP):
                b = wait_product(dve, ("nb", i))
                done(v.tensor_tensor(t8[:, i, :], t8[:, i, :], b[:, :], ALU.mult))
            read(dve, ("nb", HP - 1))
            v.tensor_copy(tiny[:, 206:207], t8[:, 0, 0:1]).then_inc(kk_ready, 1)
            doubling(3)
            keep_up(("h", 3))
            doubling(4)
            keep_up(("b", 0))
            doubling(5)
            ends = chunks(t11)[:, :, CH - 1]
            step(v.tensor_copy(csum_end, ends))
            ce = csum_end.rearrange("p (h c) -> p h c", c=NCH)
            step(v.tensor_tensor(rho.rearrange("p (h c) -> p h c", c=NCH - 1), ce[:, :, 0:NCH - 1], ce[:, :, 1:NCH], ALU.add))
            step(v.tensor_scalar(csum_end, csum_end, 0.5, None, ALU.mult))
            step(v.tensor_tensor(chunks(t10), chunks(t11), csum_end.unsqueeze(2).broadcast_to((P, HP * NCH, CH)), ALU.subtract))
            v.tensor_tensor(aT, t10, aT, ALU.subtract).then_inc(cs_ready, 1)
            keep_up(("b", 1))
            for i in range(HP):
                ins = v.scalar_tensor_tensor(t9[:, i, :], rT[:, i, :], par[:, PAR["r_k"] + i:PAR["r_k"] + i + 1],
                                             kT_[:, i, :], ALU.mult, ALU.mult)
            ins.then_inc(rk_ready, 1)
            dve.wait_ge(exps_ready, 4)
            step(v.scalar_tensor_tensor(aT, t8, -1.0, aT, ALU.mult, ALU.mult))
            dve.wait_ge(kki_ready, 1)
            v.tensor_tensor(bT, bT, t11, ALU.mult).then_inc(prods_ready, 1)
            dve.wait_ge(prods_ready, 1)
            dve.wait_ge(rp_ready, 1)
            for kind, i in CONV_BONUS:
                b = product_ready(dve, (kind, i))
                if kind == "bonus":
                    done(v.tensor_tensor(bonus[:, i, :], b[:, :], vT[:, i, :], ALU.mult))
                    continue
                read(dve, ("b", 3))
                done(v.tensor_tensor(t8[:, i, :], b[:, :], bonus[:, i, :], ALU.mult))
                read(dve, ("c", i))

                def tap(k):
                    return par[:, PAR["conv"] + 4 * k + i:PAR["conv"] + 4 * k + i + 1]

                step(v.tensor_scalar(t10[:, i, :], t8[:, i, :], tap(2), None, ALU.mult))
                step(v.scalar_tensor_tensor(t10[:, i, 1:T], t8[:, i, 0:T - 1], tap(1), t10[:, i, 1:T], ALU.mult, ALU.add))
                step(v.scalar_tensor_tensor(t10[:, i, 2:T], t8[:, i, 0:T - 2], tap(0), t10[:, i, 2:T], ALU.mult, ALU.add))
                step(v.tensor_tensor(ybT[:, i, :], ybT[:, i, :], t10[:, i, :], ALU.mult))
            read(dve, ("bonus", 3))
            v.tensor_copy(tiny[:, 201:202], tiny[:, 0:1]).then_inc(conv_done, 1)

            def group_norm_mean(s):
                b = product_ready(dve, ("mean", s))
                y = rT[:, :, P * s:P * s + P]
                done(v.tensor_tensor(y, y, b[:, :].rearrange("p (h t) -> p h t", h=HP), ALU.subtract))
                read(dve, ("mean", s))
                v.tensor_copy(tiny[:, 202:203], y[:, 0, 0:1]).then_inc(gn_in, 1)

            def group_norm_root(s):
                read(dve, ("var", s))
                v.reciprocal(gn, gn).then_inc(gn_root, 1)

            def group_norm_scale(s):
                y = rT[:, :, P * s:P * s + P]
                dve.wait_ge(gn_root, s + 1)
                step(v.tensor_tensor(y, y, gn, ALU.mult))
                for i in range(HP):
                    ins = v.tensor_scalar(y[:, i, :], y[:, i, :], par[:, PAR["lnx_g"] + i:PAR["lnx_g"] + i + 1],
                                          par[:, PAR["lnx_b"] + i:PAR["lnx_b"] + i + 1], ALU.mult, ALU.add)
                step(ins)

            def group_norm_end(s):
                tk = slice(P * s, P * s + P)
                y = rT[:, :, tk]
                step(v.tensor_tensor(y, y, bonus[:, :, tk], ALU.add))
                v.tensor_tensor(y, y, gt[:, :, tk], ALU.mult).then_inc(ya_ready, 1)
                dve.wait_ge(ya_ready, s + 1)

            for s in range(SC):
                for kind, q, name in super_products(s):
                    if kind not in SUPER_DVE:
                        continue
                    if kind == "mean":
                        group_norm_mean(s - 1)
                        continue
                    b = product_ready(dve, name)
                    if kind in ("UB", "UK"):
                        dst, lo = (MB, 0) if kind == "UB" else (MK, 2)
                        m = mask[:, lo:lo + 2, :].rearrange("p a k -> p (a k)").unsqueeze(1).broadcast_to((P, 2, 2 * P))
                        done(v.tensor_tensor(dst[:, 2 * q:2 * q + 2, :, :].rearrange("p m a k -> p m (a k)"),
                                             b[:, :].rearrange("p (m k) -> p m k", m=2), m, ALU.mult))
                    elif kind == "LL":
                        def masked(q_, j, dst):
                            m = mask[:, j, :].unsqueeze(1).broadcast_to((P, 4, P))
                            src = bank[number["LL", s, q_] % 8][:, :].rearrange("p (m k) -> p m k", m=4)
                            return v.tensor_tensor(dst[:, 4 * q_:4 * q_ + 4, :], src, m, ALU.mult)

                        masked(q, 4, m0).then_inc(d_ready, 1)
                        if q:
                            dve.wait_ge(d_ready, 2 * s + 2)
                            v.tensor_tensor(m6, MB[:, :, 0, :], ident[:, :].unsqueeze(1).broadcast_to((P, HEADS, P)),
                                            ALU.add).then_inc(p_ready, 1)
                            dve.wait_ge(p_ready, s + 1)
                            for q_ in range(2):
                                masked(q_, 5, m1)
                                done(masked(q_, 6, m2))
                    else:
                        done(v.tensor_tensor(m6[:, 4 * q:4 * q + 4, :], b[:, :].rearrange("p (m k) -> p m k", m=4),
                                             m6[:, 4 * q:4 * q + 4, :], ALU.add))
                        if q:
                            read(dve, name)
                        if kind == "Pb" and q and s:
                            group_norm_root(s - 1)
                    for _ in range(SUM_AFTER.get((kind, q), 0)):
                        sum_tile()
                for c_ in (2 * s, 2 * s + 1):
                    p_ = c_ % 2
                    h = slice(64 * p_, 64 * p_ + 64)
                    b = product_ready(dve, ("SA", c_))
                    read(dve, ("U", s))
                    done(v.tensor_tensor(saz[h, p_, :, :], b[h, :].rearrange("p (h k) -> p h k", h=HP), uu[h, :, :], ALU.add))
                    if s:
                        (group_norm_end if p_ else group_norm_scale)(s - 1)
                    if c_ == NCH - 1:
                        continue
                    b = product_ready(dve, ("DS", c_))
                    old, new = state[:, c_ % 2, :, :], state[:, (c_ + 1) % 2, :, :]
                    rc = rho.rearrange("p (h c) -> p h c", c=NCH - 1)[:, :, c_]
                    bb = b[:, :].rearrange("p (h k) -> p h k", h=HP)
                    if c_:
                        product_ready(dve, ("Y", c_ - 1))
                    for e in range(2):
                        g = slice(64 * e, 64 * e + 64)
                        k = slice(64 * e, 64 * e + 64)
                        ins = v.tensor_tensor(new[g, :, k], bb[g, :, k], old[g, :, k], ALU.add)
                    step(ins)
                    for e in range(2):
                        g = slice(64 * e, 64 * e + 64)
                        k = slice(64 * e, 64 * e + 64)
                        ins = v.tensor_tensor(new[g, :, k], new[g, :, k],
                                              rc[g].unsqueeze(2).broadcast_to((64, HP, 64)), ALU.mult)
                    done(ins)
            sum_panels()
            group_norm_mean(SC - 1)
            keep_up(ada_product(0, SUMMED[-1][0]))
            group_norm_root(SC - 1)
            group_norm_scale(SC - 1)
            group_norm_end(SC - 1)
            for i in range(HP):
                dve.wait_ge(mix_hi_ready, HP + i + 1)
                v.tensor_tensor(mix_lo[:, 4 + i, :], rT[:, i, :], mix_hi[:, 4 + i, :].bitcast(F32), ALU.subtract)\
                    .then_inc(ya_lo_ready, 1)
            read(dve, ada_product(0, 9))
            v.tensor_tensor(mod[:, 0, 16:24], mod[:, 0, 16:24], adab[:, 24:32], ALU.add)
            step(v.scalar_tensor_tensor(mod[:, 0, 24:32], mod[:, 0, 24:32], 1.0, adab[:, 32:40], ALU.add, ALU.add))

            def norm(l, j):
                if not (l == 1 and j == 1):
                    l2, o = (l, 16) if j == 0 else (1, 0)
                    base = (2 * l + j) * 8
                    step(v.tensor_tensor(scl, par[:, PAR["ln_g"] + base:PAR["ln_g"] + base + 8], mod[:, l2, o + 8:o + 16], ALU.mult))
                    step(v.tensor_tensor(shf, par[:, PAR["ln_b"] + base:PAR["ln_b"] + base + 8], mod[:, l2, o + 8:o + 16], ALU.mult))
                    step(v.tensor_tensor(shf, shf, mod[:, l2, o:o + 8], ALU.add))
                residual(l, j, j)
                if l == 1 and j == 1:
                    return

                def low_parts(r):
                    k = 8 * (2 * l + j) + 2 * r
                    for n in range(2):
                        dve.wait_ge(u_hi_ready, k + n + 1)
                        t = slice(P * r, P * r + P)
                        v.tensor_tensor(u_lo[:, 4 * n:4 * n + 4, t], u_val[r % 2][:, n, :].rearrange("p (d l) -> p d l", d=4),
                                        u_hi[:, 4 * n:4 * n + 4, t].bitcast(F32), ALU.subtract).then_inc(u_lo_ready, 1)

                for r in range(NR):
                    k = 8 * (2 * l + j) + 2 * r
                    b = wait_product(dve, ("nT", l, j, r, 0))
                    if k >= 4:
                        dve.wait_ge(u_lo_ready, k - 2)
                    for d in range(4):
                        ins = v.tensor_scalar(u_val[r % 2][:, 0, P * d:P * d + P], b[:, P * d:P * d + P], scl[:, d:d + 1],
                                              shf[:, d:d + 1], ALU.mult, ALU.add)
                    done(ins)
                    if r:
                        low_parts(r - 1)
                    if r >= 2:
                        keep_up(("nT", l, j, 0, 0), 1)
                low_parts(NR - 1)

            def residual(l, j, a_):
                gr = gate[(0, 1, 0, 2)[2 * l + j]]
                for n in range(2):
                    cols = slice(512 * n, 512 * n + 512)
                    for r in range(NR):
                        if r < NR - 1 or n == 0 or a_ < j:
                            keep_up(("y", l, j, a_, n, r))
                        b = wait_product(dve, ("y", l, j, a_, n, r))
                        if a_ == 0 and n == 0:
                            if l == 0 and j == 0:
                                dve.wait_ge(xp_in, 16)
                            else:
                                dve.wait_ge(resid_ready, 4 * (2 * l + j - 1) + r + 1)
                        done(v.tensor_tensor(ytmp[:, r % 2, :], b[:, :], gr[:, cols], ALU.mult))
                        read(dve, ("y", l, j, a_, n, r))
                        step(v.scalar_tensor_tensor(xp[:, r, cols], xp[:, r, cols], 1.0 if a_ else ALPHA, ytmp[:, r % 2, :],
                                                    ALU.mult, ALU.add))
                        if a_ == j:
                            step(v.bn_stats(stats[:, 12 * r + 6 * n:12 * r + 6 * n + 6], xp[:, r, cols]))
                            if n == 1:
                                k = 4 * (2 * l + j) + r
                                v.bn_aggr(mv[:, 2 * r:2 * r + 2], stats[:, 12 * r:12 * r + 12]).then_inc(var_ready, 1)
                                dve.wait_ge(root_ready, k + 1)
                                step(v.reciprocal(rstd[:, r:r + 1], rstd[:, r:r + 1]))
                                if l == 1 and j == 1 and r >= BY_POOL:
                                    dve.wait_ge(rows_in, 128)
                                    step(v.scalar_tensor_tensor(xp[:, r, :], xp[:, r, :], mv[:, 2 * r:2 * r + 1], grow,
                                                                ALU.subtract, ALU.mult))
                                    v.scalar_tensor_tensor(xp[:, r, :], xp[:, r, :], rstd[:, r:r + 1], brow, ALU.mult,
                                                           ALU.add).then_inc(out_ready, 1)
                                    continue
                                v.scalar_tensor_tensor(nmr[:, r:r + 1], mv[:, 2 * r:2 * r + 1], -1.0, rstd[:, r:r + 1],
                                                       ALU.mult, ALU.mult).then_inc(scale_ready, 1)

            def hidden_lo(k):
                dve.wait_ge(h_hi_ready, k + 1)
                v.tensor_tensor(h_lo[:, k % FH, :], h_val[:, k % 4, :], h_hi[:, k % FH, :].bitcast(F32), ALU.subtract)\
                    .then_inc(h_lo_ready, 1)

            for l in range(2):
                if l:
                    for g in range(GROUPS):
                        for i in range(HP):
                            b = product_ready(dve, ("k", g, i))
                            done(v.tensor_copy(kT[:, g, i, :], b[:, :]))
                        keep_up(("v", g, 0))
                    dve.wait_ge(mm_done, number[("v", GROUPS - 1, NR - 1)] + 1)
                    v.memset(qpad[64:128, 0, :, :], 0.0).then_inc(q_first_zero, 1)
                    n = HEADS * NR
                    for i in range(n + 3):
                        if i < n:
                            h, r = i // NR, i % NR
                            if r == 0:
                                dve.wait_ge(tab_in[h % 2], 16 * (h // 2 + 1))
                            if i >= 4:
                                dve.wait_ge(mm_done, number[("PT1", i - 4)] + 1)
                            t = tab[h % 2]
                            b = product_ready(dve, ("S0", i))
                            done(v.tensor_tensor(sS[i % 4][:, 0:512], b[:, :], t[:, (3 - r) * P:(7 - r) * P], ALU.add))
                            b = product_ready(dve, ("S1", i))
                            done(v.tensor_tensor(sS[i % 4][:, 512:768], b[:, 0:256], t[:, 7 * P:9 * P], ALU.add))
                            read(dve, ("S1", i))
                            if i >= 4:
                                dve.wait_ge(exp_ready, i - 3)
                            step(v.tensor_reduce(mx[:, i % 4:i % 4 + 1], sS[i % 4][:, :], AX.X, ALU.max))
                            v.tensor_scalar(nmax[:, i % 4:i % 4 + 1], mx[:, i % 4:i % 4 + 1], -1.0, None,
                                            ALU.mult).then_inc(max_ready, 1)
                        if 2 <= i <= n + 1:
                            k = i - 2
                            b = product_ready(dve, ("PT1", k))
                            done(v.tensor_copy(pT[:, k % 2, 4:6, :], b[:, 0:256].rearrange("p (m k) -> p m k", m=2)))
                            dve.wait_ge(exp_ready, k + 1)
                            v.reciprocal(rden[:, k % 4:k % 4 + 1], den[:, k % 4:k % 4 + 1]).then_inc(rden_ready, 1)
                        if i >= 3:
                            k = i - 3
                            h, r = k // NR, k % NR
                            b = product_ready(dve, ("O", k))
                            dve.wait_ge(rden_ready, k + 1)
                            done(v.tensor_scalar(otok[:, r, HD * h:HD * h + HD], b[:, 0:HD], rden[:, k % 4:k % 4 + 1], None,
                                                 ALU.mult))
                    for r in range(NR):
                        dve.wait_ge(o_hi_ready, r + 1)
                        t = slice(P * r, P * r + P)
                        v.tensor_tensor(o_lo[:, :, t], oT[:, :, t], o_hi[:, :, t].bitcast(F32), ALU.subtract)\
                            .then_inc(o_lo_ready, 1)
                norm(l, 0)
                for a_ in range(2):
                    for f in range(FH * a_, FH * a_ + FH):
                        k = 2 * FH * l + f
                        product_ready(dve, ("f", l, f))
                        read(dve, ("f", l, f))
                        v.tensor_tensor(h_val[:, k % 4, :], h_val[:, k % 4, :], h_val[:, k % 4, :], ALU.mult)\
                            .then_inc(h_value, 1)
                        if f % FH:
                            hidden_lo(k - 1)
                    hidden_lo(k)
                    if a_ == 0:
                        residual(l, 1, 0)
                if l == 0:
                    read(dve, ada_product(1, 11))
                    a1 = 48
                    v.tensor_tensor(mod[:, 1, 0:8], mod[:, 1, 0:8], adab[:, a1:a1 + 8], ALU.add)
                    v.tensor_tensor(mod[:, 1, 16:24], mod[:, 1, 16:24], adab[:, a1 + 24:a1 + 32], ALU.add)
                    v.scalar_tensor_tensor(mod[:, 1, 8:16], mod[:, 1, 8:16], 1.0, adab[:, a1 + 8:a1 + 16], ALU.add, ALU.add)
                    step(v.scalar_tensor_tensor(mod[:, 1, 24:32], mod[:, 1, 24:32], 1.0, adab[:, a1 + 32:a1 + 40], ALU.add, ALU.add))
                norm(l, 1)

        @block.tensor
        def _(pe):
            at_job, at_half = [0], [0]

            def start(name, offset=0):
                j = at_job[0]
                assert plan[j][0] == name, (plan[j], name)
                at_job[0] += 1
                if j >= 8:
                    read(pe, plan[j - 8][0])
                return bank[j % 8]

            def finish(ins):
                ins.then_inc(mm_done, 1)

            def half_panel():
                h = at_half[0]
                at_half[0] += 1
                pe.wait_ge(lo_ready, h + 1)
                return part(w_hi, h), part(w_lo, h)

            mm = pe.matmul

            def mm3(out_, left, right, first, last):
                mm(out_, left[0], right[0], start=first, stop=False)
                mm(out_, left[1], right[0], start=False, stop=False)
                return mm(out_, left[0], right[1], start=False, stop=last)

            def transpose4(b, parts):
                for i, src in enumerate(parts):
                    ins = pe.transpose(b[:, P * i:P * i + P], src, ident[:, :])
                return ins

            pe.wait_ge(band_in, 32)
            pe.wait_ge(raw_zero, 2)
            for i in range(5):
                b = start(("F", i))
                if i < 3:
                    ins = mm(b[0:HEADS, :], relb[0:33, 0:8], wconst[0:33, 512 * i:512 * i + 512], start=True, stop=True)
                elif i == 3:
                    mm(b[0:HEADS, 0:256], relb[0:33, 0:8], wconst[0:33, 1536:1792], start=True, stop=True)
                    ins = mm(b[0:HEADS, 256:512], relb[0:33, 8:16], wconst[0:33, 1792:2048], start=True, stop=True)
                else:
                    ins = mm(b[0:HEADS, 0:256], relb[0:33, 16:24], wconst[0:33, 2048:2304], start=True, stop=True)
                finish(ins)
            pe.wait_ge(block_ready, 1)
            pe.wait_ge(params_in, 16 * 14)
            pe.wait_ge(ident_in, 16)
            b = start(("par",))
            pe.transpose(b[:, 0:P], rawpar[:, 0, :], ident[:, :])
            finish(pe.transpose(b[:, P:2 * P], rawpar[:, 1, :], ident[:, :]))
            ada_done = [0]

            def ada(l, cg):
                name = ada_product(l, cg)
                b = start(name)
                ada_done[0] += 1
                pe.wait_ge(acc_ready, ada_done[0])
                src = acc[l][cg % 2]
                if name[0] == "mod":
                    for n in range(4):
                        ins = mm(b[:, n:n + 1], src[:, P * n:P * n + P], ones_col, start=True, stop=True)
                else:
                    for i in range(4):
                        col = 48 * l + 4 * cg + i
                        mm(b[:, P * i:P * i + P], adab[:, col:col + 1].broadcast_to((P, P)), ident[:, :], start=(i == 0),
                           stop=False, skip_group_check=True)
                    ins = mm(b[:, :], ones_sq, src, start=False, stop=True, skip_group_check=True)
                finish(ins)

            for cg in range(4):
                ada(0, cg)
            pe.wait_ge(x_in, 64)
            for d in range(KT):
                b = start(("x", d))
                finish(transpose4(b, [xin[:, r, P * d:P * d + P] for r in range(NR)]))

            def feature_tile(name, hi, lo):
                b = start(name)
                wh, wl = half_panel()
                for t in range(KT):
                    if name == ("p", 0):
                        pe.wait_ge(x_split_lo, t + 1)
                    ins = mm3(b[:, :], (wh[:, t, :], wl[:, t, :]), (hi[:, t, :], lo[:, t, :]), t == 0, t == KT - 1)
                finish(ins)

            for i in range(15):
                feature_tile(("p", i), u0_hi, u0_lo)
                if i in (5, 9, 13):
                    ada(0, i // 4 + 3)
            pe.wait_ge(lowrank_in, 64)
            pe.wait_ge(block_ready, 1)
            pe.wait_ge(low_ready, 1)
            for n, j in (("w", 0), ("a", 1)):
                for i in range(HP):
                    b = start((n, i))
                    finish(mm(b[:, :], lr[:, j, P * i:P * i + P], low[:, 0, :], start=True, stop=True))
            pe.wait_ge(low_ready, 2)
            for i in range(HP):
                b = start(("g", i))
                mm(b[:, :], lr[:, 2, P * i:P * i + P], low[:, 1, :], start=True, stop=False)
                finish(mm(b[:, :], lr[0:32, 3, P * i:P * i + P], low[0:32, 2, :], start=False, stop=True))
            for i in range(HP):
                feature_tile(("h", i), u0_hi, u0_lo)
                if i == 0:
                    pe.wait_ge(consts_in, 48)
                    pe.wait_ge(sq_ready, 1)
                    b = start(("nrm",))
                    for k in range(HP):
                        ins = mm(b[0:HEADS, :], head_cols[:, k, :], t9[:, k, :], start=(k == 0), stop=(k == HP - 1))
                    finish(ins)
                if i == 2:
                    pe.wait_ge(norm_ready, 1)
                    for k in range(HP):
                        b = start(("nb", k))
                        finish(mm(b[:, :], head_rows[:, k, :], norms, start=True, stop=True))
            for i in range(HP):
                feature_tile(("b", i), u0_hi, u0_lo)
            for kind, i in CONV_BONUS:
                if kind == "c":
                    feature_tile(("c", i), u0_hi, u0_lo)
                    continue
                pe.wait_ge(rk_ready, 1)
                b = start(("bonus", i))
                finish(mm(b[:, :], block_ones[:, :], t9[:, i, :], start=True, stop=True))

            pe.wait_ge(prods_ready, 1)
            pe.wait_ge(kr_ready, 1)

            def group_norm_products(kind, s):
                b = start((kind, s))
                if kind == "mean":
                    read(pe, ("Y", 2 * s + 1))
                    src = rT[:, :, P * s:P * s + P]
                else:
                    pe.wait_ge(gn_sq, s + 1)
                    src = gn
                finish(mm(b[:, :].rearrange("p (h t) -> p h t", h=HP), block_mean[:, :], src, start=True, stop=True))

            for s in range(SC):
                tk = slice(P * s, P * s + P)
                steps = {
                    "D2": (lambda h: m0[:, h, :], lambda h: MB[:, h, 0, :], ()),
                    "D4": (lambda h: m0[:, h, :], lambda h: m3[:, h, :], ("D2T",)),
                    "P2": (lambda h: m0[:, h, :], lambda h: m6[:, h, :], ("D2T",)),
                    "D8T": (lambda h: m4[:, h, :], lambda h: m5[:, h, :], ("D4T",)),
                    "P4": (lambda h: m5[:, h, :], lambda h: m6[:, h, :], ("P2",)),
                    "P8": (lambda h: m3[:, h, :], lambda h: m6[:, h, :], ("D8T", "P4")),
                    "Y1": (lambda h: m1[:, h, :], lambda h: m6[:, h, :], ("P8",)),
                    "Pa": (lambda h: m0[:, h, :], lambda h: m4[:, h, :], ("P8T", "Y1")),
                    "Y2": (lambda h: m2[:, h, :], lambda h: m6[:, h, :], ("Pa",)),
                    "Pb": (lambda h: m5[:, h, :], lambda h: m3[:, h, :], ("PaT", "Y2")),
                }
                turned = {"D2T": (m3, "D2"), "D4T": (m4, "D4"), "P8T": (m6, "P8"), "PaT": (m6, "Pa")}
                token_major = {"trK": kT_, "trB": bT, "trA": aT, "trV": vT}
                for kind, q, name in super_products(s):
                    if kind in ("mean", "var"):
                        group_norm_products(kind, s - 1)
                        continue
                    b = start(name)
                    if kind in ("UB", "UK"):
                        pe.wait_ge(arz_ready, 2 * s + 2)
                        src = bT if kind == "UB" else kT_
                        for e in range(2):
                            ins = mm(b[:, 256 * e:256 * e + 256], src[:, q, tk],
                                     arz[:, q, e, :, :].rearrange("p a k -> p (a k)"), start=True, stop=True)
                    elif kind == "LL":
                        for j in range(4):
                            h = 4 * q + j
                            ins = mm(b[:, P * j:P * j + P], arz[:, h // 2, h % 2, 0, :], bT[:, h // 2, tk], start=True,
                                     stop=True)
                    elif kind in token_major:
                        ins = transpose4(b, [token_major[kind][:, i, tk] for i in range(HP)])
                    elif kind in turned:
                        src, before = turned[kind]
                        read(pe, (before, s, q))
                        ins = transpose4(b, [src[:, 4 * q + j, :] for j in range(4)])
                    elif kind in steps:
                        left, right, before = steps[kind]
                        if kind == "D2":
                            pe.wait_ge(d_ready, 2 * s + 1 + q)
                        else:
                            pe.wait_ge(p_ready, s + 1)
                        for n in before:
                            read(pe, (n, s, q))
                        for j in range(4):
                            ins = mm(b[:, P * j:P * j + P], left(4 * q + j), right(4 * q + j), start=True, stop=True)
                    elif kind == "LakV":
                        read(pe, ("trV", s), ("UK", s, 3))
                        for h in range(HEADS):
                            ins = mm(b[:, HD * h:HD * h + HD], MK[:, h, 0, :],
                                     tokV[:, h // 2, HD * (h % 2):HD * (h % 2) + HD], start=True, stop=True)
                    elif kind == "WT":
                        read(pe, ("trA", s), ("Pb", s, 1))
                        for h in range(HEADS):
                            e = h % 2
                            ins = mm(b[64 * e:64 * e + 64, P * (h // 2):P * (h // 2) + P],
                                     tokA[:, h // 2, HD * e:HD * e + HD], m6[:, h, :], start=True, stop=True)
                    else:
                        read(pe, ("LakV", s))
                        for h in range(HEADS):
                            ins = mm(b[:, HD * h:HD * h + HD], m6[:, h, :],
                                     lakv[:, h // 2, HD * (h % 2):HD * (h % 2) + HD], start=True, stop=True)
                    finish(ins)
                read(pe, ("WT", s))
                pe.wait_ge(vz_ready, 2 * s + 2)
                for c_ in (2 * s, 2 * s + 1):
                    p_ = c_ % 2
                    S = state[:, c_ % 2, :, :]
                    b = start(("SA", c_))
                    if c_:
                        read(pe, ("DS", c_ - 1))
                    else:
                        pe.wait_ge(pads_zero, 1)
                    for i in range(HP):
                        ins = mm(b[64 * p_:64 * p_ + 64, P * i:P * i + P], wt[:, i, 64 * p_:64 * p_ + 64], S[:, i, :],
                                 start=True, stop=True)
                    finish(ins)
                    if c_ < NCH - 1:
                        b = start(("DS", c_))
                        read(pe, ("SA", c_))
                        for i in range(HP):
                            mm(b[:, P * i:P * i + P], tokK[:, i, :], vz[:, p_, i, :], start=True, stop=False)
                            ins = mm(b[:, P * i:P * i + P], tokB[:, i, :], saz[:, p_, i, :], start=False, stop=True)
                        finish(ins)
                    b = start(("Y", c_))
                    read(pe, ("SA", c_))
                    ct = slice(64 * p_, 64 * p_ + 64)
                    for i in range(HP):
                        for e in range(2):
                            o = b[64 * e:64 * e + 64, CH * i:CH * i + CH]
                            mm(o, saz[:, p_, i, HD * e:HD * e + HD], MB[:, 2 * i + e, 1, ct], start=True, stop=False,
                               skip_group_check=True)
                            mm(o, vz[:, p_, i, HD * e:HD * e + HD], MK[:, 2 * i + e, 1, ct], start=False, stop=False,
                               skip_group_check=True)
                        ins = mm(b[:, CH * i:CH * i + CH], S[:, i, :], rT[:, i, CH * c_:CH * c_ + CH], start=False,
                                 stop=True, skip_group_check=True)
                    finish(ins)
                if s == SC - 1:
                    group_norm_products("mean", s)
                for cg in SUMMED[s]:
                    ada(0, cg)
            group_norm_products("var", SC - 1)

            def token_tiles(names, order, left):
                banks = [start(n) for n in names]
                n = len(order)
                for k in range(0, n - 4, 2):
                    wh, wl = half_panel()
                    for t in range(2):
                        for r in range(NR):
                            ins = mm3(banks[r][:, :], left(order[k + t], r), (wh[:, t, :], wl[:, t, :]), k + t == 0, False)
                    ins.then_inc(half_used, 1)
                last = [half_panel(), half_panel()]
                for r in range(NR):
                    for m, (wh, wl) in enumerate(last):
                        for t in range(2):
                            k = n - 4 + 2 * m + t
                            ins = mm3(banks[r][:, :], left(order[k], r), (wh[:, t, :], wl[:, t, :]), k == 0, k == n - 1)
                    finish(ins)

            def norm_turns(l, j):
                for r in range(NR):
                    pe.wait_ge(normed, 4 * (2 * l + j) + r + 1)
                    for n in range(2):
                        b = start(("nT", l, j, r, n))
                        finish(transpose4(b, [xp[:, r, P * d:P * d + P] for d in range(4 * n, 4 * n + 4)]))

            def first_feature_tiles(names, n):
                banks = [start(name) for name in names]
                parts = []
                for half in range(2):
                    pe.wait_ge(u_lo_ready, 8 * n + 4 * half + 4)
                    cols = slice(256 * half, 256 * half + 256)
                    for i, b in enumerate(banks):
                        if not half:
                            parts.append(half_panel())
                        wh, wl = parts[i]
                        for t in range(KT):
                            ins = mm3(b[:, cols], (wh[:, t, :], wl[:, t, :]), (u_hi[:, t, cols], u_lo[:, t, cols]), t == 0,
                                      t == KT - 1)
                        if half:
                            finish(ins)

            for l in range(2):
                if l == 0:
                    def left(k, r):
                        m = (k + 4) % 8
                        if (r, m) in waits:
                            if m < HP:
                                pe.wait_ge(yb_lo_ready, 1)
                            else:
                                pe.wait_ge(ya_lo_ready, m - HP + 1)
                            waits.discard((r, m))
                        return mix_hi[:, m, r:T:NR], mix_lo[:, m, r:T:NR]

                    waits = {(0, m) for m in range(8)}
                    for n in range(2):
                        token_tiles([("y", 0, 0, 0, n, r) for r in range(NR)], (4, 5, 6, 7, 0, 1, 2, 3), left)
                else:
                    def token_u(k, r):
                        return u_hi[:, k, P * r:P * r + P], u_lo[:, k, P * r:P * r + P]

                    for g in range(GROUPS):
                        if g == 0:
                            first_feature_tiles([("q", 0, i) for i in range(3)], 1)
                        for n in ("q", "k"):
                            for i in range(3 if (n, g) == ("q", 0) else 0, HP):
                                feature_tile((n, g, i), u_hi, u_lo)
                        token_tiles([("v", g, r) for r in range(NR)], range(8), token_u)
                    read(pe, ("q", 2, 3), ("k", 2, 3))
                    read(pe, ("v", 2, 3))
                    n = HEADS * NR
                    for i in range(n + 3):
                        if i < n:
                            h, r = i // NR, i % NR
                            e, hp = h % 2, h // 2
                            if h:
                                pe.wait_ge(q_padded, h)
                            else:
                                pe.wait_ge(q_first, 1)
                                pe.wait_ge(q_first_zero, 1)
                            b = start(("S0", i))
                            finish(mm(b[:, :], qpad[:, e, 0, P * r:P * r + P], kT[:, 0, hp, :], start=True, stop=True))
                            b = start(("S1", i))
                            for g in (1, 2):
                                ins = mm(b[:, P * (g - 1):P * g], qpad[:, e, g, P * r:P * r + P],
                                         kT[:, g, hp, P * r:P * r + P], start=True, stop=True)
                            finish(ins)
                        if 2 <= i <= n + 1:
                            k = i - 2
                            pe.wait_ge(exp_ready, k + 1)
                            b = start(("PT0", k))
                            finish(transpose4(b, [sS[k % 4][:, P * m:P * m + P] for m in range(4)]))
                            b = start(("PT1", k))
                            finish(transpose4(b, [sS[k % 4][:, P * m:P * m + P] for m in range(4, 6)]))
                        if i >= 3:
                            k = i - 3
                            h, r = k // NR, k % NR
                            b = start(("O", k))
                            read(pe, ("PT0", k), ("PT1", k))
                            for m in range(6):
                                vs = v_at[0][:, m, :] if m < 4 else v_at[m - 3][:, r, :]
                                ins = mm(b[:, 0:HD], pT[:, k % 2, m, :], vs[:, HD * h:HD * h + HD], start=(m == 0),
                                         stop=(m == 5))
                            finish(ins)
                    read(pe, ("O", n - 1))
                    for r in range(NR):
                        b = start(("oT", r))
                        finish(transpose4(b, [otok[:, r, P * i:P * i + P] for i in range(HP)]))
                    pe.wait_ge(o_lo_ready, NR)
                    for n in range(2):
                        token_tiles([("y", 1, 0, 0, n, r) for r in range(NR)], range(4),
                                    lambda k, r: (o_hi[:, k, P * r:P * r + P], o_lo[:, k, P * r:P * r + P]))
                norm_turns(l, 0)
                for a in range(2):
                    if a == 0:
                        first_feature_tiles([("f", l, f) for f in range(3)], 2 * l)
                    for f in range(FH * a, FH * a + FH):
                        if f >= 3:
                            feature_tile(("f", l, f), u_hi, u_lo)
                        if l == 0 and f in ADA_AFTER:
                            ada(1, ADA_AFTER[f])
                    waits = set(range(FH))

                    def hidden(k, r):
                        if k in waits:
                            pe.wait_ge(h_lo_ready, 2 * FH * l + FH * a + k + 1)
                            waits.discard(k)
                        return h_hi[:, k, P * r:P * r + P], h_lo[:, k, P * r:P * r + P]

                    for n in range(2):
                        token_tiles([("y", l, 1, a, n, r) for r in range(NR)], range(FH), hidden)
                if l == 0:
                    norm_turns(0, 1)
            assert at_job[0] == len(plan) and at_half[0] == len(halves)


_INS = ['x', 'c', 'ada_w', 'ada_b', 'ln_g', 'ln_b', 'ab_w_in', 'rw_mu', 'rw_w0', 'rw_w_up', 'rw_a0', 'rw_a_up', 'rw_g_up',
        'rw_k_k', 'rw_k_a', 'rw_r_k', 'rw_lnx_g', 'rw_lnx_b', 'sc_conv_w', 'ab_w_out', 'dil_w_qkv', 'dil_w_out',
        'rel_bias', 'mlp_w1', 'mlp_w2']


def shape_constants():
    i, j = np.arange(P)[:, None], np.arange(P)[None, :]

    def same(n):
        return i // n == j // n

    masks = np.stack([same(16) & (i < j), same(64) & (i <= j), same(64) & (i < j), same(64) & (i <= j),
                      same(16) & (i > j), same(32) & ~same(16) & (i > j), same(64) & ~same(32) & (i > j)], axis=1)
    n = np.arange(BW)
    steps = P - 1 - n
    buckets = np.zeros((33, BAND, BW), np.float32)
    for b in range(BAND):
        if b < 7:
            dist = 4 * steps + 3 - b
            valid = (dist >= 0) & (dist <= 128)
        elif b == 7:
            dist = 4 * steps
            valid = steps >= 0
        else:
            dist = 4 * steps
            valid = (steps >= 0) & (steps % 4 == 0)
        d = np.where(valid, dist, 0)
        exact = 16
        far = exact + (np.log(np.maximum(d, 1) / exact) / np.log(2048 / exact) * exact).astype(np.int64)
        bucket = np.where(d < exact, d, np.minimum(far, 31))
        buckets[bucket[valid], b, n[valid]] = 1.0
        buckets[32, b, ~valid] = NEG
    heads = np.zeros((P, HP * HEADS + HP * P), np.float32)
    for i in range(HP):
        for ch in range(P):
            h = 2 * i + ch // HD
            heads[ch, HEADS * i + h] = 1.0
            heads[h, HP * HEADS + P * i + ch] = 1.0
    return np.eye(P, dtype=np.float32), masks.astype(np.float32), heads, buckets.reshape(33, BAND * BW)


def kernel(**inputs):
    import concourse.bacc as bacc
    from concourse.bass_utils import run_bass_kernel_spmd

    nc = bacc.Bacc("TRN2", target_bir_lowering=False, num_devices=1)
    arrays, args = {}, []
    for name in _INS:
        arrays[f"in_{name}"] = np.ascontiguousarray(inputs[name])
    for name, value in zip(("identity", "masks", "heads", "buckets"), shape_constants()):
        arrays[f"in_{name}"] = value
    for name, value in arrays.items():
        args.append(nc.dram_tensor(name, value.shape, F32, kind="ExternalInput").ap())
    args.append(nc.dram_tensor("out", (1, T, D), F32, kind="ExternalOutput").ap())
    args.append(nc.dram_tensor("band", (HEADS, BAND * BW), F32).ap())
    args.append(nc.dram_tensor("skew", (HEADS, P, BAND * BW), F32).ap())
    trunk(nc, *args)
    r = run_bass_kernel_spmd(nc, [arrays], core_ids=[0])
    return r.results[0]["out"]
```
